# Optimizing a Trainium2 kernel written in Bass

```python
import jax, jax.numpy as jnp
from jax import lax
import numpy as np
import jax
import jax.numpy as jnp

D_MODEL = 1024
BATCH = 1
SEQ = 256
DEPTH = 1

CHUNK = 64
Q_BLOCK = 128
HEAD_DIM = 64
D_MIX = D_MODEL
SB_HEADS = 8
SB_WIDTH = SB_HEADS * HEAD_DIM
RW_WIDTH = D_MIX - SB_WIDTH
RW_HEADS = RW_WIDTH // HEAD_DIM
DECAY_LORA = 64
AAA_LORA = 64
GATE_LORA = 128
RW_PROJ = 3 * RW_WIDTH + DECAY_LORA + AAA_LORA + GATE_LORA
PROJ_WIDTH = 3 * SB_WIDTH + RW_PROJ
D_FF = 2816
FFN_HALF = 0.5
RMS_EPS = 1e-6
LNX_EPS = 64e-5


def rms_norm(x, g, eps=RMS_EPS):
    xf = x.astype(jnp.float32)
    ms = jnp.mean(xf * xf, axis=-1, keepdims=True)
    return (xf * lax.rsqrt(ms + eps) * g.astype(jnp.float32)).astype(x.dtype)

def swiglu(x, w_gate, w_up, w_down):
    return (jax.nn.silu(x @ w_gate) * (x @ w_up)) @ w_down

def token_shift(u):
    return jnp.pad(u[:, :-1], ((0, 0), (1, 0), (0, 0)))

def stick_breaking_attention(q, k, v):
    S, Dh = q.shape[1], q.shape[-1]
    scale = Dh ** -0.5
    outs = []
    for blk in range(S // Q_BLOCK):
        q0 = blk * Q_BLOCK
        kv_len = q0 + Q_BLOCK
        qb, kb, vb = q[:, q0:kv_len], k[:, :kv_len], v[:, :kv_len]
        z = jnp.einsum('bqhd,bkhd->bhqk', qb, kb).astype(jnp.float32) * scale
        q_pos = q0 + jnp.arange(Q_BLOCK)[:, None]
        k_pos = jnp.arange(kv_len)[None, :]
        mask = k_pos < q_pos
        log_beta = jax.nn.log_sigmoid(z)
        log_1m_beta = jnp.where(mask, jax.nn.log_sigmoid(-z), 0.0)
        log_remain = lax.cumsum(log_1m_beta, axis=3, reverse=True) - log_1m_beta
        att = jnp.where(mask, jnp.exp(log_beta + log_remain), 0.0)
        outs.append(jnp.einsum('bhqk,bkhd->bqhd', att.astype(vb.dtype), vb))
    return jnp.concatenate(outs, axis=1)

def rwkv7_recurrence(r, decay, k, v, a_vec, b_vec):
    B, S, H, N = r.shape
    n_chunks = S // CHUNK

    def to_chunks(t):
        return t.astype(jnp.float32).transpose(1, 0, 2, 3).reshape(n_chunks, CHUNK, B, H, N)

    xs = (to_chunks(r), to_chunks(decay), to_chunks(k), to_chunks(v),
          to_chunks(a_vec), to_chunks(b_vec))

    def step(state, inp):
        r_t, w_t, k_t, v_t, a_t, b_t = inp
        sa = jnp.einsum('bhvk,bhk->bhv', state, a_t)
        state = (state * w_t[:, :, None, :] + sa[..., None] * b_t[:, :, None, :]
                 + v_t[..., None] * k_t[:, :, None, :])
        return state, jnp.einsum('bhvk,bhk->bhv', state, r_t)

    def chunk_step(state, chunk_xs):
        return lax.scan(step, state, chunk_xs)

    state0 = jnp.zeros((B, H, N, N), jnp.float32)
    _, y = lax.scan(chunk_step, state0, xs)
    return y.reshape(S, B, H, N).transpose(1, 0, 2, 3)

def rwkv7_time_mix(u, mu, w0, w2, a0, a2, g2, k_k, k_a, r_k, ln_w, ln_b):
    B, S, _ = u.shape
    u = u + (token_shift(u) - u) * mu
    x_r, x_k, x_v, x_w, x_a, x_g = jnp.split(
        u, [RW_WIDTH, 2 * RW_WIDTH, 3 * RW_WIDTH, 3 * RW_WIDTH + DECAY_LORA,
            3 * RW_WIDTH + DECAY_LORA + AAA_LORA], axis=-1)
    log_w = -jax.nn.softplus(-(w0 + jnp.tanh(x_w) @ w2)) - 0.5
    decay = jnp.exp(-jnp.exp(log_w.astype(jnp.float32)))
    a = jax.nn.sigmoid(a0 + x_a @ a2).astype(jnp.float32)
    g = jax.nn.sigmoid(x_g) @ g2

    def heads(t):
        return t.reshape(B, S, RW_HEADS, HEAD_DIM)

    r = heads(x_r).astype(jnp.float32)
    v = heads(x_v).astype(jnp.float32)
    kk = heads(x_k * k_k).astype(jnp.float32)
    kk = kk / jnp.maximum(jnp.linalg.norm(kk, axis=-1, keepdims=True), 1e-12)
    kf = heads(x_k * (1.0 + (a - 1.0) * k_a)).astype(jnp.float32)
    a = heads(a)
    y = rwkv7_recurrence(r, heads(decay), kf, v, -kk, kk * a)
    mean = jnp.mean(y, axis=-1, keepdims=True)
    var = jnp.mean(jnp.square(y - mean), axis=-1, keepdims=True)
    yn = (y - mean) * lax.rsqrt(var + LNX_EPS)
    yn = yn * ln_w.astype(jnp.float32).reshape(RW_HEADS, HEAD_DIM) + ln_b.astype(jnp.float32).reshape(RW_HEADS, HEAD_DIM)
    bonus = jnp.sum(r * kf * r_k.astype(jnp.float32), axis=-1, keepdims=True) * v
    return ((yn + bonus).reshape(B, S, RW_WIDTH) * g.astype(jnp.float32)).astype(u.dtype)

def first_inputs(seed: int = 0) -> dict:
    key = jax.random.key(seed)
    ks = jax.random.split(key, 26)
    L, D = DEPTH, D_MODEL
    f32 = jnp.float32

    def nrm(k, shape, scale):
        return scale * jax.random.normal(k, shape, f32)

    def gain(k, shape):
        return 1.0 + 0.05 * jax.random.normal(k, shape, f32)

    return {
        "x": jax.random.normal(ks[0], (BATCH, SEQ, D), f32),
        "norm_ffn1": gain(ks[1], (L, D)),
        "ffn1_gate": nrm(ks[2], (L, D, D_FF), D ** -0.5),
        "ffn1_up": nrm(ks[3], (L, D, D_FF), D ** -0.5),
        "ffn1_down": nrm(ks[4], (L, D_FF, D), D_FF ** -0.5),
        "norm_mix": gain(ks[5], (L, D)),
        "w_in": nrm(ks[6], (L, D, PROJ_WIDTH), D ** -0.5),
        "sb_q_norm": gain(ks[7], (L, HEAD_DIM)),
        "sb_k_norm": gain(ks[8], (L, HEAD_DIM)),
        "sb_out_norm": gain(ks[9], (L, SB_WIDTH)),
        "rw_mu": jax.random.uniform(ks[10], (L, RW_PROJ), f32),
        "rw_w0": jax.random.uniform(ks[11], (L, RW_WIDTH), f32, minval=-5.0, maxval=-1.0),
        "rw_w2": nrm(ks[12], (L, DECAY_LORA, RW_WIDTH), 0.5 * DECAY_LORA ** -0.5),
        "rw_a0": nrm(ks[13], (L, RW_WIDTH), 0.1),
        "rw_a2": nrm(ks[14], (L, AAA_LORA, RW_WIDTH), 0.5 * AAA_LORA ** -0.5),
        "rw_g2": nrm(ks[15], (L, GATE_LORA, RW_WIDTH), GATE_LORA ** -0.5),
        "rw_k_k": 0.85 + 0.05 * jax.random.normal(ks[16], (L, RW_WIDTH), f32),
        "rw_k_a": gain(ks[17], (L, RW_WIDTH)),
        "rw_r_k": nrm(ks[18], (L, RW_HEADS, HEAD_DIM), 0.1),
        "rw_ln_w": gain(ks[19], (L, RW_WIDTH)),
        "rw_ln_b": nrm(ks[20], (L, RW_WIDTH), 0.01),
        "w_out": nrm(ks[21], (L, D_MIX, D), D_MIX ** -0.5),
        "norm_ffn2": gain(ks[22], (L, D)),
        "ffn2_gate": nrm(ks[23], (L, D, D_FF), D ** -0.5),
        "ffn2_up": nrm(ks[24], (L, D, D_FF), D ** -0.5),
        "ffn2_down": nrm(ks[25], (L, D_FF, D), D_FF ** -0.5),
    }

def first_block(x, norm_ffn1, ffn1_gate, ffn1_up, ffn1_down, norm_mix, w_in,
              sb_q_norm, sb_k_norm, sb_out_norm, rw_mu, rw_w0, rw_w2, rw_a0, rw_a2,
              rw_g2, rw_k_k, rw_k_a, rw_r_k, rw_ln_w, rw_ln_b, w_out, norm_ffn2,
              ffn2_gate, ffn2_up, ffn2_down):
    B, S, _ = x.shape
    for l in range(DEPTH):
        x = x + FFN_HALF * swiglu(rms_norm(x, norm_ffn1[l]), ffn1_gate[l], ffn1_up[l], ffn1_down[l])

        h = rms_norm(x, norm_mix[l])
        p = h @ w_in[l]
        sb_q, sb_k, sb_v, rw_in = jnp.split(p, [SB_WIDTH, 2 * SB_WIDTH, 3 * SB_WIDTH], axis=-1)

        q = rms_norm(sb_q.reshape(B, S, SB_HEADS, HEAD_DIM), sb_q_norm[l])
        k = rms_norm(sb_k.reshape(B, S, SB_HEADS, HEAD_DIM), sb_k_norm[l])
        v = sb_v.reshape(B, S, SB_HEADS, HEAD_DIM)
        o_sb = stick_breaking_attention(q, k, v)
        o_sb = rms_norm(o_sb, sb_out_norm[l].reshape(SB_HEADS, HEAD_DIM)).reshape(B, S, SB_WIDTH)

        o_rw = rwkv7_time_mix(rw_in, rw_mu[l], rw_w0[l], rw_w2[l], rw_a0[l], rw_a2[l], rw_g2[l],
                              rw_k_k[l], rw_k_a[l], rw_r_k[l], rw_ln_w[l], rw_ln_b[l])

        x = x + jnp.concatenate([o_sb, o_rw], axis=-1) @ w_out[l]

        x = x + FFN_HALF * swiglu(rms_norm(x, norm_ffn2[l]), ffn2_gate[l], ffn2_up[l], ffn2_down[l])
    return x


GRID_W = 64
CTX_LEN = 256
A_HEADS = 8
A_KV_HEADS = 2
A_GROUPS = A_HEADS // A_KV_HEADS
B_HEADS = 8
B_KV_HEADS = 2
B_GROUPS = B_HEADS // B_KV_HEADS
WINDOW = 128
BLOCK = 128
ROPE_THETA = 10000.0
CONV_WIDTH = 3
LN_EPS = 1e-5
QK_EPS = 1e-6
N_MOD = 6
DEEPNORM_ALPHA = (2.0 * DEPTH) ** 0.25
DEEPNORM_BETA = (8.0 * DEPTH) ** -0.25

OFF_QA = 0
OFF_KA = OFF_QA + A_HEADS * HEAD_DIM
OFF_VA = OFF_KA + A_KV_HEADS * HEAD_DIM
OFF_QB = OFF_VA + A_KV_HEADS * HEAD_DIM
OFF_KB = OFF_QB + B_HEADS * HEAD_DIM
OFF_VB = OFF_KB + B_KV_HEADS * HEAD_DIM
OFF_GA = OFF_VB + B_KV_HEADS * HEAD_DIM
OFF_GB = OFF_GA + D_MODEL
IN_COLS = OFF_GB + D_MODEL


def _layer_norm(x, g, b):
    xf = x.astype(jnp.float32)
    mu = jnp.mean(xf, axis=-1, keepdims=True)
    var = jnp.mean(jnp.square(xf - mu), axis=-1, keepdims=True)
    return ((xf - mu) * lax.rsqrt(var + LN_EPS) * g + b).astype(x.dtype)

def _qk_rms(t, g):
    tf = t.astype(jnp.float32)
    return (tf * lax.rsqrt(jnp.mean(tf * tf, axis=-1, keepdims=True) + QK_EPS) * g).astype(t.dtype)

def _axial_rope_tables(n_tok, dtype):
    pos = jnp.arange(n_tok, dtype=jnp.int32)
    rows = (pos // GRID_W).astype(jnp.float32)
    cols = (pos % GRID_W).astype(jnp.float32)
    n_freq = HEAD_DIM // 4
    inv_freq = ROPE_THETA ** (-jnp.arange(n_freq, dtype=jnp.float32) / n_freq)
    ang_r = rows[:, None, None] * inv_freq
    ang_c = cols[:, None, None] * inv_freq
    return (jnp.cos(ang_r).astype(dtype), jnp.sin(ang_r).astype(dtype),
            jnp.cos(ang_c).astype(dtype), jnp.sin(ang_c).astype(dtype))

def _rotate_half(t, cos, sin):
    t1, t2 = jnp.split(t, 2, axis=-1)
    return jnp.concatenate([t1 * cos - t2 * sin, t2 * cos + t1 * sin], axis=-1)

def _rope_2d(t, tables):
    cos_r, sin_r, cos_c, sin_c = tables
    t_row, t_col = jnp.split(t, 2, axis=-1)
    return jnp.concatenate([_rotate_half(t_row, cos_r, sin_r), _rotate_half(t_col, cos_c, sin_c)], axis=-1)

def _gqa_scores(q, k):
    return jnp.einsum("bqhgd,bkhd->bhgqk", q, k).astype(jnp.float32) * (HEAD_DIM ** -0.5)

def _gqa_values(p, v):
    return jnp.einsum("bhgqk,bkhd->bqhgd", p.astype(v.dtype), v)

def _sink_softmax(scores, sink):
    sink = sink.astype(jnp.float32)[:, :, None, None]
    m = jnp.maximum(jnp.max(scores, axis=-1, keepdims=True), sink)
    e = jnp.exp(scores - m)
    return e / (jnp.sum(e, axis=-1, keepdims=True) + jnp.exp(sink - m))

def _windowed_attention(q, k, v, k_ctx, v_ctx, sink):
    bsz, n_tok = q.shape[:2]
    pad = ((0, 0), (BLOCK, BLOCK), (0, 0), (0, 0))
    k_pad = jnp.pad(k, pad)
    v_pad = jnp.pad(v, pad)
    ctx_mask = jnp.ones((BLOCK, k_ctx.shape[1]), dtype=bool)

    def one_block(i):
        start = i * BLOCK
        q_blk = lax.dynamic_slice_in_dim(q, start, BLOCK, axis=1)
        k_blk = jnp.concatenate([lax.dynamic_slice_in_dim(k_pad, start, 3 * BLOCK, axis=1), k_ctx], axis=1)
        v_blk = jnp.concatenate([lax.dynamic_slice_in_dim(v_pad, start, 3 * BLOCK, axis=1), v_ctx], axis=1)
        q_pos = start + jnp.arange(BLOCK)
        k_pos = start - BLOCK + jnp.arange(3 * BLOCK)
        band = ((jnp.abs(q_pos[:, None] - k_pos[None, :]) <= WINDOW)
                & (k_pos[None, :] >= 0) & (k_pos[None, :] < n_tok))
        mask = jnp.concatenate([band, ctx_mask], axis=1)
        scores = jnp.where(mask, _gqa_scores(q_blk, k_blk), -jnp.inf)
        return _gqa_values(_sink_softmax(scores, sink), v_blk)

    out = lax.map(one_block, jnp.arange(n_tok // BLOCK))
    return jnp.moveaxis(out, 0, 1).reshape(bsz, n_tok, -1)

def _global_attention(q, k_all, v_all):
    bsz, n_tok = q.shape[:2]

    def one_block(i):
        q_blk = lax.dynamic_slice_in_dim(q, i * BLOCK, BLOCK, axis=1)
        p = jax.nn.softmax(_gqa_scores(q_blk, k_all), axis=-1)
        return _gqa_values(p, v_all)

    out = lax.map(one_block, jnp.arange(n_tok // BLOCK))
    return jnp.moveaxis(out, 0, 1).reshape(bsz, n_tok, -1)

def _merge_branches(o_a, o_b, gate_logits, w_branch_a, w_branch_b, w_out):
    g_a, g_b = jnp.split(jax.nn.sigmoid(gate_logits), 2, axis=-1)
    return (g_a * (o_a @ w_branch_a) + g_b * (o_b @ w_branch_b)) @ w_out

def _context_kv(h_c, w_in, b_in, k_norm_g):
    bsz, n_ctx, _ = h_c.shape
    kv_a = (h_c @ w_in[:, OFF_KA:OFF_QB] + b_in[OFF_KA:OFF_QB]).reshape(bsz, n_ctx, 2 * A_KV_HEADS, HEAD_DIM)
    kv_b = (h_c @ w_in[:, OFF_KB:OFF_GA] + b_in[OFF_KB:OFF_GA]).reshape(bsz, n_ctx, 2 * B_KV_HEADS, HEAD_DIM)
    k_a, v_a = jnp.split(kv_a, 2, axis=2)
    k_b, v_b = jnp.split(kv_b, 2, axis=2)
    return (k_a, v_a, _qk_rms(k_b, k_norm_g), v_b)

def _latent_token_mixer(h, kv_ctx, w_in, b_in, sink, q_norm_g, k_norm_g,
                        w_branch_a, w_branch_b, w_out, rope):
    bsz, n_tok, _ = h.shape
    k_a_c, v_a_c, k_b_c, v_b_c = kv_ctx
    proj = h @ w_in + b_in

    def heads(lo, hi, n):
        return proj[..., lo:hi].reshape(bsz, n_tok, n, HEAD_DIM)

    q_a = _rope_2d(heads(OFF_QA, OFF_KA, A_HEADS), rope).reshape(bsz, n_tok, A_KV_HEADS, A_GROUPS, HEAD_DIM)
    k_a = _rope_2d(heads(OFF_KA, OFF_VA, A_KV_HEADS), rope)
    v_a = heads(OFF_VA, OFF_QB, A_KV_HEADS)
    q_b = _rope_2d(_qk_rms(heads(OFF_QB, OFF_KB, B_HEADS), q_norm_g), rope).reshape(
        bsz, n_tok, B_KV_HEADS, B_GROUPS, HEAD_DIM)
    k_b = _rope_2d(_qk_rms(heads(OFF_KB, OFF_VB, B_KV_HEADS), k_norm_g), rope)
    v_b = heads(OFF_VB, OFF_GA, B_KV_HEADS)
    o_a = _windowed_attention(q_a, k_a, v_a, k_a_c, v_a_c, sink.reshape(A_KV_HEADS, A_GROUPS))
    o_b = _global_attention(q_b, jnp.concatenate([k_b, k_b_c], axis=1), jnp.concatenate([v_b, v_b_c], axis=1))
    return _merge_branches(o_a, o_b, proj[..., OFF_GA:], w_branch_a, w_branch_b, w_out)

def _context_token_mixer(h_c, kv_ctx, w_in, b_in, sink, q_norm_g, w_branch_a, w_branch_b, w_out):
    bsz, n_ctx, _ = h_c.shape
    k_a_c, v_a_c, k_b_c, v_b_c = kv_ctx
    q_a = (h_c @ w_in[:, OFF_QA:OFF_KA] + b_in[OFF_QA:OFF_KA]).reshape(bsz, n_ctx, A_KV_HEADS, A_GROUPS, HEAD_DIM)
    q_b = _qk_rms((h_c @ w_in[:, OFF_QB:OFF_KB] + b_in[OFF_QB:OFF_KB]).reshape(bsz, n_ctx, B_HEADS, HEAD_DIM),
                  q_norm_g).reshape(bsz, n_ctx, B_KV_HEADS, B_GROUPS, HEAD_DIM)
    gate_logits = h_c @ w_in[:, OFF_GA:] + b_in[OFF_GA:]
    o_a = _gqa_values(_sink_softmax(_gqa_scores(q_a, k_a_c), sink.reshape(A_KV_HEADS, A_GROUPS)), v_a_c)
    o_b = _gqa_values(jax.nn.softmax(_gqa_scores(q_b, k_b_c), axis=-1), v_b_c)
    return _merge_branches(o_a.reshape(bsz, n_ctx, -1), o_b.reshape(bsz, n_ctx, -1), gate_logits,
                           w_branch_a, w_branch_b, w_out)

def _conv_ffn(h, w_up, conv_w, conv_b, w_down):
    u = h @ w_up
    half = CONV_WIDTH // 2
    u = lax.conv_general_dilated(u, conv_w[:, None, :], window_strides=(1,), padding=((half, half),),
                                 dimension_numbers=("NWC", "WIO", "NWC"),
                                 feature_group_count=u.shape[-1]) + conv_b
    gate, val = jnp.split(u, 2, axis=-1)
    return (jax.nn.silu(gate) * val) @ w_down

def second_inputs(seed: int = 0) -> dict:
    key = jax.random.key(seed)
    ks = jax.random.split(key, 24)
    f32 = jnp.float32

    def normal(k, shape, scale):
        return jax.random.normal(k, shape, f32) * scale

    L = DEPTH
    return {
        "x": normal(ks[0], (BATCH, SEQ, D_MODEL), 1.0),
        "c": normal(ks[1], (BATCH, D_MODEL), 1.0),
        "ctx": normal(ks[2], (BATCH, CTX_LEN, D_MODEL), 1.0),
        "c_ctx": normal(ks[3], (D_MODEL,), 1.0),
        "w_mod": normal(ks[4], (L, D_MODEL, N_MOD * D_MODEL), 0.5 * D_MODEL ** -0.5),
        "b_mod": normal(ks[5], (L, N_MOD * D_MODEL), 0.02),
        "w_in": normal(ks[6], (L, D_MODEL, IN_COLS), D_MODEL ** -0.5),
        "b_in": normal(ks[7], (L, IN_COLS), 0.02),
        "attn_sink": normal(ks[8], (L, A_HEADS), 0.5),
        "q_norm_g": 1.0 + normal(ks[9], (L, HEAD_DIM), 0.05),
        "k_norm_g": 1.0 + normal(ks[10], (L, HEAD_DIM), 0.05),
        "w_branch_a": normal(ks[11], (L, A_HEADS * HEAD_DIM, D_MODEL), (A_HEADS * HEAD_DIM) ** -0.5),
        "w_branch_b": normal(ks[12], (L, B_HEADS * HEAD_DIM, D_MODEL), (B_HEADS * HEAD_DIM) ** -0.5),
        "w_out": normal(ks[13], (L, D_MODEL, D_MODEL), DEEPNORM_BETA * D_MODEL ** -0.5),
        "ln1_g": 1.0 + normal(ks[14], (L, D_MODEL), 0.05),
        "ln1_b": normal(ks[15], (L, D_MODEL), 0.02),
        "w_up": normal(ks[16], (L, D_MODEL, 2 * D_FF), D_MODEL ** -0.5),
        "conv_w": normal(ks[17], (L, CONV_WIDTH, 2 * D_FF), CONV_WIDTH ** -0.5),
        "conv_b": normal(ks[18], (L, 2 * D_FF), 0.02),
        "w_down": normal(ks[19], (L, D_FF, D_MODEL), DEEPNORM_BETA * D_FF ** -0.5),
        "ln2_g": 1.0 + normal(ks[20], (L, D_MODEL), 0.05),
        "ln2_b": normal(ks[21], (L, D_MODEL), 0.02),
    }

def second_block(x, c, ctx, c_ctx, w_mod, b_mod, w_in, b_in, attn_sink, q_norm_g, k_norm_g,
              w_branch_a, w_branch_b, w_out, ln1_g, ln1_b, w_up, conv_w, conv_b, w_down,
              ln2_g, ln2_b):
    n_tok = x.shape[1]
    rope = _axial_rope_tables(n_tok, x.dtype)
    for l in range(DEPTH):
        last = l == DEPTH - 1
        mod = jax.nn.silu(c) @ w_mod[l] + b_mod[l]
        shift1, scale1, gate1, shift2, scale2, gate2 = jnp.split(mod[:, None, :], N_MOD, axis=-1)
        n_mod_c = 2 if last else N_MOD
        mod_c = jax.nn.silu(c_ctx) @ w_mod[l, :, :n_mod_c * D_MODEL] + b_mod[l, :n_mod_c * D_MODEL]
        mods_c = jnp.split(mod_c, n_mod_c)
        h_c = ctx * (1.0 + mods_c[1]) + mods_c[0]
        kv_ctx = _context_kv(h_c, w_in[l], b_in[l], k_norm_g[l])

        h = x * (1.0 + scale1) + shift1
        y = _latent_token_mixer(h, kv_ctx, w_in[l], b_in[l], attn_sink[l], q_norm_g[l], k_norm_g[l],
                                w_branch_a[l], w_branch_b[l], w_out[l], rope)
        x = _layer_norm(DEEPNORM_ALPHA * x + gate1 * y, ln1_g[l], ln1_b[l])

        h = x * (1.0 + scale2) + shift2
        y = _conv_ffn(h, w_up[l], conv_w[l], conv_b[l], w_down[l])
        x = _layer_norm(DEEPNORM_ALPHA * x + gate2 * y, ln2_g[l], ln2_b[l])

        if not last:
            y_c = _context_token_mixer(h_c, kv_ctx, w_in[l], b_in[l], attn_sink[l], q_norm_g[l],
                                       w_branch_a[l], w_branch_b[l], w_out[l])
            ctx = _layer_norm(DEEPNORM_ALPHA * ctx + mods_c[2] * y_c, ln1_g[l], ln1_b[l])
            h_c = ctx * (1.0 + mods_c[4]) + mods_c[3]
            y_c = _conv_ffn(h_c, w_up[l], conv_w[l], conv_b[l], w_down[l])
            ctx = _layer_norm(DEEPNORM_ALPHA * ctx + mods_c[5] * y_c, ln2_g[l], ln2_b[l])
    return x


def setup_inputs(seed=0):
    out = dict(first_inputs(seed))
    for name, value in second_inputs(seed + 1).items():
        if name != "x":
            out[name + "_2"] = value
    return out


def reference(
    x, norm_ffn1, ffn1_gate, ffn1_up, ffn1_down, norm_mix, w_in, sb_q_norm, sb_k_norm,
    sb_out_norm, rw_mu, rw_w0, rw_w2, rw_a0, rw_a2, rw_g2, rw_k_k, rw_k_a, rw_r_k, rw_ln_w,
    rw_ln_b, w_out, norm_ffn2, ffn2_gate, ffn2_up, ffn2_down, c_2, ctx_2, c_ctx_2, w_mod_2,
    b_mod_2, w_in_2, b_in_2, attn_sink_2, q_norm_g_2, k_norm_g_2, w_branch_a_2, w_branch_b_2,
    w_out_2, ln1_g_2, ln1_b_2, w_up_2, conv_w_2, conv_b_2, w_down_2, ln2_g_2, ln2_b_2,
):
    x = first_block(
        x, norm_ffn1, ffn1_gate, ffn1_up, ffn1_down, norm_mix, w_in, sb_q_norm, sb_k_norm,
        sb_out_norm, rw_mu, rw_w0, rw_w2, rw_a0, rw_a2, rw_g2, rw_k_k, rw_k_a, rw_r_k, rw_ln_w,
        rw_ln_b, w_out, norm_ffn2, ffn2_gate, ffn2_up, ffn2_down,
    )
    return second_block(
        x, c_2, ctx_2, c_ctx_2, w_mod_2, b_mod_2, w_in_2, b_in_2, attn_sink_2, q_norm_g_2,
        k_norm_g_2, w_branch_a_2, w_branch_b_2, w_out_2, ln1_g_2, ln1_b_2, w_up_2, conv_w_2,
        conv_b_2, w_down_2, ln2_g_2, ln2_b_2,
    )


_drawn_inputs = setup_inputs


def setup_inputs(seed=0):
    import zlib

    import numpy as np

    out = dict(_drawn_inputs(seed))
    spreads = {}
    factors = {'sb_q_norm': 4.313,
     'sb_k_norm': 4.529,
     'rw_w2': 6.397,
     'rw_a0': 4.218,
     'rw_k_k': 5.569,
     'rw_k_a': 3.489,
     'rw_ln_w': 4.018,
     'rw_ln_b': 8.0,
     'norm_ffn2': 3.541,
     'ctx_2': 8.0,
     'c_ctx_2': 5.106,
     'b_mod_2': 6.092,
     'b_in_2': 8.0,
     'attn_sink_2': 8.0,
     'q_norm_g_2': 8.0,
     'k_norm_g_2': 8.0,
     'w_branch_b_2': 3.617,
     'ln1_b_2': 2.872,
     'conv_b_2': 8.0,
     'ln2_b_2': 2.851}
    for name, (base, spread) in spreads.items():
        noise = np.random.default_rng([zlib.crc32(name.encode()), seed]).standard_normal(out[name].shape)
        drawn = base * np.exp(spread * noise) if base else spread * noise
        out[name] = jnp.asarray(drawn.astype(out[name].dtype))
    for name, factor in factors.items():
        out[name] = (out[name] * factor).astype(out[name].dtype)
    return out
```

```python
from contextlib import ExitStack

import concourse.bass as bass
from concourse import mybir

F32 = mybir.dt.float32
F32R = mybir.dt.float32r
BF16 = mybir.dt.bfloat16
ALU = mybir.AluOpType
ACT = mybir.ActivationFunctionType
ds = bass.ds

P = 128
SEQ = 256
TB = SEQ // P
D = 1024
KT = D // P
HALF = D // 2
D_FF = 2816
PAIRS = D_FF // (2 * P)
SLAB = 2048
RING = 3

N_FFN = 3 * PAIRS
N_WIN, N_MOD, N_OUT, N_CTX, N_WIN2, N_BRANCH = 13, 24, 4, 2, 14, 4
B_FFN1 = 0
B_WIN = B_FFN1 + N_FFN
B_MOD = B_WIN + N_WIN
B_OUT1 = B_MOD + N_MOD
B_CTX = B_OUT1 + N_OUT
B_FFN2 = B_CTX + N_CTX
B_WIN2 = B_FFN2 + N_FFN
B_BRANCH = B_WIN2 + N_WIN2
B_OUT2 = B_BRANCH + N_BRANCH
B_FFN3 = B_OUT2 + N_OUT
N_SLABS = B_FFN3 + N_FFN
S_FFN1, S_WIN = B_FFN1, B_WIN
S_OUT1, S_CTX, S_FFN2, S_WIN2, S_BRANCH, S_OUT2, S_FFN3 = (
    b - N_MOD for b in (B_OUT1, B_CTX, B_FFN2, B_WIN2, B_BRANCH, B_OUT2, B_FFN3))
N_SPLIT = N_SLABS - N_MOD

RMS_EPS = 1e-6
LN_EPS = 1e-5
LNX_EPS = 64e-5
DECAY_SCALE = 0.6065306597126334
DEEPNORM_ALPHA = 2.0 ** 0.25
HEAD = 64
SCALE = HEAD ** -0.5
NEG = -1.0e30
LEAD = 1
ACTS, VECS, POOLS = 9, 12, 5

V = {}
_at = 0
for _name, _n in (("g1", KT), ("g2", KT), ("g3", KT), ("sbq", 1), ("sbk", 1), ("sbo", 4), ("mu", 14),
                  ("w0", 4), ("a0", 4), ("kk", 4), ("ka", 4), ("rk", 4), ("lnw", 4), ("lnb", 4),
                  ("c", 2 * KT), ("bmod", 48), ("b2", 26), ("qg", 1), ("kg", 1), ("conv", 16 * (PAIRS + 1))):
    V[_name] = _at
    _at += _n
N_VEC = _at

C_ALL = {"ident": (0, 128), "ones": (128, 128), "heads": (256, 64), "spread": (320, 512)}
N_ALL = 832
C_MIX = {"mask2": (0, 256), "lower": (256, 128), "same16": (384, 128), "only32": (512, 128), "only64": (640, 128),
         "suffix": (768, 128), "minus": (896, 128), "sbmask": (1024, 384), "sbneg": (1408, 384),
         "block": (1792, 128), "mean": (1920, 128), "chunk": (2048, 256)}
N_MIX = 2304
C_ATT = {"cos": (0, 256), "sin": (256, 256), "rot": (512, 128), "band": (640, 256)}
N_ATT = 896
N_ROW = 4 * D + 256 + 8


def build_block(nc, slabs, x, ctx_t, vecs, c_all, c_mix, c_att, lora, rows, out):
    stack = ExitStack()
    with stack:
        def sb(name, shape, dt=F32, where=stack):
            return where.enter_context(nc.sbuf_tensor(name, shape, dt))

        def sem(name):
            return stack.enter_context(nc.semaphore(name))

        stage = sb("stage", [P, RING, SLAB])
        X = sb("x_res", [P, TB, D])
        HF = sb("h_full", [P, KT, SEQ])
        VEC = sb("vec", [P, N_VEC])
        CA = sb("c_all_sb", [P, N_ALL])
        ZERO = sb("zero", [P, 512], BF16)
        MODV = sb("mod_v", [P, 48, 2])
        SC = sb("silu_c", [P, KT, 2])
        BN = sb("bn", [P, TB, 2, 6])
        SM = sb("small", [P, 128])
        EPS = sb("eps", [P, 4])
        MODP = sb("mod_p", [P, 48, 2])
        ident = CA[:, 0:128]
        ones = CA[:, 128:256]

        def spread(j):
            return CA[0:16, 320 + j * 128:448 + j * 128]

        def heads(j):
            return CA[:, 256 + 16 * j:272 + 16 * j]

        w_mix = ExitStack()
        ANV = sb("anv", [P, TB, 8, 128], where=w_mix)
        BTOK = sb("b_tok", [P, TB, 512], where=w_mix)
        KTOK = sb("k_tok", [P, TB, 512], where=w_mix)
        VTOK = sb("v_tok", [P, TB, 512], where=w_mix)
        NR = sb("n_r", [P, 16, 256], where=w_mix)
        MB = sb("m_b", [P, 16, 256], where=w_mix)
        AU = sb("a_u", [P, TB, 8, 128], where=w_mix)
        RT = sb("r_t", [P, 4, SEQ], where=w_mix)
        w_mix.close()
        WHI = sb("w_hi", [P, RING, SLAB], F32R)
        WLO = sb("w_lo", [P, RING, SLAB], F32R)
        HHI = sb("h_hi", [P, KT, SEQ], F32R)
        HLO = sb("h_lo", [P, KT, SEQ], F32R)

        a_mix = ExitStack()
        U = sb("u", [P, 22, SEQ], where=a_mix)
        SBV = sb("sb_v", [P, TB, 512], where=a_mix)
        early = ExitStack()
        EA = sb("e_a", [P, 4, SEQ], where=early)
        ER = sb("e_r", [P, 4, SEQ], where=early)
        EI = sb("e_i", [P, 4, SEQ], where=early)
        AA = sb("aa", [P, 4, SEQ], where=early)
        KK = sb("kk", [P, 4, SEQ], where=early)
        SQ = sb("sq", [P, 4, SEQ], where=early)
        DT = sb("d_t", [P, 2, SEQ], where=early)
        LW = sb("lw", [P, SEQ], where=early)
        LG = sb("lg", [P, SEQ], where=early)
        early.close()
        sbt = ExitStack()
        ZT = sb("z_t", [P, 4, 384], where=sbt)
        LT = sb("l_t", [P, 4, 384], where=sbt)
        SQ2 = sb("sq2", [P, 4, SEQ], where=sbt)
        OS = sb("o_s", [P, 4, SEQ], where=sbt)
        sbt.close()
        yset = ExitStack()
        YS = sb("y_s", [P, 4, SEQ], where=yset)
        YC = sb("y_c", [P, 4, SEQ], where=yset)
        YQ = sb("y_q", [P, 4, SEQ], where=yset)
        yset.close()
        T = [[sb(f"t{lane}_{n}", [P, 4, 128], where=a_mix) for n in range(7)] for lane in range(2)]
        RKR = sb("rkr", [P, 4, SEQ], where=a_mix)
        AR = sb("a_r", [P, 8, 2, 128], where=a_mix)
        BH = sb("b_h", [P, 4, SEQ], where=a_mix)
        KH = sb("k_h", [P, 4, SEQ], where=a_mix)
        CM = sb("c_mix_sb", [P, N_MIX], where=a_mix)
        LORA = sb("lora", [P, 2, 512], where=a_mix)
        ET = sb("e_t", [P, 2, 4, HEAD], where=a_mix)
        ST = sb("s_t", [P, 3, 4, HEAD], where=a_mix)
        DL = sb("d_l", [P, 4, 4], where=a_mix)
        KA1 = sb("k_a1", [P, 4], where=a_mix)
        RN = sb("r_n", [16, 2, SEQ], where=a_mix)
        a_mix.close()

        a_att = ExitStack()
        KALL = sb("k_all", [P, 2, 2 * SEQ], where=a_att)
        VALL = sb("v_all", [P, 4, 256], where=a_att)
        ROW = sb("row", [P, 2 * D], where=a_att)
        ROWS = sb("row_small", [P, 264], where=a_att)
        GB = sb("gate_b", [P, 2, D], where=a_att)
        CT = sb("c_att_sb", [P, N_ATT], where=a_att)
        ffn = ExitStack()
        XS = sb("x_s", [P, TB, D], where=ffn)
        SG = sb("s_g", [P, 2, 2, SEQ], where=ffn)
        HID = sb("hid", [P, 2, 2, SEQ], where=ffn)
        DHI = sb("d_hi", [P, 2, 2, SEQ], F32R, where=ffn)
        DLO = sb("d_lo", [P, 2, 2, SEQ], F32R, where=ffn)
        CG = sb("c_g", [P, 2, 4, SEQ], where=ffn)
        CW = sb("c_w", [P, 2, 16], where=ffn)
        CX = sb("ctx_f", [P, KT, SEQ], where=ffn)
        CHI = sb("ctx_hi", [P, KT, SEQ], F32R, where=ffn)
        CLO = sb("ctx_lo", [P, KT, SEQ], F32R, where=ffn)
        DG = sb("d_g", [P, 2, 4, 128], where=ffn)
        ffn.close()
        att = ExitStack()
        GT = sb("gate_t", [P, 16, SEQ], where=att)
        QR = sb("q_raw", [P, 10, SEQ], where=att)
        att2 = ExitStack()
        QN = sb("q_n", [P, 8, SEQ], where=att2)
        PM = sb("p_m", [P, 2, 2, 512], where=att2)
        PT = sb("p_t", [P, 2, 2, 512], where=att2)
        OT = sb("o_tok", [P, TB, D], where=att2)
        TR = sb("t_r", [P, 4, SEQ], where=att2)
        TK = sb("t_k", [P, 2, SEQ], where=att2)
        NS = sb("n_s", [P, 8], where=att2)
        RA = sb("r_a", [16, 768], where=att2)
        att2.close()
        MF = sb("m_f", [P, KT, SEQ], where=att)
        MHI = sb("m_hi", [P, KT, SEQ], F32R, where=att)
        MLO = sb("m_lo", [P, KT, SEQ], F32R, where=att)
        MT = sb("m_t", [P, 4, SEQ], where=att)
        YT = sb("y_t", [P, TB, D], where=att)
        att.close()
        a_att.close()

        PS = stack.enter_context(nc.psum_tensor("psum", [P, 8, 512], F32))

        stage_ready = [sem(f"stage_ready{n}") for n in range(RING)]
        stage_free = [sem(f"stage_free{n}") for n in range(RING)]
        hi_ready = sem("hi_ready")
        lo_ready = sem("lo_ready")
        slabs_used = sem("slabs_used")
        silu_done = sem("silu_done")
        hidden_done = sem("hidden_done")
        hid_hi = sem("hid_hi")
        hid_lo = sem("hid_lo")
        act_step = sem("act_step")
        vec_step = sem("vec_step")
        x_loaded = sem("x_loaded")
        vec_loaded = sem("vec_loaded")
        zero_ready = sem("zero_ready")
        eps_ready = sem("eps_ready")
        x_new = sem("x_new")
        sq_sum = sem("sq_sum")
        root = sem("root")
        xs_ready = sem("xs_ready")
        x_turned = sem("x_turned")
        h_full = sem("h_full_ready")
        h_hi = sem("h_hi_ready")
        h_lo = sem("h_lo_ready")
        out_done = sem("out_done")
        mix_loaded = sem("mix_loaded")
        u_copied = sem("u_copied")
        shifted = sem("shifted")
        lora_in = sem("lora_in")
        lora_done = sem("lora_done")
        sigma_ready = sem("sigma_ready")
        decay_ready = sem("decay_ready")
        exp_ready = sem("exp_ready")
        head_sum = sem("head_sum")
        head_root = sem("head_root")
        head_rn = sem("head_rn")
        head_spread = sem("head_spread")
        feature = sem("feature")
        gate_copied = sem("gate_copied")
        qk_square = sem("qk_square")
        qk_ready = sem("qk_ready")
        sbv_ready = sem("sbv_ready")
        tok_turned = sem("tok_turned")
        tok_copied = sem("tok_copied")
        z_ready = sem("z_ready")
        ln_ready = sem("ln_ready")
        l_ready = sem("l_ready")
        e_ready = sem("e_ready")
        e_masked = sem("e_masked")
        att_ready = sem("att_ready")
        o_ready = sem("o_ready")
        o_copied = sem("o_copied")
        u_pe = [sem(f"unit_products{n}") for n in range(2)]
        u_act = [sem(f"unit_act{n}") for n in range(2)]
        u_vec = [sem(f"unit_vec{n}") for n in range(2)]
        u_pool = [sem(f"unit_pool{n}") for n in range(2)]
        s_products = sem("state_products")
        s_ready = sem("state_ready")
        y_products = sem("y_products")
        y_step = sem("y_step")
        cat_ready = sem("cat_ready")
        cat_hi = sem("cat_hi")
        cat_lo = sem("cat_lo")
        mod_done = sem("mod_done")
        mod_ready = sem("mod_ready")
        att_loaded = sem("att_loaded")
        row_loaded = sem("row_loaded")
        gate_diag = sem("gate_diag")
        gate_rows = sem("gate_rows")
        gate_row_copied = sem("gate_row_copied")
        ctx_full = sem("ctx_full")
        ctx_hi = sem("ctx_hi")
        ctx_lo = sem("ctx_lo")
        ctx_copied = sem("ctx_copied")
        p_copied = sem("p_copied")
        v_copied = sem("v_copied")
        k_square = sem("k_square")
        rope_in = sem("rope_in")
        rotated = sem("rotated")
        roped = sem("roped")
        scored = sem("scored")
        max_done = sem("max_done")
        sink_in = sem("sink_in")
        sink_exp = sem("sink_exp")
        p_ready = sem("p_ready")
        p_turned = sem("p_turned")
        pt_act = sem("pt_act")
        pt_vec = sem("pt_vec")
        pv_done = sem("pv_done")
        o_scaled = sem("o_scaled")
        merged = sem("merged")
        m_hi = sem("m_hi")
        m_lo = sem("m_lo")
        ln_var = sem("ln_var")
        ln_root = sem("ln_root")
        center = sem("center")
        tap_before = sem("tap_before")
        conv_done = sem("conv_done")
        taps_ready = sem("taps_ready")

        block = stack.enter_context(nc.Block())

        def slot_of(s):
            return s % RING

        def shift(s):
            return N_MOD if s >= S_OUT1 else 0

        def mixc(name):
            a, n = C_MIX[name]
            return CM[:, a:a + n]

        def vcol(name, j=0):
            return VEC[:, V[name] + j:V[name] + j + 1]

        def over(ap, n, at=1):
            return ap.unsqueeze(at).broadcast_to([P, n, ap.shape[1]] if at == 1 else [P, ap.shape[1], n])

        def unit_heads(g):
            return [4 * g + h for h in (0, 2, 1, 3)]

        @block.sync
        def _(sp):
            sp.dma_start(X[:, :, :], x.rearrange("t p n -> p t n")).then_inc(x_loaded, 16)
            sp.dma_start(VEC[:, :], vecs).then_inc(vec_loaded, 16)
            sp.dma_start(CA[:, :], c_all).then_inc(vec_loaded, 16)
            for i in range(RING):
                sp.dma_start(stage[:, i, :], slabs[i, :, :]).then_inc(stage_ready[i], 16)
            sp.dma_start(CM[:, :], c_mix).then_inc(mix_loaded, 16)
            sp.dma_start(LORA[:, :, :], lora).then_inc(mix_loaded, 16)
            full = N_SLABS // RING
            with sp.Fori(1, full) as i:
                for j in range(RING):
                    sp.wait_ge(stage_free[j], i)
                    sp.dma_start(stage[:, j, :], slabs[ds(i * RING + j, 1), :, :].rearrange("a p n -> (a p) n"))\
                      .then_inc(stage_ready[j], 16)
            for s in range(full * RING, N_SLABS):
                sp.wait_ge(stage_free[s % RING], full)
                sp.dma_start(stage[:, s % RING, :], slabs[s, :, :]).then_inc(stage_ready[s % RING], 16)
            sp.wait_ge(x_new, 20)
            sp.dma_start(out.rearrange("t p n -> p t n"), X[:, :, :]).then_inc(out_done, 16)
            sp.wait_ge(out_done, 16)

        @block.gpsimd
        def _(pool):
            pool.memset(ZERO[:, :], 0.0).then_inc(zero_ready, 1)
            for half in range(2):
                for n in (2, 5):
                    for lane in range(2):
                        t = T[lane]
                        at = 8 * half + 4 * lane

                        def part(to, src, mask, op=ALU.mult):
                            pool.tensor_tensor(to[:, :, :], src, over(mask, 4), op).then_inc(u_pool[lane], 1)

                        if n == 2:
                            pool.wait_ge(u_vec[lane], VECS * half + 3)
                            if half:
                                pool.wait_ge(u_pe[lane], 12 * half)
                            part(t[2], t[0][:, :, :], mixc("same16"))
                            part(t[1], MB[:, at:at + 4, 0:128], mixc("same16"))
                            pool.wait_ge(u_pool[lane], POOLS * half + 2)
                            part(t[5], t[1][:, :, :], ident, ALU.add)
                        else:
                            pool.wait_ge(u_pe[lane], 12 * half + 4)
                            part(t[4], t[0][:, :, :], mixc("only32"))
                            pool.wait_ge(u_pool[lane], POOLS * half + 4)
                            part(t[0], t[0][:, :, :], mixc("only64"))
            pool.wait_ge(x_new, 16)
            with pool.Fori(0, 6) as i:
                for par in range(2):
                    if par:
                        pool.wait_ge(hidden_done, LEAD + i * 2 + 2 * PAIRS)
                    else:
                        pool.wait_ge(hidden_done, LEAD + i * 2 + (2 * PAIRS - 1))
                    pool.tensor_copy(CW[:, par, :], VEC[:, ds(i * 32 + (V["conv"] + 16 * par), 16)]).then_inc(taps_ready, 1)

        @block.tensor
        def _(pe):
            def mm(out_ap, lhs, rhs, start):
                return pe.matmul(out_ap, lhs, rhs, start=start, stop=True, skip_group_check=True)

            def three(out_ap, w_hi, w_lo, h_high, h_low, first, swap=False):
                ins = None
                for n, (w, h) in enumerate(((w_hi, h_high), (w_hi, h_low), (w_lo, h_high))):
                    lhs, rhs = (h, w) if swap else (w, h)
                    ins = mm(out_ap, lhs, rhs, first and n == 0)
                return ins

            def columns(slot, c, out_ap, hi, lo):
                for k in range(KT):
                    a = k * 256 + c * P
                    ins = three(out_ap, WHI[:, slot, a:a + P], WLO[:, slot, a:a + P],
                                hi[:, k, :], lo[:, k, :], k == 0)
                return ins

            def turn_x(src):
                for k in range(KT):
                    for t in range(TB):
                        o = (k % 2) * 256 + t * P
                        ins = pe.transpose(PS[:, 4 + k // 2, o:o + P], src[:, t, k * P:(k + 1) * P], ident)
                    if k % 2:
                        ins.then_inc(x_turned, 1)

            def down(slot, buf):
                for f in range(2):
                    for t in range(TB):
                        hi = DHI[:, buf, f, t * P:(t + 1) * P]
                        lo = DLO[:, buf, f, t * P:(t + 1) * P]
                        for n in range(2):
                            a = f * D + n * HALF
                            ins = three(PS[:, 2 * t + n, :], WHI[:, slot, a:a + HALF], WLO[:, slot, a:a + HALF],
                                        hi, lo, False, swap=True)
                ins.then_inc(slabs_used, 1)

            def gate_up(base, p, par):
                for m in range(2):
                    pe.wait_ge(lo_ready, base + 3 * p + m + 1)
                    for f in range(2):
                        ins = columns(slot_of(base + m), f, PS[:, 4 + 2 * par + f, m * 256:m * 256 + 256], HHI, HLO)
                    ins.then_inc(slabs_used, 1)

            def ffn_products(q, turn, b):
                for n in range(4):
                    mm(PS[:, n, :], ZERO[:, 0:P], ZERO[:, :], True)
                pe.wait_ge(h_lo, 2 * turn + 2)
                gate_up(b, 0, 0)
                with pe.Fori(0, PAIRS // 2) as i:
                    for par in range(1, 3):
                        p = i * 2 + par
                        pe.wait_ge(hidden_done, LEAD + i * 2 + (PAIRS * q + par - 1))
                        gate_up(b - 1, p, par % 2)
                        pe.wait_ge(hid_lo, i * 2 + (PAIRS * q + par))
                        pe.wait_ge(lo_ready, i * 6 + (b + 3 * par + 2))
                        down(slot_of(b + 1), 1 - par % 2)
                pe.wait_ge(hid_lo, PAIRS * q + PAIRS)
                pe.wait_ge(lo_ready, b + N_FFN)
                down(slot_of(b + N_FFN - 1), 0)

            pe.wait_ge(zero_ready, 1)
            pe.wait_ge(vec_loaded, 32)
            pe.wait_ge(xs_ready, 2)
            turn_x(XS)
            ffn_products(0, 0, S_FFN1)

            pe.wait_ge(xs_ready, 4)
            turn_x(XS)
            pe.wait_ge(h_lo, 4)

            def win_slab(s):
                pe.wait_ge(lo_ready, S_WIN + s + 1)
                if s >= 2:
                    pe.wait_ge(u_copied, s - 1)
                for c in range(2):
                    ins = columns(slot_of(S_WIN + s), c, PS[:, s % 2, c * 256:c * 256 + 256], HHI, HLO)
                ins.then_inc(slabs_used, 1)

            def sum_heads(j, src, out_ap):
                return mm(out_ap, heads(j), src, j == 0)

            for s in range(3):
                win_slab(s)
            pe.wait_ge(mix_loaded, 32)
            pe.wait_ge(lora_in, 1)
            pe.wait_ge(shifted, 1)
            for j in range(4):
                o = (j % 2) * 256
                mm(PS[:, 4 + j // 2, o:o + 256], LORA[0:64, 0, j * P:(j + 1) * P], LW[0:64, :], True)
            for j in range(4):
                o = (j % 2) * 256
                ins = mm(PS[:, 6 + j // 2, o:o + 256], LORA[64:128, 0, j * P:(j + 1) * P], U[64:128, 0, :], True)
            ins.then_inc(lora_done, 1)
            for s in range(3, 6):
                win_slab(s)
            pe.wait_ge(sigma_ready, 4)
            for j in range(4):
                ins = sum_heads(j, SQ[:, j, :], PS[0:16, 2, 0:256])
            ins.then_inc(head_sum, 1)
            win_slab(6)
            pe.wait_ge(head_rn, 1)
            for j in range(4):
                o = (j % 2) * 256
                ins = mm(PS[:, 4 + j // 2, o:o + 256], spread(j), RN[:, 0, :], True)
            ins.then_inc(head_spread, 1)
            win_slab(7)
            pe.wait_ge(lora_in, 2)
            for j in range(4):
                o = (j % 2) * 256
                ins = mm(PS[:, 6 + j // 2, o:o + 256], LORA[:, 1, j * P:(j + 1) * P], LG[:, :], True)
            ins.then_inc(lora_done, 1)
            win_slab(8)
            pe.wait_ge(feature, 2)
            for j in range(4):
                o = (j % 2) * 256
                ins = mm(PS[:, 4 + j // 2, o:o + 256], mixc("block"), RKR[:, j, :], True)
            ins.then_inc(head_spread, 1)
            win_slab(9)
            win_slab(10)
            for s in (11, 12):
                pe.wait_ge(lo_ready, S_WIN + s + 1)
                slot = slot_of(S_WIN + s)
                for k in range(4):
                    for t in range(TB):
                        a = 4 * (s - 11) + k
                        ins = three(PS[:, 2 + t, :], WHI[:, slot, k * 512:k * 512 + 512],
                                    WLO[:, slot, k * 512:k * 512 + 512], HHI[:, a, t * P:(t + 1) * P],
                                    HLO[:, a, t * P:(t + 1) * P], a == 0, swap=True)
                ins.then_inc(slabs_used, 1)

            def mod_part(m):
                for i in range(3 * m, 3 * m + 3):
                    slot = (B_MOD + i) % RING
                    pe.wait_ge(stage_ready[slot], 16 * ((B_MOD + i) // RING + 1))
                    for c in range(2):
                        for k in range(KT):
                            a = k * 256 + c * P
                            ins = mm(PS[:, 7, (2 * i + c) * 2:(2 * i + c) * 2 + 2], stage[:, slot, a:a + P],
                                     SC[:, k, :], k == 0)
                    ins.then_inc(stage_free[slot], 1)
                if m == 7:
                    mm(PS[0:16, 6, 0:2], heads(0), SC[:, 0, :], True).then_inc(mod_done, 1)

            pe.wait_ge(gate_copied, 1)
            mod_part(0)
            turned = 0
            pe.wait_ge(feature, 4)
            pe.wait_ge(u_copied, 11)
            for src in ("a", "b", "k", "v"):
                for blk in range(TB):
                    if turned >= 2:
                        pe.wait_ge(tok_copied, turned - 1)
                    for j in range(4):
                        f = {"a": AR[:, 2 * j + blk, 0, :], "b": BH[:, j, blk * P:(blk + 1) * P],
                             "k": KH[:, j, blk * P:(blk + 1) * P], "v": U[:, 10 + j, blk * P:(blk + 1) * P]}[src]
                        ins = pe.transpose(PS[:, turned % 2, j * P:(j + 1) * P], f, ident)
                    ins.then_inc(tok_turned, 1)
                    turned += 1

            pe.wait_ge(sbv_ready, 1)
            for m in range(2):
                pe.wait_ge(qk_square, m + 1)
                for j in range(4):
                    ins = sum_heads(j, (SQ2 if m == 0 else OS)[:, j, :], PS[0:16, 2, m * 256:m * 256 + 256])
            ins.then_inc(head_sum, 1)
            mod_part(1)
            pe.wait_ge(head_rn, 2)
            for m in range(2):
                for j in range(4):
                    o = (j % 2) * 256
                    ins = mm(PS[:, 3 + 2 * m + j // 2, o:o + 256], spread(j), RN[:, m, :], True)
                ins.then_inc(head_spread, 1)
            mod_part(2)
            for g in range(2):
                pe.wait_ge(qk_ready, 2)
                pe.wait_ge(tok_copied, 8)
                if g:
                    pe.wait_ge(e_masked, g)
                for hh in range(4):
                    h = 4 * g + hh
                    pb = 64 * (h % 2)
                    q, k = U[pb:pb + 64, 14 + h // 2, :], U[pb:pb + 64, 18 + h // 2, :]
                    mm(PS[:, hh, 0:256], k[:, 0:128], q, True)
                    ins = mm(PS[:, hh, 256:384], k[:, 128:256], q[:, 128:256], False)
                ins.then_inc(z_ready, 1)
                if g == 0:
                    mod_part(3)
                pe.wait_ge(l_ready, g + 1)
                for hh in range(4):
                    mm(PS[:, hh, 0:256], mixc("suffix"), LT[:, hh, 0:256], False)
                    mm(PS[:, hh, 128:256], mixc("minus"), LT[:, hh, 256:384], False)
                    ins = mm(PS[:, hh, 256:384], mixc("suffix"), LT[:, hh, 256:384], False)
                ins.then_inc(e_ready, 1)
                pe.wait_ge(att_ready, g + 1)
                for hh in range(4):
                    h = 4 * g + hh
                    pb = 64 * (h % 2)
                    o = (hh // 2) * 256
                    mm(PS[pb:pb + 64, 4 + g, o:o + 256], SBV[:, 0, h * 64:h * 64 + 64], LT[:, hh, 0:256], True)
                    ins = mm(PS[pb:pb + 64, 4 + g, o + 128:o + 256], SBV[:, 1, h * 64:h * 64 + 64],
                             LT[:, hh, 256:384], False)
                ins.then_inc(o_ready, 1)
            mod_part(4)
            pe.wait_ge(o_copied, 2)
            for j in range(4):
                ins = sum_heads(j, SQ2[:, j, :], PS[0:16, 6, 0:256])
            ins.then_inc(head_sum, 1)
            pe.wait_ge(head_rn, 3)
            for j in range(4):
                o = (j % 2) * 256
                ins = mm(PS[:, 2 + j // 2, o:o + 256], spread(j), RN[:, 0, :], True)
            ins.then_inc(head_spread, 1)
            pe.wait_ge(cat_ready, 1)

            def unit_stage(n, lane, half):
                blk, g = half, lane
                b0, b1, b2 = 3 * lane, 3 * lane + 1, 3 * lane + 2
                t = T[lane]
                hs = unit_heads(g)
                first = 12 * half

                def four(bank, lhs, rhs, width=128):
                    for i in range(4):
                        ins = mm(PS[:, bank, i * width:(i + 1) * width], lhs(i), rhs(i), True)
                    return ins

                def wait(act=0, vec=0, pool=0):
                    if act or half:
                        pe.wait_ge(u_act[lane], act + ACTS * half)
                    if vec or half:
                        pe.wait_ge(u_vec[lane], vec + VECS * half)
                    if pool:
                        pe.wait_ge(u_pool[lane], pool + POOLS * half)

                def feat(ap, h):
                    pb = 64 * (h % 2)
                    return ap[pb:pb + 64, h // 2, blk * P:(blk + 1) * P]

                def a_r(h):
                    pb = 64 * (h % 2)
                    return AR[pb:pb + 64, 2 * (h // 2) + blk, :, :].rearrange("p c n -> p (c n)")

                if n == 1:
                    wait(0, 0)
                    for i in range(4):
                        o = (i % 2) * 256
                        mm(PS[:, b0 + i // 2, o:o + 256], feat(KH, hs[i]), a_r(hs[i]), True)
                    for i in range(4):
                        if i == 2 and lane:
                            pe.wait_ge(u_vec[0], VECS * half + 1)
                        o = (i % 2) * 128
                        to = PS[:, b2, o:o + 128] if i < 2 else PS[:, 6, 256 * lane + o:256 * lane + o + 128]
                        ins = mm(to, a_r(hs[i])[:, 0:128], feat(BH, hs[i]), True)
                elif n == 2:
                    wait(vec=2)
                    for i in range(4):
                        o = (i % 2) * 256
                        ins = mm(PS[:, b0 + i // 2, o:o + 256], feat(BH, hs[i]), a_r(hs[i]), True)
                elif n == 3:
                    wait(vec=3, pool=3)
                    four(b0, lambda i: t[2][:, i, :], lambda i: t[1][:, i, :])
                    four(b1, lambda i: t[1][:, i, :], lambda i: t[2][:, i, :])
                    ins = four(b2, lambda i: NR[:, 8 * half + 4 * lane + i, 0:128],
                               lambda i: VTOK[:, blk, hs[i] * 64:hs[i] * 64 + 64], 64)
                elif n == 4:
                    wait(act=2, vec=4)
                    four(b0, lambda i: t[4][:, i, :], lambda i: t[5][:, i, :])
                    four(b1, lambda i: t[4][:, i, :], lambda i: t[3][:, i, :])
                    ins = four(b2, lambda i: t[3][:, i, :], lambda i: t[4][:, i, :])
                elif n == 5:
                    wait(act=4, vec=5)
                    four(b0, lambda i: t[2][:, i, :], lambda i: t[6][:, i, :])
                    ins = four(b1, lambda i: t[1][:, i, :], lambda i: t[2][:, i, :])
                elif n == 6:
                    wait(act=5, vec=6)
                    ins = four(b2, lambda i: t[3][:, i, :], lambda i: t[5][:, i, :])
                elif n in (7, 9):
                    src, low = (t[6], t[4]) if n == 7 else (t[5], t[0])
                    wait(vec=7 if n == 7 else 9, pool=5)
                    for i in range(4):
                        pe.transpose(PS[:, b0, i * P:(i + 1) * P], src[:, i, :], ident)
                    ins = four(b1, lambda i: low[:, i, :], lambda i: src[:, i, :])
                elif n in (8, 10):
                    wait(act=6 if n == 8 else 7, vec=8 if n == 8 else 10)
                    ins = four(b2, lambda i: t[1][:, i, :], lambda i: t[2][:, i, :])
                elif n == 11:
                    wait(vec=11)
                    ins = four(b0, lambda i: t[6][:, i, :], lambda i: ANV[:, blk, hs[i], :])
                else:
                    wait(act=8)
                    for i in range(4):
                        h = hs[i]
                        pb, o = 64 * (h % 2), (h // 2 - 2 * g) * 128
                        mm(PS[pb:pb + 64, b1, o:o + 128], AU[:, blk, h, 0:64],
                           MB[:, 8 * half + 4 * lane + i, 128:256], True)
                    c = 1 if blk == 0 else 2
                    rs = 64 * (c % 2)
                    for i in range(4):
                        h = hs[i]
                        pb, o = 64 * (h % 2), (h // 2 - 2 * g) * 64
                        ins = mm(PS[pb:pb + 64, b2, o:o + 64], AU[rs:rs + 64, blk, h, 0:64],
                                 BTOK[rs:rs + 64, blk, h * 64:h * 64 + 64], True)
                ins.then_inc(u_pe[lane], 1)

            for half in range(2):
                for n in range(1, 13):
                    for lane in range(2):
                        unit_stage(n, lane, half)
                    if half == 0 and n in (4, 8, 12):
                        mod_part(5 + n // 4 - 1)

            for lane in range(2):
                pe.wait_ge(u_act[lane], 2 * ACTS)
                pe.wait_ge(u_vec[lane], 2 * VECS)
            for c in range(3):
                blk, rs = c // 2, 64 * (c % 2)
                if c:
                    pe.wait_ge(s_ready, c)
                for h in range(8):
                    pb, j = 64 * (h % 2), h // 2
                    o = PS[pb:pb + 64, 3, j * 64:j * 64 + 64]
                    ch = slice(h * 64, h * 64 + 64)
                    mm(o, BTOK[rs:rs + 64, blk, ch], AU[rs:rs + 64, blk, h, 64:128], True)
                    ins = mm(o, KTOK[rs:rs + 64, blk, ch], VTOK[rs:rs + 64, blk, ch], False)
                    if c:
                        ins = mm(PS[pb:pb + 64, 0, j * 64:j * 64 + 64], ET[pb:pb + 64, c - 1, j, :],
                                 ST[pb:pb + 64, c - 1, j, :], True)
                ins.then_inc(s_products, 1)
            pe.wait_ge(s_ready, 3)
            for h in range(8):
                pb, j = 64 * (h % 2), h // 2
                g, i = h // 4, unit_heads(h // 4).index(h)
                for blk in range(TB):
                    o = (j % 2) * 256 + blk * P
                    at = 8 * blk + 4 * g + i
                    mm(PS[pb:pb + 64, 4 + j // 2, o:o + P], VTOK[:, blk, h * 64:h * 64 + 64], NR[:, at, 128:256], True)
                    ins = mm(PS[pb:pb + 64, 4 + j // 2, o:o + P], AU[:, blk, h, 64:128], MB[:, at, 128:256], False)
                    for c in (1,) if blk == 0 else (2, 3):
                        q = (c % 2) * 64
                        ins = mm(PS[pb:pb + 64, 4 + j // 2, o + q:o + q + 64], ST[pb:pb + 64, c - 1, j, :],
                                 RT[pb:pb + 64, j, blk * P + q:blk * P + q + 64], False)
            ins.then_inc(y_products, 1)
            pe.wait_ge(y_step, 1)
            for j in range(4):
                ins = mm(PS[:, j // 2, (j % 2) * 256:(j % 2) * 256 + 256], mixc("mean"), YS[:, j, :], True)
            ins.then_inc(y_products, 1)
            pe.wait_ge(y_step, 3)
            for j in range(4):
                ins = sum_heads(j, YQ[:, j, :], PS[0:16, 2, 0:256])
            ins.then_inc(head_sum, 1)
            pe.wait_ge(head_rn, 4)
            for j in range(4):
                ins = mm(PS[:, 4 + j // 2, (j % 2) * 256:(j % 2) * 256 + 256], spread(j), RN[:, 0, :], True)
            ins.then_inc(head_spread, 1)

            def out_products(s0, hi, lo):
                for i in range(4):
                    pe.wait_ge(lo_ready, s0 + i + 1)
                    slot = slot_of(s0 + i)
                    for kk in range(2):
                        k = 2 * i + kk
                        for t in range(TB):
                            for n in range(2):
                                a = kk * D + n * HALF
                                ins = three(PS[:, 2 * t + n, :], WHI[:, slot, a:a + HALF], WLO[:, slot, a:a + HALF],
                                            hi[:, k, t * P:(t + 1) * P], lo[:, k, t * P:(t + 1) * P], k == 0, swap=True)
                    ins.then_inc(slabs_used, 1)

            pe.wait_ge(cat_lo, 1)
            out_products(S_OUT1, HHI, HLO)

            for r in range(4):
                pe.wait_ge(gate_diag, r + 1)
                if r >= 2:
                    pe.wait_ge(gate_row_copied, r - 1)
                mm(PS[:, 6 + r % 2, :], ones, DG[:, r % 2, :, :].rearrange("p a n -> p (a n)"), True)\
                    .then_inc(gate_rows, 1)
            pe.wait_ge(ctx_lo, 1)
            pe.wait_ge(lo_ready, S_CTX + 1)
            for c in range(2):
                ins = columns(slot_of(S_CTX), c, PS[:, 4, c * 256:c * 256 + 256], CHI, CLO)
            ins.then_inc(slabs_used, 1)

            def values(s, bank, hi, lo):
                pe.wait_ge(lo_ready, s + 1)
                slot = slot_of(s)
                for t in range(TB):
                    for k in range(KT):
                        ins = three(PS[:, bank, t * 256:t * 256 + 256], WHI[:, slot, k * 256:k * 256 + 256],
                                    WLO[:, slot, k * 256:k * 256 + 256], hi[:, k, t * P:(t + 1) * P],
                                    lo[:, k, t * P:(t + 1) * P], k == 0, swap=True)
                ins.then_inc(slabs_used, 1)

            values(S_CTX + 1, 5, CHI, CLO)

            pe.wait_ge(xs_ready, 6)
            pe.wait_ge(ctx_copied, 3)
            pe.wait_ge(gate_row_copied, 4)
            turn_x(XS)
            ffn_products(1, 2, S_FFN2)

            pe.wait_ge(x_new, 12)
            turn_x(X)
            pe.wait_ge(h_lo, 8)
            pe.wait_ge(att_loaded, 48)

            def win2_slab(s, turn):
                pe.wait_ge(lo_ready, S_WIN2 + s + 1)
                if turn >= 2:
                    pe.wait_ge(p_copied, turn - 1)
                for c in range(2):
                    ins = columns(slot_of(S_WIN2 + s), c, PS[:, turn % 2, c * 256:c * 256 + 256], HHI, HLO)
                ins.then_inc(slabs_used, 1)

            def rotate(bank, tiles):
                for n, tile in enumerate(tiles):
                    o = (n % 2) * 256
                    ins = mm(PS[:, bank + n // 2, o:o + 256], CT[:, 512:640], tile, True)
                ins.then_inc(rotated, 1)

            win2_slab(0, 0)
            values(S_WIN2 + 1, 2, HHI, HLO)
            win2_slab(2, 1)
            pe.wait_ge(k_square, 1)
            mm(PS[0:16, 3, :], heads(0), TR[:, 0:2, :].rearrange("p a n -> p (a n)"), True).then_inc(head_sum, 1)
            win2_slab(3, 2)
            pe.wait_ge(head_rn, 5)
            mm(PS[:, 4, :], spread(0), RA[:, 0:512], True).then_inc(head_spread, 1)
            pe.wait_ge(p_copied, 3)
            rotate(5, [QR[:, 2 + j, :] for j in range(4)])
            win2_slab(4, 3)
            pe.wait_ge(rope_in, 1)
            rotate(3, [QR[:, 0, :], KALL[:, 1, 0:256]])
            win2_slab(5, 4)
            pe.wait_ge(k_square, 2)
            pe.wait_ge(roped, 3)
            for j in range(4):
                ins = mm(PS[0:16, 3, 0:256], heads(j), TR[:, j, :], j == 0)
            ins.then_inc(head_sum, 1)
            win2_slab(6, 5)
            pe.wait_ge(head_rn, 6)
            pe.wait_ge(roped, 1)
            for j in range(4):
                o = (j % 2) * 256
                ins = mm(PS[:, 5 + j // 2, o:o + 256], spread(j), RA[:, 0:256], True)
            ins.then_inc(head_spread, 1)
            win2_slab(7, 6)
            pe.wait_ge(rope_in, 2)
            rotate(3, [QR[:, 6 + j, :] for j in range(4)])
            for s in range(8, 14):
                win2_slab(s, s - 1)

            pe.wait_ge(roped, 4)
            pe.wait_ge(v_copied, 1)
            pe.wait_ge(p_copied, 13)

            def score(i):
                br, t, j = i // 8, (i // 4) % 2, i % 4
                if i >= 2:
                    pe.wait_ge(p_ready, 2 * (i - 1))
                for par in range(2):
                    pb = 64 * par
                    ins = mm(PS[:, 2 * (i % 2) + par, :], QN[pb:pb + 64, 4 * br + j, t * P:(t + 1) * P],
                             KALL[pb:pb + 64, br, :], True)
                ins.then_inc(scored, 1)

            def turn_p(i):
                pe.wait_ge(p_ready, 2 * i + 2)
                if i:
                    pe.wait_ge(pt_act, i)
                    pe.wait_ge(pt_vec, i)
                for par in range(2):
                    for k in range(4):
                        ins = pe.transpose(PS[:, 4 + par, k * P:(k + 1) * P], PM[:, i % 2, par, k * P:(k + 1) * P], ident)
                ins.then_inc(p_turned, 1)

            def weigh(i):
                br, t, j = i // 8, (i // 4) % 2, i % 4
                pe.wait_ge(pt_act, i + 1)
                pe.wait_ge(pt_vec, i + 1)
                if j == 0 and i >= 8:
                    pe.wait_ge(o_scaled, i // 4 - 1)
                for par in range(2):
                    o = j * 128 + par * 64
                    for k in range(4):
                        ins = mm(PS[:, 6 + t, o:o + 64], PT[:, i % 2, par, k * P:(k + 1) * P],
                                 VALL[:, k, br * 128 + par * 64:br * 128 + par * 64 + 64], k == 0)
                ins.then_inc(pv_done, 1)

            for i in range(18):
                if i < 16:
                    score(i)
                if 1 <= i < 17:
                    turn_p(i - 1)
                if i >= 2:
                    weigh(i - 2)
            pe.wait_ge(o_scaled, 4)
            turn_x(OT)
            for half in range(2):
                for br in range(2):
                    s = S_BRANCH + 2 * half + br
                    pe.wait_ge(h_lo, 10)
                    pe.wait_ge(lo_ready, s + 1)
                    slot = slot_of(s)
                    for c in range(4):
                        o = (c % 2) * 256
                        for k in range(4):
                            a = k * 512 + c * P
                            ins = three(PS[:, 4 * half + 2 * br + c // 2, o:o + 256], WHI[:, slot, a:a + P],
                                        WLO[:, slot, a:a + P], HHI[:, 4 * br + k, :], HLO[:, 4 * br + k, :], k == 0)
                    ins.then_inc(slabs_used, 1)
            pe.wait_ge(m_lo, 2)
            out_products(S_OUT2, MHI, MLO)

            pe.wait_ge(x_new, 16)
            turn_x(X)
            ffn_products(2, 5, S_FFN3)

        @block.scalar
        def _(act):
            n_step = [0]

            def step(ins):
                n_step[0] += 1
                ins.then_inc(act_step, 1)

            def own():
                act.wait_ge(act_step, n_step[0])

            def high(base, p=0):
                slot = slot_of(base)
                act.wait_ge(stage_ready[slot], p * 16 + 16 * ((base + shift(base)) // RING + 1))
                if not (isinstance(p, int) and base + 3 * p < RING):
                    act.wait_ge(slabs_used, p * 3 + (base - RING + 1))
                act.activation(WHI[:, slot, :], stage[:, slot, :], ACT.Copy).then_inc(hi_ready, 1)

            def norm_sums(n, ready):
                for t in range(TB):
                    ready(t)
                    step(act.activation(XS[:, t, :], X[:, t, :], ACT.Square, accum_out=SM[:, t:t + 1]))
                own()
                act.activation(SM[:, 2:4], SM[:, 0:2], ACT.Sqrt, scale=1.0 / D, bias=EPS[:, 0:1]).then_inc(root, 1)

            def h_high(turn):
                for half in range(2):
                    act.wait_ge(h_full, 4 * turn + 2 * half + 2)
                    act.activation(HHI[:, 4 * half:4 * half + 4, :], HF[:, 4 * half:4 * half + 4, :], ACT.Copy)\
                       .then_inc(h_hi, 1)

            def ffn_act(q, b, tail):
                def pair(p, par, i, first=False, ahead=2):
                    k = i * 2 if i is not None else 0
                    six = 2 * i if i is not None else 0
                    if not first:
                        high(b + 3 * par + 2, six)
                    act.wait_ge(slabs_used, six * 3 + (b + 3 * par + (2 if first else 1)))
                    act.wait_ge(hidden_done, LEAD + k + max(PAIRS * q + par - 1, 0))
                    bank = 4 + 2 * (par % 2)
                    if q < 2:
                        act.activation(SG[:, par % 2, :, :], PS[:, bank:bank + 2, 0:256], ACT.Silu)\
                           .then_inc(silu_done, 1)
                    else:
                        act.wait_ge(taps_ready, k + (par + 1))
                        for a in range(4):
                            src = PS[:, bank + a % 2, (a // 2) * 256:(a // 2) * 256 + 256]
                            ins = act.activation(CG[:, par % 2, a, :], src, ACT.Identity,
                                                 scale=CW[:, par % 2, 4 * a + 1:4 * a + 2],
                                                 bias=CW[:, par % 2, 4 * a + 3:4 * a + 4])
                        ins.then_inc(center, 1)
                    if ahead:
                        high(b + 3 * par + 3, six)
                    if q == 2:
                        act.wait_ge(conv_done, k + (par + 1))
                        act.activation(SG[:, par % 2, :, :], CG[:, par % 2, 0:2, :], ACT.Silu).then_inc(silu_done, 1)
                    act.wait_ge(hidden_done, LEAD + k + (PAIRS * q + par + 1))
                    if not first:
                        act.wait_ge(slabs_used, six * 3 + (b + 3 * par - 1))
                    act.activation(DHI[:, par % 2, :, :], HID[:, par % 2, :, :], ACT.Copy).then_inc(hid_hi, 1)
                    if ahead:
                        high(b + 3 * par + 4, six)

                pair(0, 0, None, first=True)
                loops = PAIRS // 2 - (0 if tail else 1)
                with act.Fori(0, loops) as i:
                    for par in range(1, 3):
                        pair(None, par, i)
                if not tail:
                    pair(None, PAIRS - 2, None)
                    pair(None, PAIRS - 1, None, ahead=0)

            act.wait_ge(vec_loaded, 32)
            act.activation(SC[:, :, :].rearrange("p k n -> p (k n)"), VEC[:, V["c"]:V["c"] + 16], ACT.Silu)\
               .then_inc(hid_hi, LEAD)
            act.wait_ge(x_loaded, 16)
            act.wait_ge(eps_ready, 1)
            norm_sums(0, lambda t: None)
            for s in range(3):
                high(s)
            h_high(0)
            ffn_act(0, S_FFN1, True)

            norm_sums(1, lambda t: act.wait_ge(x_new, 2 * t + 2))
            h_high(1)
            high(S_WIN + 2)

            def copy_u(s):
                act.wait_ge(slabs_used, S_WIN + s + 1)
                act.activation(U[:, 2 * s:2 * s + 2, :].rearrange("p a n -> p (a n)"), PS[:, s % 2, :], ACT.Copy)\
                   .then_inc(u_copied, 1)

            for s in range(11):
                copy_u(s)
                if s + 3 < 13:
                    high(S_WIN + s + 3)
                if s == 1:
                    act.wait_ge(shifted, 1)
                    act.activation(LW[0:64, :], U[0:64, 0, :], ACT.Tanh).then_inc(lora_in, 1)
                    act.activation(LG[:, :], U[:, 1, :], ACT.Sigmoid).then_inc(lora_in, 1)
                if s == 3:
                    act.wait_ge(lora_done, 1)
                    for n, (to, name) in enumerate(((EA, "w0"), (AA, "a0"))):
                        for j in range(4):
                            o = (j % 2) * 256
                            ins = act.activation(to[:, j, :], PS[:, 4 + 2 * n + j // 2, o:o + 256], ACT.Sigmoid,
                                                 bias=vcol(name, j))
                        ins.then_inc(sigma_ready, 1)
                    act.wait_ge(shifted, 3)
                    for j in range(4):
                        ins = act.activation(KK[:, j, :], U[:, 2 + j, :], ACT.Copy, scale=vcol("kk", j))
                    ins.then_inc(sigma_ready, 1)
                    act.wait_ge(sigma_ready, 3)
                    act.activation(SQ[:, :, :], KK[:, :, :], ACT.Square).then_inc(sigma_ready, 1)
                if s == 6:
                    act.wait_ge(head_sum, 1)
                    act.activation(RN[:, 0, :], PS[0:16, 2, 0:256], ACT.Sqrt).then_inc(head_root, 1)
                    act.wait_ge(decay_ready, 1)
                    act.activation(EI[:, :, :], ER[:, :, :], ACT.Exp, scale=DECAY_SCALE).then_inc(exp_ready, 1)
                    act.activation(EA[:, :, :], EA[:, :, :], ACT.Exp, scale=-DECAY_SCALE).then_inc(exp_ready, 1)
                    act.activation(ER[:, :, :], ER[:, :, :], ACT.Exp, scale=-DECAY_SCALE).then_inc(exp_ready, 1)
                if s == 9:
                    act.wait_ge(feature, 2)
                    act.wait_ge(lora_done, 2)
                    act.activation(U[:, 6:10, :].rearrange("p a n -> p (a n)"),
                                   PS[:, 6:8, :].rearrange("p a n -> p (a n)"), ACT.Copy).then_inc(gate_copied, 1)
            act.wait_ge(feature, 4)
            act.wait_ge(u_copied, 11)
            act.activation(SQ2[:, :, :], U[:, 14:18, :], ACT.Square).then_inc(qk_square, 1)
            act.activation(OS[:, :, :], U[:, 18:22, :], ACT.Square).then_inc(qk_square, 1)
            act.wait_ge(slabs_used, S_WIN + N_WIN)
            act.activation(SBV[:, :, :], PS[:, 2:4, :], ACT.Copy).then_inc(sbv_ready, 1)
            for n in range(8):
                blk = n % 2
                act.wait_ge(tok_turned, n + 1)
                to = [ANV[:, blk, :, 0:64], BTOK[:, blk, :], KTOK[:, blk, :], VTOK[:, blk, :]][n // 2]
                src = PS[:, n % 2, :]
                if n < 2:
                    src = src.rearrange("p (h c) -> p h c", h=8)
                act.activation(to, src, ACT.Copy).then_inc(tok_copied, 1)
            act.wait_ge(head_sum, 2)
            step(act.activation(RN[:, 0, :], PS[0:16, 2, 0:256], ACT.Sqrt, bias=EPS[0:16, 3:4]))
            act.activation(RN[:, 1, :], PS[0:16, 2, 256:512], ACT.Sqrt, scale=1.0 / HEAD, bias=EPS[0:16, 0:1])\
               .then_inc(head_root, 1)
            for g in range(2):
                act.wait_ge(z_ready, g + 1)
                if g:
                    act.wait_ge(att_ready, g)
                step(act.activation(ZT[:, :, :], PS[:, 0:4, 0:384], ACT.Abs))
                own()
                step(act.activation(ZT[:, :, :], ZT[:, :, :], ACT.Exp, scale=-1.0))
                own()
                act.activation(ZT[:, :, :], ZT[:, :, :], ACT.Ln, bias=ones[:, 0:1]).then_inc(ln_ready, 1)
                act.wait_ge(e_masked, g + 1)
                act.activation(LT[:, :, :], ZT[:, :, :], ACT.Exp).then_inc(att_ready, 1)
                act.wait_ge(o_ready, g + 1)
                if g == 0:
                    act.wait_ge(head_rn, 2)
                step(act.activation(OS[:, 2 * g:2 * g + 2, :].rearrange("p a n -> p (a n)"), PS[:, 4 + g, :], ACT.Copy))
                own()
                act.activation(SQ2[:, 2 * g:2 * g + 2, :], OS[:, 2 * g:2 * g + 2, :], ACT.Square).then_inc(o_copied, 1)
            act.wait_ge(head_sum, 3)
            act.activation(RN[:, 0, :], PS[0:16, 6, 0:256], ACT.Sqrt, scale=1.0 / HEAD, bias=EPS[0:16, 0:1])\
               .then_inc(head_root, 1)

            def copies(n, lane, half):
                b0, b1, b2 = 3 * lane, 3 * lane + 1, 3 * lane + 2
                t, blk, g = T[lane], half, lane
                todo = {3: [(t[3], b0), ("nv", b2)], 4: [(t[1], b1), (t[2], b2)], 5: [(t[3], b1)],
                        7: [(t[1], b0)], 9: [(t[1], b0)], 11: [("au", b0)], 12: [("et", b2)]}.get(n, [])
                if todo:
                    act.wait_ge(u_pe[lane], 12 * half + n)
                for to, bank in todo:
                    if to == "nv":
                        for par in range(2):
                            src = PS[:, bank, par * 128:par * 128 + 128].rearrange("p (a n) -> p a n", a=2)
                            ins = act.activation(ANV[:, blk, 4 * g + par:4 * g + par + 3:2, 64:128], src, ACT.Copy)
                        ins.then_inc(u_act[lane], 1)
                    elif to == "au":
                        for par in range(2):
                            src = PS[:, bank, par * 256:par * 256 + 256].rearrange("p (a n) -> p a n", a=2)
                            ins = act.activation(AU[:, blk, 4 * g + par:4 * g + par + 3:2, :], src, ACT.Copy)
                        ins.then_inc(u_act[lane], 1)
                    elif to == "et":
                        act.activation(ET[:, blk, 2 * g:2 * g + 2, :],
                                       PS[:, bank, 0:128].rearrange("p (a n) -> p a n", a=2), ACT.Copy)\
                           .then_inc(u_act[lane], 1)
                    else:
                        act.activation(to[:, :, :], PS[:, bank, :].rearrange("p (a n) -> p a n", a=4), ACT.Copy)\
                           .then_inc(u_act[lane], 1)

            for half in range(2):
                for n in range(1, 13):
                    for lane in range(2):
                        copies(n, lane, half)

            act.wait_ge(y_products, 1)
            act.activation(YS[:, :, :].rearrange("p a n -> p (a n)"), PS[:, 4:6, :].rearrange("p a n -> p (a n)"),
                           ACT.Copy).then_inc(y_step, 1)
            act.wait_ge(y_step, 2)
            act.activation(YQ[:, :, :], YC[:, :, :], ACT.Square).then_inc(y_step, 1)
            act.wait_ge(head_sum, 4)
            act.activation(RN[:, 0, :], PS[0:16, 2, 0:256], ACT.Sqrt, scale=1.0 / HEAD, bias=EPS[0:16, 2:3])\
               .then_inc(head_root, 1)
            for s in range(3):
                high(S_OUT1 + s)
            act.wait_ge(cat_ready, 2)
            act.activation(HHI[:, :, :], HF[:, :, :], ACT.Copy).then_inc(cat_hi, 1)
            high(S_OUT1 + 3)

            act.dma_start(CX[:, :, :], ctx_t).then_inc(att_loaded, 16)
            act.dma_start(CT[:, :], c_att).then_inc(att_loaded, 16)
            act.dma_start(ROWS[:, :], rows[0:1, 4 * D:N_ROW].broadcast_to([P, 264])).then_inc(att_loaded, 16)
            act.dma_start(ROW[:, :], rows[0:1, 0:2 * D].broadcast_to([P, 2 * D])).then_inc(row_loaded, 16)
            for half in range(2):
                part = slice(4 * half, 4 * half + 4)
                act.wait_ge(ctx_full, half + 1)
                act.activation(CHI[:, part, :], CX[:, part, :], ACT.Copy).then_inc(ctx_hi, 1)
            high(S_CTX)
            for r in range(4):
                act.wait_ge(gate_rows, r + 1)
                act.activation(GB[:, r // 2, (r % 2) * HALF:(r % 2) * HALF + HALF], PS[:, 6 + r % 2, :], ACT.Copy)\
                   .then_inc(gate_row_copied, 1)
            high(S_CTX + 1)
            norm_sums(2, lambda t: act.wait_ge(x_new, 4 + 2 * t + 2))
            high(S_FFN2)
            high(S_FFN2 + 1)
            h_high(2)
            high(S_FFN2 + 2)
            ffn_act(1, S_FFN2, True)

            high(S_WIN2 + 2)
            h_high(3)

            def out_of(turn, s, to, tile, func=ACT.Identity):
                act.wait_ge(slabs_used, S_WIN2 + s + 1)
                for a in range(2):
                    ins = act.activation(to[a], PS[:, turn % 2, a * 256:a * 256 + 256], func, bias=vcol("b2", tile + a))
                ins.then_inc(p_copied, 1)

            def win2_out(s):
                turn = s if s == 0 else s - 1
                if s == 0:
                    out_of(0, 0, (QR[:, 0, :], KALL[:, 1, 0:256]), 0)
                elif s < 6:
                    out_of(turn, s, (QR[:, 2 * s - 2, :], QR[:, 2 * s - 1, :]), 2 * s - 2)
                elif s < 14:
                    out_of(turn, s, (GT[:, 2 * s - 12, :], GT[:, 2 * s - 11, :]), 2 * s - 2, ACT.Sigmoid)

            win2_out(0)
            high(S_WIN2 + 3)
            act.wait_ge(p_copied, 1)
            act.activation(TR[:, 0:2, :].rearrange("p a n -> p (a n)"), KALL[:, 1, :], ACT.Square).then_inc(k_square, 1)
            high(S_WIN2 + 4)
            win2_out(2)
            high(S_WIN2 + 5)
            act.wait_ge(head_sum, 5)
            act.activation(RA[:, 0:512], PS[0:16, 3, :], ACT.Sqrt, scale=1.0 / HEAD, bias=EPS[0:16, 0:1])\
               .then_inc(head_root, 1)
            win2_out(3)
            high(S_WIN2 + 6)
            win2_out(4)
            high(S_WIN2 + 7)
            win2_out(5)
            high(S_WIN2 + 8)
            act.wait_ge(roped, 1)
            act.wait_ge(p_copied, 5)
            act.activation(TR[:, :, :], QR[:, 6:10, :], ACT.Square).then_inc(k_square, 1)
            act.wait_ge(head_sum, 6)
            act.activation(RA[:, 0:256], PS[0:16, 3, 0:256], ACT.Sqrt, scale=1.0 / HEAD, bias=EPS[0:16, 0:1])\
               .then_inc(head_root, 1)
            for s in range(6, 14):
                win2_out(s)
                high(S_WIN2 + s + 3)

            def exps(i):
                act.wait_ge(max_done, i + 1)
                if i >= 2:
                    act.wait_ge(p_turned, i - 1)
                for par in range(2):
                    at = 2 * i + par
                    act.activation(PM[:, i % 2, par, :], PS[:, 2 * (i % 2) + par, :], ACT.Exp, scale=SCALE,
                                   bias=SM[:, 32 + at:33 + at], accum_out=SM[:, 64 + at:65 + at]).then_inc(p_ready, 1)

            def copy_pt(i):
                act.wait_ge(p_turned, i + 1)
                if i >= 2:
                    act.wait_ge(pv_done, i - 1)
                act.activation(PT[:, i % 2, 0, :], PS[:, 4, :], ACT.Copy).then_inc(pt_act, 1)

            for i in range(17):
                if i < 16:
                    exps(i)
                if i >= 1:
                    copy_pt(i - 1)
                if i == 8:
                    act.wait_ge(sink_in, 1)
                    act.activation(SM[:, 96:112], SM[:, 96:112], ACT.Exp).then_inc(sink_exp, 1)
            h_high(4)
            for half in range(2):
                act.wait_ge(merged, half + 1)
                part = slice(4 * half, 4 * half + 4)
                act.activation(MHI[:, part, :], MF[:, part, :], ACT.Copy).then_inc(m_hi, 1)
                high(S_BRANCH + 3 + 2 * half)
                high(S_BRANCH + 4 + 2 * half)
            high(S_OUT2 + 3)
            high(S_FFN3)

            def ln_act(n):
                for t in range(TB):
                    act.wait_ge(ln_var, 2 * n + t + 1)
                    act.activation(SM[:, 16 + 4 * t + 2:16 + 4 * t + 3], SM[:, 16 + 4 * t + 1:16 + 4 * t + 2], ACT.Sqrt,
                                   bias=EPS[:, 1:2]).then_inc(ln_root, 1)

            high(S_FFN3 + 1)
            ln_act(0)
            act.wait_ge(x_new, 16)
            act.dma_start(ROW[:, :], rows[0:1, 2 * D:4 * D].broadcast_to([P, 2 * D])).then_inc(row_loaded, 16)
            h_high(5)
            high(S_FFN3 + 2)
            ffn_act(2, S_FFN3, False)
            ln_act(1)

        @block.vector
        def _(vec):
            n_step = [0]

            def step(ins):
                n_step[0] += 1
                ins.then_inc(vec_step, 1)

            def own():
                vec.wait_ge(vec_step, n_step[0])

            def low(base, p=0):
                slot = slot_of(base)
                vec.wait_ge(hi_ready, p * 3 + (base + 1))
                vec.tensor_tensor(WLO[:, slot, :], stage[:, slot, :], WHI[:, slot, :].bitcast(F32), ALU.subtract)\
                   .then_inc(lo_ready, 1)
                vec.wait_ge(lo_ready, p * 3 + (base + 1))
                vec.sem_inc(stage_free[slot], 1)

            def norm_scale(n):
                vec.wait_ge(root, n + 1)
                step(vec.reciprocal(SM[:, 4:6], SM[:, 2:4]))
                own()
                for t in range(TB):
                    vec.tensor_scalar(XS[:, t, :], X[:, t, :], SM[:, 4 + t:5 + t], None, ALU.mult)\
                       .then_inc(xs_ready, 1)

            def h_scale(turn, mul, add=None):
                for n in range(4):
                    vec.wait_ge(x_turned, 4 * turn + n + 1)
                    for k in (2 * n, 2 * n + 1):
                        ins = vec.tensor_scalar(HF[:, k, :], PS[:, 4 + n, (k % 2) * 256:(k % 2) * 256 + 256], mul(k),
                                                add(k) if add else None, ALU.mult, ALU.add if add else ALU.bypass)
                    ins.then_inc(h_full, 1)
                for half in range(2):
                    vec.wait_ge(h_hi, 2 * turn + half + 1)
                    part = slice(4 * half, 4 * half + 4)
                    vec.tensor_tensor(HLO[:, part, :], HF[:, part, :], HHI[:, part, :].bitcast(F32), ALU.subtract)\
                       .then_inc(h_lo, 1)

            def add_half(s, half=0.5):
                vec.wait_ge(slabs_used, s)
                for t in range(TB):
                    for n in range(2):
                        part = X[:, t, n * HALF:(n + 1) * HALF]
                        vec.scalar_tensor_tensor(part, PS[:, 2 * t + n, :], half, part, ALU.mult, ALU.add)\
                           .then_inc(x_new, 1)

            def ffn_vec(q, b, tail):
                def pair(par, i, first=False, ahead=2):
                    k = i * 2 if i is not None else 0
                    if not first:
                        low(b + 3 * par + 2, k)
                    if q == 2:
                        vec.wait_ge(center, k + (par + 1))
                        bank = 4 + 2 * (par % 2)
                        for m in range(2):
                            if m:
                                vec.wait_ge(tap_before, k + (par + 1))
                            for a in range(4):
                                src = PS[:, bank + a % 2, (a // 2) * 256:(a // 2) * 256 + 256]
                                c = CG[:, par % 2, a, :]
                                src, c = (src[:, 1:256], c[:, 0:255]) if m else (src[:, 0:255], c[:, 1:256])
                                ins = vec.scalar_tensor_tensor(c, src, CW[:, par % 2, 4 * a + 2 * m:4 * a + 2 * m + 1],
                                                               c, ALU.mult, ALU.add)
                            ins.then_inc(conv_done if m else tap_before, 1)
                        if ahead:
                            low(b + 3 * par + 3, k)
                    vec.wait_ge(silu_done, k + (PAIRS * q + par + 1))
                    vec.wait_ge(hid_hi, LEAD + k + max(PAIRS * q + par - 1, 0))
                    bank = 4 + 2 * (par % 2)
                    up = PS[:, bank:bank + 2, 256:512] if q < 2 else CG[:, par % 2, 2:4, :]
                    vec.tensor_tensor(HID[:, par % 2, :, :], SG[:, par % 2, :, :], up, ALU.mult).then_inc(hidden_done, 1)
                    if ahead and q < 2:
                        low(b + 3 * par + 3, k)
                    vec.wait_ge(hid_hi, LEAD + k + (PAIRS * q + par + 1))
                    vec.tensor_tensor(DLO[:, par % 2, :, :], HID[:, par % 2, :, :],
                                      DHI[:, par % 2, :, :].bitcast(F32), ALU.subtract).then_inc(hid_lo, 1)
                    if ahead:
                        low(b + 3 * par + 4, k)

                pair(0, None, first=True)
                with vec.Fori(0, PAIRS // 2 - (0 if tail else 1)) as i:
                    for par in range(1, 3):
                        pair(par, i)
                if not tail:
                    pair(PAIRS - 2, None)
                    pair(PAIRS - 1, None, ahead=0)

            vec.memset(EPS[:, 0:1], RMS_EPS).then_inc(hidden_done, LEAD)
            step(vec.memset(EPS[:, 1:2], LN_EPS))
            step(vec.memset(EPS[:, 2:3], LNX_EPS))
            vec.memset(EPS[:, 3:4], HEAD * RMS_EPS).then_inc(eps_ready, 1)
            vec.wait_ge(x_loaded, 16)
            vec.wait_ge(vec_loaded, 32)
            norm_scale(0)
            low(0)
            low(1)
            h_scale(0, lambda k: VEC[:, V["g1"] + k:V["g1"] + k + 1])
            low(2)
            ffn_vec(0, S_FFN1, True)
            add_half(S_FFN1 + N_FFN)

            norm_scale(1)
            h_scale(1, lambda k: vcol("g2", k))
            low(S_WIN + 2)
            step(vec.tensor_scalar(KA1[:, :], VEC[:, V["ka"]:V["ka"] + 4], -1.0, 1.0, ALU.mult, ALU.add))

            def shift_tokens(s):
                vec.wait_ge(u_copied, s + 1)
                own()
                u = U[:, 2 * s:2 * s + 2, :]
                step(vec.tensor_tensor(DT[:, :, 1:256], u[:, :, 0:255], u[:, :, 1:256], ALU.subtract))
                step(vec.tensor_scalar(DT[:, :, 0:1], u[:, :, 0:1], -1.0, None, ALU.mult))
                own()
                for a in range(2):
                    ins = vec.scalar_tensor_tensor(U[:, 2 * s + a, :], DT[:, a, :], vcol("mu", 2 * s + a),
                                                   U[:, 2 * s + a, :], ALU.mult, ALU.add)
                ins.then_inc(shifted, 1)

            def flat(ap):
                return ap.rearrange("p a n -> p (a n)")

            for s in range(7):
                shift_tokens(s)
                low(S_WIN + s + 3)
                if s == 3:
                    vec.wait_ge(sigma_ready, 2)
                    for j in range(4):
                        step(vec.tensor_tensor_scan(ER[:, j, :], mixc("chunk"), EA[:, j, :], 0.0, ALU.mult, ALU.add))
                    own()
                    vec.tensor_tensor(flat(EA), flat(ER), flat(EA), ALU.subtract).then_inc(decay_ready, 1)
                if s == 4:
                    vec.wait_ge(sigma_ready, 3)
                    vec.wait_ge(shifted, 5)
                    for m in range(2):
                        for a in range(2):
                            j = 2 * m + a
                            step(vec.tensor_scalar(DT[:, a, :], AA[:, j, :], vcol("ka", j), KA1[:, j:j + 1],
                                                   ALU.mult, ALU.add))
                        own()
                        step(vec.tensor_tensor(U[:, 2 + 2 * m:4 + 2 * m, :], U[:, 2 + 2 * m:4 + 2 * m, :], DT[:, :, :],
                                               ALU.mult))
                        own()
            vec.wait_ge(head_root, 1)
            step(vec.tensor_scalar(RN[:, 0, :], RN[:, 0, :], 1e-12, None, ALU.max))
            own()
            vec.reciprocal(RN[:, 0, :], RN[:, 0, :]).then_inc(head_rn, 1)
            low(S_WIN + 10)
            vec.wait_ge(shifted, 7)
            for j in range(4):
                step(vec.scalar_tensor_tensor(RKR[:, j, :], U[:, 6 + j, :], vcol("rk", j), U[:, 2 + j, :],
                                              ALU.mult, ALU.mult))
            vec.wait_ge(exp_ready, 3)
            step(vec.tensor_copy(DL[:, :, :], ER[:, :, 63:256:64]))

            def by_block(ap):
                return ap.rearrange("p a (b n) -> p (a b) n", b=2)

            vec.tensor_tensor(AR[:, :, 1, :], by_block(U[:, 6:10, :]), by_block(ER), ALU.mult).then_inc(feature, 1)
            vec.wait_ge(head_spread, 1)
            vec.tensor_tensor(flat(KK), flat(KK), PS[:, 4:6, :].rearrange("p a n -> p (a n)"), ALU.mult)\
               .then_inc(feature, 1)
            low(S_WIN + 11)
            vec.wait_ge(feature, 2)
            step(vec.scalar_tensor_tensor(AR[:, :, 0, :], by_block(KK), -1.0, by_block(EA), ALU.mult, ALU.mult))
            step(vec.tensor_tensor(flat(AA), flat(KK), flat(AA), ALU.mult))
            vec.tensor_tensor(flat(KH), flat(U[:, 2:6, :]), flat(EI), ALU.mult).then_inc(feature, 1)
            own()
            vec.tensor_tensor(flat(BH), flat(AA), flat(EI), ALU.mult).then_inc(feature, 1)
            low(S_WIN + 12)
            vec.wait_ge(head_spread, 2)
            step(vec.tensor_tensor(flat(RKR), PS[:, 4:6, :].rearrange("p a n -> p (a n)"), flat(U[:, 10:14, :]), ALU.mult))

            vec.wait_ge(head_root, 2)
            vec.reciprocal(RN[:, :, :], RN[:, :, :]).then_inc(head_rn, 1)
            for m, name in enumerate(("sbq", "sbk")):
                vec.wait_ge(head_spread, 3 + m)
                u = flat(U[:, 14 + 4 * m:18 + 4 * m, :])
                vec.scalar_tensor_tensor(u, u, vcol(name), PS[:, 3 + 2 * m:5 + 2 * m, :].rearrange("p a n -> p (a n)"),
                                         ALU.mult, ALU.mult).then_inc(qk_ready, 1)
            for g in range(2):
                vec.wait_ge(ln_ready, g + 1)
                step(vec.scalar_tensor_tensor(LT[:, :, :], PS[:, 0:4, 0:384], 0.0, ZT[:, :, :], ALU.max, ALU.add))
                own()
                vec.tensor_tensor(LT[:, :, :], LT[:, :, :], over(mixc("sbmask"), 4), ALU.mult).then_inc(l_ready, 1)
                vec.wait_ge(e_ready, g + 1)
                vec.tensor_tensor(ZT[:, :, :], PS[:, 0:4, 0:384], over(mixc("sbneg"), 4), ALU.min).then_inc(e_masked, 1)
            vec.wait_ge(head_root, 3)
            vec.reciprocal(RN[:, 0, :], RN[:, 0, :]).then_inc(head_rn, 1)
            vec.wait_ge(head_spread, 5)
            for j in range(4):
                o = (j % 2) * 256
                ins = vec.scalar_tensor_tensor(HF[:, j, :], OS[:, j, :], vcol("sbo", j), PS[:, 2 + j // 2, o:o + 256],
                                               ALU.mult, ALU.mult)
            ins.then_inc(cat_ready, 1)

            def shares(n, lane, half):
                b0, b1, b2 = 3 * lane, 3 * lane + 1, 3 * lane + 2
                t, blk, g = T[lane], half, lane
                at = 8 * half + 4 * lane

                def tiles(bank):
                    return PS[:, bank, :].rearrange("p (a n) -> p a n", a=4)

                def double(bank):
                    return PS[:, bank:bank + 2, :].rearrange("p b (a n) -> p (b a) n", a=2)

                if n in (1, 2, 3, 4, 5, 6, 7, 8, 9, 10, 12):
                    vec.wait_ge(u_pe[lane], 12 * half + n)
                done = lambda ins: ins.then_inc(u_vec[lane], 1)
                if n == 1:
                    if half:
                        vec.wait_ge(u_pe[lane], 12)
                    two = over(mixc("lower"), 2)
                    vec.tensor_tensor(t[0][:, 0:2, :], tiles(b2)[:, 0:2, :], two, ALU.mult)
                    done(vec.tensor_tensor(t[0][:, 2:4, :], tiles(6)[:, 2 * lane:2 * lane + 2, :], two, ALU.mult))
                    done(vec.tensor_tensor(NR[:, at:at + 4, :], double(b0), over(mixc("mask2"), 4), ALU.mult))
                elif n == 2:
                    done(vec.tensor_tensor(MB[:, at:at + 4, :], double(b0), over(mixc("mask2"), 4), ALU.mult))
                elif n == 3:
                    done(vec.tensor_copy(t[4][:, :, :], tiles(b1)))
                elif n in (4, 5, 6, 8, 10):
                    to, old, bank = {4: (6, 5, b0), 5: (5, 6, b0), 6: (6, 5, b2), 8: (5, 6, b2), 10: (6, 5, b2)}[n]
                    done(vec.tensor_tensor(t[to][:, :, :], t[old][:, :, :], tiles(bank), ALU.add))
                elif n in (7, 9):
                    done(vec.tensor_copy(t[2][:, :, :], tiles(b1)))
                elif n == 12:
                    r = AR[:, 4 * g + blk:4 * g + blk + 3:2, 1, :]
                    done(vec.tensor_tensor(RT[:, 2 * g:2 * g + 2, blk * P:(blk + 1) * P],
                                           PS[:, b1, 0:256].rearrange("p (a n) -> p a n", a=2), r, ALU.add))

            for half in range(2):
                for n in range(1, 13):
                    for lane in range(2):
                        shares(n, lane, half)
            vec.wait_ge(mod_done, 1)
            step(vec.tensor_tensor(MODV[:, :, :], PS[:, 7, 0:96].rearrange("p (a n) -> p a n", n=2),
                                   over(VEC[:, V["bmod"]:V["bmod"] + 48], 2, 2), ALU.add))
            own()
            vec.tensor_scalar(MODP[:, :, :], MODV[:, :, :], 1.0, None, ALU.add).then_inc(mod_ready, 1)
            for c in range(3):
                vec.wait_ge(s_products, c + 1)
                src = PS[:, 3, 0:256].rearrange("p (a n) -> p a n", a=4)
                decay = DL[:, :, c:c + 1].broadcast_to([P, 4, HEAD])
                if c:
                    through = PS[:, 0, 0:256].rearrange("p (a n) -> p a n", a=4)
                    step(vec.tensor_tensor(ST[:, c, :, :], through, ST[:, c - 1, :, :], ALU.add))
                    own()
                    step(vec.tensor_tensor(ST[:, c, :, :], src, ST[:, c, :, :], ALU.add))
                    own()
                    src = ST[:, c, :, :]
                vec.tensor_tensor(ST[:, c, :, :], src, decay, ALU.mult).then_inc(s_ready, 1)
            vec.wait_ge(y_products, 2)
            vec.tensor_tensor(flat(YC), flat(YS), PS[:, 0:2, :].rearrange("p a n -> p (a n)"), ALU.subtract)\
               .then_inc(y_step, 1)
            vec.wait_ge(head_root, 4)
            vec.reciprocal(RN[:, 0, :], RN[:, 0, :]).then_inc(head_rn, 1)
            low(S_OUT1)
            vec.wait_ge(head_spread, 6)
            step(vec.tensor_tensor(flat(YS), flat(YC), PS[:, 4:6, :].rearrange("p a n -> p (a n)"), ALU.mult))
            own()
            for j in range(4):
                step(vec.scalar_tensor_tensor(YC[:, j, :], YS[:, j, :], vcol("lnw", j), RKR[:, j, :], ALU.mult, ALU.add))
            own()
            for j in range(4):
                ins = vec.scalar_tensor_tensor(HF[:, 4 + j, :], YC[:, j, :], vcol("lnb", j), U[:, 6 + j, :],
                                               ALU.add, ALU.mult)
            ins.then_inc(cat_ready, 1)
            low(S_OUT1 + 1)
            vec.wait_ge(cat_hi, 1)
            vec.tensor_tensor(HLO[:, :, :], HF[:, :, :], HHI[:, :, :].bitcast(F32), ALU.subtract).then_inc(cat_lo, 1)
            low(S_OUT1 + 2)
            low(S_OUT1 + 3)

            vec.wait_ge(att_loaded, 48)
            vec.wait_ge(mod_ready, 1)
            for half in range(2):
                for k in range(4 * half, 4 * half + 4):
                    ins = vec.tensor_scalar(CX[:, k, :], CX[:, k, :], MODP[:, 8 + k, 1:2], MODV[:, k, 1:2],
                                            ALU.mult, ALU.add)
                ins.then_inc(ctx_full, 1)
            for r in range(4):
                if r >= 2:
                    vec.wait_ge(gate_rows, r - 1)
                for a in range(4):
                    col = (16 if r < 2 else 40) + 4 * (r % 2) + a
                    ins = vec.tensor_scalar(DG[:, r % 2, a, :], ident, MODV[:, col, 0:1], None, ALU.mult)
                ins.then_inc(gate_diag, 1)
                if r == 1:
                    for half in range(2):
                        part = slice(4 * half, 4 * half + 4)
                        vec.wait_ge(ctx_hi, half + 1)
                        ins = vec.tensor_tensor(CLO[:, part, :], CX[:, part, :], CHI[:, part, :].bitcast(F32), ALU.subtract)
                    ins.then_inc(ctx_lo, 1)
                    low(S_CTX)
            add_half(S_OUT1 + N_OUT, 1.0)
            norm_scale(2)
            low(S_CTX + 1)
            low(S_FFN2)
            vec.wait_ge(slabs_used, S_CTX + 1)
            for n in range(2):
                vec.tensor_scalar(KALL[:, n, 256:512], PS[:, 4, n * 256:n * 256 + 256], vcol("b2", n), None, ALU.add)\
                   .then_inc(ctx_copied, 1)

            def add_value_bias(to, bank):
                return vec.tensor_tensor(to, PS[:, bank, :].rearrange("p (a n) -> p a n", a=2),
                                         over(ROWS[:, 0:256], 2), ALU.add)

            low(S_FFN2 + 1)
            vec.wait_ge(slabs_used, S_CTX + 2)
            add_value_bias(VALL[:, 2:4, :], 5).then_inc(ctx_copied, 1)
            h_scale(2, lambda k: vcol("g3", k))
            low(S_FFN2 + 2)
            ffn_vec(1, S_FFN2, True)
            add_half(S_FFN2 + N_FFN)

            low(S_WIN2 + 2)
            h_scale(3, lambda k: MODP[:, 8 + k, 0:1], lambda k: MODV[:, k, 0:1])
            low(S_WIN2 + 3)
            vec.wait_ge(slabs_used, S_WIN2 + 2)
            add_value_bias(VALL[:, 0:2, :], 2).then_inc(v_copied, 1)
            low(S_WIN2 + 4)
            low(S_WIN2 + 5)
            vec.wait_ge(head_root, 5)
            vec.reciprocal(RA[:, 0:512], RA[:, 0:512]).then_inc(head_rn, 1)
            vec.wait_ge(head_spread, 7)
            vec.scalar_tensor_tensor(KALL[:, 1, :], KALL[:, 1, :], vcol("kg"), PS[:, 4, :], ALU.mult, ALU.mult)\
               .then_inc(rope_in, 1)
            low(S_WIN2 + 6)

            def rope(n, to, src, bank, tiles):
                cos, sin = over(CT[:, 0:256], tiles), over(CT[:, 256:512], tiles)
                ps = PS[:, bank:bank + (tiles + 1) // 2, :].rearrange("p b (a n) -> p (b a) n", a=2)[:, 0:tiles, :]
                vec.wait_ge(rotated, n)
                step(vec.tensor_tensor(TR[:, 0:tiles, :], ps, sin, ALU.mult))
                step(vec.tensor_tensor(to, src, cos, ALU.mult))
                own()
                return vec.tensor_tensor(to, to, TR[:, 0:tiles, :], ALU.add)

            rope(1, QN[:, 0:4, :], QR[:, 2:6, :], 5, 4).then_inc(roped, 1)
            low(S_WIN2 + 7)
            vec.wait_ge(rotated, 2)
            for n in range(2):
                src, to = (QR[:, 0, :], KALL[:, 0, 0:256]) if n == 0 else (KALL[:, 1, 0:256], KALL[:, 1, 0:256])
                step(vec.tensor_tensor(TK[:, n, :], PS[:, 3, n * 256:n * 256 + 256], CT[:, 256:512], ALU.mult))
                step(vec.tensor_tensor(to, src, CT[:, 0:256], ALU.mult))
                own()
                vec.tensor_tensor(to, to, TK[:, n, :], ALU.add).then_inc(roped, 1)
            low(S_WIN2 + 8)
            vec.wait_ge(head_root, 6)
            vec.reciprocal(RA[:, 0:256], RA[:, 0:256]).then_inc(head_rn, 1)
            low(S_WIN2 + 9)
            vec.wait_ge(head_spread, 8)
            q = flat(QR[:, 6:10, :])
            vec.scalar_tensor_tensor(q, q, vcol("qg"), PS[:, 5:7, :].rearrange("p a n -> p (a n)"), ALU.mult, ALU.mult)\
               .then_inc(rope_in, 1)
            low(S_WIN2 + 10)
            vec.wait_ge(rope_in, 2)
            rope(3, QN[:, 4:8, :], QR[:, 6:10, :], 3, 4).then_inc(roped, 1)
            for s in range(11, 17):
                low(S_WIN2 + s)
            step(vec.tensor_scalar(NS[:, :], ROWS[:, 256:264], -1.0, None, ALU.mult))
            own()

            def maxima(i):
                br, t, j = i // 8, (i // 4) % 2, i % 4
                vec.wait_ge(scored, i + 1)
                ps = PS[:, 2 * (i % 2):2 * (i % 2) + 2, :]
                if br == 0:
                    o = 128 * (1 - t)
                    step(vec.tensor_tensor(ps[:, :, o:o + 128], ps[:, :, o:o + 128],
                                           over(CT[:, 640 + 128 * t:768 + 128 * t], 2), ALU.add))
                    own()
                at = 2 * i
                step(vec.tensor_reduce(SM[:, at % 16:at % 16 + 2], ps, mybir.AxisListType.X, ALU.max))
                own()
                to, mx = SM[:, 32 + at:34 + at], SM[:, at % 16:at % 16 + 2]
                if br == 0:
                    vec.scalar_tensor_tensor(to, mx, -SCALE, NS[:, j:j + 5:4], ALU.mult, ALU.min).then_inc(max_done, 1)
                else:
                    vec.tensor_scalar(to, mx, -SCALE, None, ALU.mult).then_inc(max_done, 1)

            def scale_o(n):
                br, t = n // 2, n % 2
                vec.wait_ge(pv_done, 4 * n + 4)
                at = 64 + 8 * n
                if br == 0:
                    step(vec.tensor_tensor(SM[:, at:at + 8], SM[:, at:at + 8], SM[:, 96 + 8 * n:104 + 8 * n], ALU.add))
                    own()
                step(vec.reciprocal(SM[:, at:at + 8], SM[:, at:at + 8]))
                own()
                vec.tensor_tensor(OT[:, t, br * 512:br * 512 + 512].rearrange("p (h c) -> p h c", h=8),
                                  PS[:, 6 + t, :].rearrange("p (h c) -> p h c", h=8),
                                  SM[:, at:at + 8].unsqueeze(2).broadcast_to([P, 8, 64]), ALU.mult).then_inc(o_scaled, 1)

            for i in range(17):
                if i < 16:
                    maxima(i)
                if i >= 1:
                    vec.wait_ge(p_turned, i)
                    if i >= 3:
                        vec.wait_ge(pv_done, i - 2)
                    vec.tensor_copy(PT[:, (i - 1) % 2, 1, :], PS[:, 5, :]).then_inc(pt_vec, 1)
                if i == 7:
                    vec.wait_ge(max_done, 8)
                    for t in range(TB):
                        for par in range(2):
                            ins = vec.tensor_tensor(SM[:, 96 + 8 * t + par:104 + 8 * t + par:2],
                                                    SM[:, 32 + 8 * t + par:40 + 8 * t + par:2],
                                                    ROWS[:, 256 + 4 * par:260 + 4 * par], ALU.add)
                    ins.then_inc(sink_in, 1)
                if i == 9:
                    vec.wait_ge(sink_exp, 1)
                if i in (9, 13, 15):
                    scale_o((9, 13, 15).index(i))
            scale_o(3)
            h_scale(4, lambda k: 1.0)
            for half in range(2):
                vec.wait_ge(slabs_used, S_BRANCH + 2 * half + 2)
                part = slice(4 * half, 4 * half + 4)
                bank = 4 * half
                step(vec.tensor_tensor(flat(MF[:, part, :]), flat(GT[:, part, :]),
                                       PS[:, bank:bank + 2, :].rearrange("p a n -> p (a n)"), ALU.mult))
                step(vec.tensor_tensor(flat(MT), flat(GT[:, 8 + 4 * half:12 + 4 * half, :]),
                                       PS[:, bank + 2:bank + 4, :].rearrange("p a n -> p (a n)"), ALU.mult))
                own()
                vec.tensor_tensor(flat(MF[:, part, :]), flat(MF[:, part, :]), flat(MT), ALU.add).then_inc(merged, 1)
                vec.wait_ge(m_hi, half + 1)
                vec.tensor_tensor(MLO[:, part, :], MF[:, part, :], MHI[:, part, :].bitcast(F32), ALU.subtract)\
                   .then_inc(m_lo, 1)
                low(S_BRANCH + 3 + 2 * half)
                low(S_BRANCH + 4 + 2 * half)
            low(S_OUT2 + 3)
            low(S_FFN3)

            def layer_norm(n, used):
                vec.wait_ge(slabs_used, used)
                vec.wait_ge(row_loaded, 16 * n + 16)
                vec.wait_ge(gate_row_copied, 4)
                for t in range(TB):
                    y = PS[:, 2 * t:2 * t + 2, :].rearrange("p a n -> p (a n)")
                    step(vec.tensor_tensor(YT[:, t, :], GB[:, n, :], y, ALU.mult))
                    own()
                    step(vec.scalar_tensor_tensor(X[:, t, :], X[:, t, :], DEEPNORM_ALPHA, YT[:, t, :], ALU.mult, ALU.add))
                    own()
                    for h in range(2):
                        step(vec.bn_stats(BN[:, t, h, :], X[:, t, h * HALF:(h + 1) * HALF]))
                    own()
                    vec.bn_aggr(SM[:, 16 + 4 * t:18 + 4 * t], BN[:, t, :, :].rearrange("p a n -> p (a n)"))\
                       .then_inc(ln_var, 1)
                for t in range(TB):
                    vec.wait_ge(ln_root, 2 * n + t + 1)
                    step(vec.reciprocal(SM[:, 19 + 4 * t:20 + 4 * t], SM[:, 18 + 4 * t:19 + 4 * t]))
                    own()
                    step(vec.tensor_scalar(X[:, t, :], X[:, t, :], SM[:, 16 + 4 * t:17 + 4 * t], SM[:, 19 + 4 * t:20 + 4 * t],
                                           ALU.subtract, ALU.mult))
                    own()
                    step(vec.tensor_tensor(X[:, t, :], X[:, t, :], ROW[:, 0:D], ALU.mult))
                    own()
                    for h in range(2):
                        part = slice(h * HALF, (h + 1) * HALF)
                        vec.tensor_tensor(X[:, t, part], X[:, t, part], ROW[:, D + h * HALF:D + (h + 1) * HALF], ALU.add)\
                           .then_inc(x_new, 1)

            low(S_FFN3 + 1)
            layer_norm(0, S_OUT2 + N_OUT)
            h_scale(5, lambda k: MODP[:, 32 + k, 0:1], lambda k: MODV[:, 24 + k, 0:1])
            low(S_FFN3 + 2)
            ffn_vec(2, S_FFN3, False)
            layer_norm(1, S_FFN3 + N_FFN)
    return nc


def place(pieces, width):
    import numpy as np
    return np.ascontiguousarray(np.concatenate([np.asarray(p, np.float32).reshape(P, -1) for p in pieces], axis=1))


def constants():
    import numpy as np
    i, j = np.arange(P)[:, None], np.arange(P)[None, :]
    heads = np.zeros((P, 4, 16))
    spread = np.zeros((P, 4, P))
    for t in range(4):
        for h in range(2):
            heads[64 * h:64 * h + 64, t, 2 * t + h] = 1
            spread[2 * t + h, t, 64 * h:64 * h + 64] = 1
    c_all = place([np.eye(P), np.ones((P, P)), heads, spread], N_ALL)

    same = lambda n: i // n == j // n
    on = np.ones((P, P))
    strict = i < j
    c_mix = place([
        strict & same(64), (i <= j) & same(64),
        (j < i) & same(64),
        same(16), same(32) & ~same(16), same(64) & ~same(32),
        -1.0 * (i >= j), -on,
        strict, on, strict,
        np.where(strict, 0, NEG), 0 * on, np.where(strict, 0, NEG),
        same(64), same(64) / 64.0,
        np.where(np.arange(SEQ)[None, :] % 64 == 0, 0.0, 1.0) * np.ones((P, 1)),
    ], N_MIX)

    grid, theta, n_freq = 64, np.float32(10000.0), HEAD // 4
    freq = theta ** (-np.arange(n_freq, dtype=np.float32) / np.float32(n_freq))
    pos = np.arange(SEQ)
    where = np.arange(P) % HEAD
    axis = np.where((where < 32)[:, None], (pos // grid)[None, :], (pos % grid)[None, :]).astype(np.float32)
    angle = axis * freq[where % 16][:, None].astype(np.float32)
    rot = np.zeros((P, P))
    for c in range(P):
        if c % 32 < 16:
            rot[c + 16, c] = -1
        else:
            rot[c - 16, c] = 1
    c_att = place([np.cos(angle), np.sin(angle), rot,
                   np.where(j <= i, 0, NEG), np.where(j >= i, 0, NEG)], N_ATT)
    return c_all, c_mix, c_att


HEAD_ORDER = [0, 4, 1, 5, 2, 6, 3, 7]


def layout(i):
    import numpy as np
    f = {k: np.asarray(v, np.float32) for k, v in i.items()}

    def by_columns(w, width=256):
        kt, n = w.shape[0] // P, w.shape[1] // width
        return w.reshape(kt, P, n, width).transpose(2, 1, 0, 3).reshape(n, P, kt * width)

    def by_rows(w):
        per = SLAB // w.shape[1]
        return w.reshape(-1, per, P, w.shape[1]).transpose(0, 2, 1, 3).reshape(-1, P, SLAB)

    def ffn(gate, up, down):
        g, u, d = by_columns(gate), by_columns(up), by_rows(down)
        order = [g[0], u[0]]
        for p in range(1, PAIRS):
            order += [g[p], u[p], d[p - 1]]
        return order + [d[PAIRS - 1]]

    w = f["w_in"][0]
    sb, rw = w[:, :1536], w[:, 1536:]
    win = np.concatenate([rw[:, 1536:1664], rw[:, 1664:1792], rw[:, 512:1024], rw[:, 0:512], rw[:, 1024:1536],
                          sb[:, 0:1024]], axis=1)
    w2 = f["w_in_2"][0]
    by_head = np.concatenate([np.arange(h * HEAD, (h + 1) * HEAD) for h in HEAD_ORDER])
    qa, ka, va = w2[:, 0:512][:, by_head], w2[:, 512:640], w2[:, 640:768]
    qb, kb, vb = w2[:, 768:1280][:, by_head], w2[:, 1280:1408], w2[:, 1408:1536]
    keys, values = np.concatenate([ka, kb], axis=1), np.concatenate([va, vb], axis=1)
    ba, bb = by_columns(f["w_branch_a_2"][0][by_head], 512), by_columns(f["w_branch_b_2"][0][by_head], 512)
    slabs = (ffn(f["ffn1_gate"][0], f["ffn1_up"][0], f["ffn1_down"][0])
             + list(by_columns(win)) + list(by_rows(sb[:, 1024:1536]))
             + list(by_columns(f["w_mod_2"][0])) + list(by_rows(f["w_out"][0]))
             + list(by_columns(keys)) + list(by_columns(values))
             + ffn(f["ffn2_gate"][0], f["ffn2_up"][0], f["ffn2_down"][0])
             + list(by_columns(keys)) + list(by_columns(values))
             + list(by_columns(np.concatenate([qa, qb, w2[:, 1536:]], axis=1)))
             + [ba[0], bb[0], ba[1], bb[1]] + list(by_rows(f["w_out_2"][0]))
             + ffn(f["w_up_2"][0][:, :D_FF], f["w_up_2"][0][:, D_FF:], f["w_down_2"][0]))
    slabs = np.stack(slabs)

    def cols(v):
        return v.reshape(-1, P).T

    mu = f["rw_mu"][0]
    mu = np.concatenate([mu[1536:1664], mu[1664:1792], mu[512:1024], mu[0:512], mu[1024:1536]])
    b2 = f["b_in_2"][0]
    b2 = np.concatenate([b2[512:640], b2[1280:1408], b2[0:512][by_head], b2[768:1280][by_head], b2[1536:]])
    twice = lambda v: np.concatenate([v, v]).reshape(P, 1)
    cw, cb = f["conv_w_2"][0], f["conv_b_2"][0]
    taps = np.concatenate([cw, cb[None]], axis=0).reshape(4, 2, PAIRS, 2, P)
    taps = taps.transpose(4, 2, 1, 3, 0).reshape(P, PAIRS * 16)
    taps = np.concatenate([taps, np.zeros((P, 16), np.float32)], axis=1)
    c2 = np.stack([cols(f["c_2"][0]), cols(f["c_ctx_2"])], axis=2).reshape(P, 16)
    vecs = np.concatenate([
        cols(f["norm_ffn1"][0]), cols(f["norm_mix"][0]), cols(f["norm_ffn2"][0]), twice(f["sb_q_norm"][0]),
        twice(f["sb_k_norm"][0]), cols(f["sb_out_norm"][0]), cols(mu), cols(f["rw_w0"][0]), cols(f["rw_a0"][0]),
        cols(f["rw_k_k"][0]), cols(f["rw_k_a"][0]), cols(f["rw_r_k"][0].reshape(-1)), cols(f["rw_ln_w"][0]),
        cols(f["rw_ln_b"][0]), c2, cols(f["b_mod_2"][0]), cols(b2), twice(f["q_norm_g_2"][0]),
        twice(f["k_norm_g_2"][0]), taps], axis=1)
    c_all, c_mix, c_att = constants()
    lora = np.stack([np.concatenate([f["rw_w2"][0], f["rw_a2"][0]]), f["rw_g2"][0]], axis=1)
    b_in = f["b_in_2"][0]
    rows = np.concatenate([f["ln1_g_2"][0], f["ln1_b_2"][0], f["ln2_g_2"][0], f["ln2_b_2"][0],
                           b_in[640:768], b_in[1408:1536], f["attn_sink_2"][0]]).reshape(1, N_ROW)
    return {
        "slabs": slabs, "x": f["x"][0].reshape(TB, P, D),
        "ctx_t": f["ctx_2"][0].T.reshape(KT, P, SEQ).transpose(1, 0, 2),
        "vecs": vecs, "c_all": c_all, "c_mix": c_mix, "c_att": c_att, "lora": lora, "rows": rows,
    }


def kernel(**inputs):
    import numpy as np
    import concourse.bacc as bacc
    from concourse.bass_utils import run_bass_kernel_spmd

    nc = bacc.Bacc("TRN2", target_bir_lowering=False, num_devices=1)
    arrays = {f"in_{k}": np.ascontiguousarray(v) for k, v in layout(inputs).items()}
    args = [nc.dram_tensor(k, a.shape, mybir.dt.from_np(a.dtype), kind="ExternalInput").ap()
            for k, a in arrays.items()]
    out = nc.dram_tensor("out", (TB, P, D), F32, kind="ExternalOutput").ap()
    build_block(nc, *args, out)
    r = run_bass_kernel_spmd(nc, [arrays], core_ids=[0])
    return r.results[0]["out"].reshape(1, SEQ, D)
```

```python
from contextlib import ExitStack

import concourse.bass as bass
from concourse import mybir

F32 = mybir.dt.float32
F32R = mybir.dt.float32r
BF16 = mybir.dt.bfloat16
ALU = mybir.AluOpType
ACT = mybir.ActivationFunctionType
ds = bass.ds

P = 128
SEQ = 256
TB = SEQ // P
D = 1024
KT = D // P
HALF = D // 2
D_FF = 2816
PAIRS = D_FF // (2 * P)
SLAB = 2048
RING = 3

N_FFN = 3 * PAIRS
N_WIN, N_MOD, N_OUT, N_CTX, N_WIN2, N_BRANCH = 13, 9, 4, 2, 14, 4
B_FFN1 = 0
B_WIN = B_FFN1 + N_FFN
B_MOD = B_WIN + N_WIN
B_OUT1 = B_MOD + N_MOD
B_CTX = B_OUT1 + N_OUT
B_FFN2 = B_CTX + N_CTX
B_WIN2 = B_FFN2 + N_FFN
B_BRANCH = B_WIN2 + N_WIN2
B_OUT2 = B_BRANCH + N_BRANCH
B_FFN3 = B_OUT2 + N_OUT
N_SLABS = B_FFN3 + N_FFN
N_SIDE = 6 * D // 256 - N_MOD
S_FFN1, S_WIN = B_FFN1, B_WIN
S_OUT1, S_CTX, S_FFN2, S_WIN2, S_BRANCH, S_OUT2, S_FFN3 = (
    b - N_MOD for b in (B_OUT1, B_CTX, B_FFN2, B_WIN2, B_BRANCH, B_OUT2, B_FFN3))

RMS_EPS = 1e-6
LN_EPS = 1e-5
LNX_EPS = 64e-5
DECAY_SCALE = 0.6065306597126334
DEEPNORM_ALPHA = 2.0 ** 0.25
HEAD = 64
SCALE = HEAD ** -0.5
NEG = -1.0e30
LEAD = 1
ACTS, VECS, PARTS = 9, 12, 5
MOD_TILES = 2 * N_MOD
POOL_STEPS = 5
N_RING_POOL = 6
SUM_STEPS = 4
MOD_STAGES = {1: 3, 4: 4, 7: 5}


V = {}
_at = 0
for _name, _n in (("g1", KT), ("g2", KT), ("g3", KT), ("sbq", 1), ("sbk", 1), ("sbo", 4), ("mu", 14),
                  ("w0", 4), ("a0", 4), ("kk", 4), ("ka", 4), ("rk", 4), ("lnw", 4), ("lnb", 4),
                  ("c", 2 * KT), ("bmod", 48), ("b2", 26), ("qg", 1), ("kg", 1), ("ln1g", KT), ("ln1b", KT), ("conv", 16 * (PAIRS + 1))):
    V[_name] = _at
    _at += _n
N_VEC = _at

N_ALL = 832
C_MIX = {"mask2": (0, 256), "lower": (256, 128), "same16": (384, 128), "only32": (512, 128), "only64": (640, 128),
         "suffix": (768, 128), "minus": (896, 128), "sbmask": (1024, 384), "sbneg": (1408, 384),
         "block": (1792, 128), "mean": (1920, 128), "chunk": (2048, 256)}
N_MIX = 2304
N_ATT = 896
N_ROW = 4 * D + 256 + 8


def build_block(nc, slabs, mods, x, ctx_t, vecs, c_all, c_mix, c_att, lora, rows, out):
    stack = ExitStack()
    with stack:
        def sb(name, shape, dt=F32, where=stack):
            return where.enter_context(nc.sbuf_tensor(name, shape, dt))

        def sem(name):
            return stack.enter_context(nc.semaphore(name))

        stage = sb("stage", [P, RING, SLAB])
        X = sb("x_res", [P, TB, D])
        HF = sb("h_full", [P, KT, SEQ])
        VEC = sb("vec", [P, N_VEC])
        CA = sb("c_all_sb", [P, N_ALL])
        ZERO = sb("zero", [P, 512], BF16)
        MODV = sb("mod_v", [P, 48, 2])
        SC = sb("silu_c", [P, KT, 2])
        GAIN = sb("gain", [P, 2, KT])
        BN = sb("bn", [P, TB, 2, 6])
        SM = sb("small", [P, 128])
        EPS = sb("eps", [P, 4])
        MODP = sb("mod_p", [P, 48, 2])
        ident = CA[:, 0:128]
        ones = CA[:, 128:256]

        def spread(j):
            return CA[0:16, 320 + j * 128:448 + j * 128]

        def heads(j):
            return CA[:, 256 + 16 * j:272 + 16 * j]

        w_mix = ExitStack()
        ANV = sb("anv", [P, TB, 8, 128], where=w_mix)
        BTOK = sb("b_tok", [P, TB, 512], where=w_mix)
        KTOK = sb("k_tok", [P, TB, 512], where=w_mix)
        VTOK = sb("v_tok", [P, TB, 512], where=w_mix)
        NR = sb("n_r", [P, 16, 256], where=w_mix)
        MB = sb("m_b", [P, 16, 256], where=w_mix)
        AU = sb("a_u", [P, TB, 8, 128], where=w_mix)
        RT = sb("r_t", [P, 4, SEQ], where=w_mix)
        w_mix.close()
        WHI = sb("w_hi", [P, RING, SLAB], F32R)
        WLO = sb("w_lo", [P, RING, SLAB], F32R)
        HHI = sb("h_hi", [P, KT, SEQ], F32R)
        HLO = sb("h_lo", [P, KT, SEQ], F32R)

        a_mix = ExitStack()
        U = sb("u", [P, 22, SEQ], where=a_mix)
        SBV = sb("sb_v", [P, TB, 512], where=a_mix)
        early = ExitStack()
        EA = sb("e_a", [P, 4, SEQ], where=early)
        ER = sb("e_r", [P, 4, SEQ], where=early)
        EI = sb("e_i", [P, 4, SEQ], where=early)
        AA = sb("aa", [P, 4, SEQ], where=early)
        KK = sb("kk", [P, 4, SEQ], where=early)
        SQ = sb("sq", [P, 4, SEQ], where=early)
        DT = sb("d_t", [P, 2, SEQ], where=early)
        LW = sb("lw", [P, SEQ], where=early)
        LG = sb("lg", [P, SEQ], where=early)
        early.close()
        sbt = ExitStack()
        ZT = sb("z_t", [P, 4, 384], where=sbt)
        LT = sb("l_t", [P, 4, 384], where=sbt)
        SQ2 = sb("sq2", [P, 4, SEQ], where=sbt)
        OS = sb("o_s", [P, 4, SEQ], where=sbt)
        sbt.close()
        yset = ExitStack()
        YS = sb("y_s", [P, 4, SEQ], where=yset)
        YC = sb("y_c", [P, 4, SEQ], where=yset)
        YQ = sb("y_q", [P, 4, SEQ], where=yset)
        yset.close()
        T = [[sb(f"t{lane}_{n}", [P, 4, 128], where=a_mix) for n in range(7)] for lane in range(2)]
        RKR = sb("rkr", [P, 4, SEQ], where=a_mix)
        AR = sb("a_r", [P, 8, 2, 128], where=a_mix)
        BH = sb("b_h", [P, 4, SEQ], where=a_mix)
        KH = sb("k_h", [P, 4, SEQ], where=a_mix)
        CM = sb("c_mix_sb", [P, N_MIX], where=a_mix)
        LORA = sb("lora", [P, 2, 512], where=a_mix)
        ET = sb("e_t", [P, 2, 4, HEAD], where=a_mix)
        ST = sb("s_t", [P, 3, 4, HEAD], where=a_mix)
        DL = sb("d_l", [P, 4, 4], where=a_mix)
        KA1 = sb("k_a1", [P, 4], where=a_mix)
        RN = sb("r_n", [16, 2, SEQ], where=a_mix)
        a_mix.close()

        side_stage = ExitStack()
        MST = sb("mod_stage", [P, RING, SLAB], where=side_stage)
        side_stage.close()
        a_att = ExitStack()
        KALL = sb("k_all", [P, 2, 2 * SEQ], where=a_att)
        VALL = sb("v_all", [P, 4, 256], where=a_att)
        ROW = sb("row", [P, 2 * D], where=a_att)
        ROWS = sb("row_small", [P, 264], where=a_att)
        GB = sb("gate_b", [P, 2, D], where=a_att)
        CT = sb("c_att_sb", [P, N_ATT], where=a_att)
        ffn = ExitStack()
        XS = sb("x_s", [P, TB, D], where=ffn)
        SG = sb("s_g", [P, 2, 2, SEQ], where=ffn)
        HID = sb("hid", [P, 2, 2, SEQ], where=ffn)
        DHI = sb("d_hi", [P, 2, 2, SEQ], F32R, where=ffn)
        DLO = sb("d_lo", [P, 2, 2, SEQ], F32R, where=ffn)
        CW = sb("c_w", [P, 2, 16], where=ffn)
        side_set = ExitStack()
        ACC = sb("mod_acc", [P, N_SIDE * 256], where=side_set)
        side_set.close()
        CG = sb("c_g", [P, 2, 4, SEQ], where=ffn)
        CX = sb("ctx_f", [P, KT, SEQ], where=ffn)
        CHI = sb("ctx_hi", [P, KT, SEQ], F32R, where=ffn)
        CLO = sb("ctx_lo", [P, KT, SEQ], F32R, where=ffn)
        DG = sb("d_g", [P, 2, 4, 128], where=ffn)
        ffn.close()
        att = ExitStack()
        GT = sb("gate_t", [P, 16, SEQ], where=att)
        QR = sb("q_raw", [P, 10, SEQ], where=att)
        att2 = ExitStack()
        QN = sb("q_n", [P, 8, SEQ], where=att2)
        PM = sb("p_m", [P, 2, 2, 512], where=att2)
        PT = sb("p_t", [P, 2, 2, 512], where=att2)
        OT = sb("o_tok", [P, TB, D], where=att2)
        TR = sb("t_r", [P, 4, SEQ], where=att2)
        TK = sb("t_k", [P, 2, SEQ], where=att2)
        NS = sb("n_s", [P, 8], where=att2)
        RA = sb("r_a", [16, 768], where=att2)
        att2.close()
        MF = sb("m_f", [P, KT, SEQ], where=att)
        MHI = sb("m_hi", [P, KT, SEQ], F32R, where=att)
        MLO = sb("m_lo", [P, KT, SEQ], F32R, where=att)
        MT = sb("m_t", [P, 4, SEQ], where=att)
        YT = sb("y_t", [P, TB, D], where=att)
        att.close()
        a_att.close()

        MOD_SUM = [HF[:, 4:6, :], HF[:, 6:8, :]]

        PS = stack.enter_context(nc.psum_tensor("psum", [P, 8, 512], F32))

        stage_ready = [sem(f"stage_ready{n}") for n in range(RING)]
        stage_free = [sem(f"stage_free{n}") for n in range(RING)]
        hi_ready = sem("hi_ready")
        block_done = sem("block_done")
        lo_ready = sem("lo_ready")
        slabs_used = sem("slabs_used")
        silu_done = sem("silu_done")
        hidden_done = sem("hidden_done")
        hid_hi = sem("hid_hi")
        hid_lo = sem("hid_lo")
        act_step = sem("act_step")
        vec_step = sem("vec_step")
        x_loaded = [sem(f"x_loaded{t}") for t in range(TB)]
        vec_loaded = sem("vec_loaded")
        zero_ready = sem("zero_ready")
        eps_ready = sem("eps_ready")
        x_new = sem("x_new")
        root = sem("root")
        xs_ready = sem("xs_ready")
        x_turned = sem("x_turned")
        h_full = sem("h_full_ready")
        h_hi = sem("h_hi_ready")
        h_lo = sem("h_lo_ready")
        out_done = sem("out_done")
        mix_loaded = sem("mix_loaded")
        u_copied = sem("u_copied")
        shifted = sem("shifted")
        lora_in = sem("lora_in")
        lora_done = sem("lora_done")
        sigma_ready = sem("sigma_ready")
        decay_ready = sem("decay_ready")
        exp_ready = sem("exp_ready")
        head_sum = sem("head_sum")
        head_root = sem("head_root")
        head_rn = sem("head_rn")
        head_spread = sem("head_spread")
        feature = sem("feature")
        gate_copied = sem("gate_copied")
        qk_square = sem("qk_square")
        qk_ready = sem("qk_ready")
        sbv_ready = sem("sbv_ready")
        tok_turned = sem("tok_turned")
        tok_copied = sem("tok_copied")
        tok_moved = sem("tok_moved")
        z_ready = sem("z_ready")
        ln_ready = sem("ln_ready")
        l_ready = sem("l_ready")
        e_ready = sem("e_ready")
        e_masked = sem("e_masked")
        att_ready = sem("att_ready")
        o_ready = sem("o_ready")
        o_copied = sem("o_copied")
        u_pe = [sem(f"unit_products{n}") for n in range(2)]
        u_act = [sem(f"unit_act{n}") for n in range(2)]
        u_vec = [sem(f"unit_vec{n}") for n in range(2)]
        u_part = [sem(f"unit_part{n}") for n in range(2)]
        s_products = sem("state_products")
        s_ready = sem("state_ready")
        y_products = sem("y_products")
        y_step = sem("y_step")
        cat_ready = sem("cat_ready")
        cat_hi = sem("cat_hi")
        cat_lo = sem("cat_lo")
        mod_done = sem("mod_done")
        mod_copied = sem("mod_copied")
        side_loaded = [sem(f"side_loaded{n}") for n in range(RING)]
        sum_step = sem("sum_step")
        sums_read = sem("sums_read")
        side_step = sem("side_step")
        mod_ready = sem("mod_ready")
        att_loaded = sem("att_loaded")
        row_loaded = sem("row_loaded")
        gate_diag = sem("gate_diag")
        gate_rows = sem("gate_rows")
        gate_row_copied = sem("gate_row_copied")
        ctx_full = sem("ctx_full")
        ctx_hi = sem("ctx_hi")
        ctx_lo = sem("ctx_lo")
        ctx_copied = sem("ctx_copied")
        p_copied = sem("p_copied")
        v_copied = sem("v_copied")
        k_square = sem("k_square")
        rope_in = sem("rope_in")
        rotated = sem("rotated")
        roped = sem("roped")
        scored = sem("scored")
        max_done = sem("max_done")
        sink_in = sem("sink_in")
        sink_exp = sem("sink_exp")
        p_ready = sem("p_ready")
        p_turned = sem("p_turned")
        pt_act = sem("pt_act")
        pt_vec = sem("pt_vec")
        pv_done = sem("pv_done")
        o_scaled = sem("o_scaled")
        merged = sem("merged")
        m_hi = sem("m_hi")
        m_lo = sem("m_lo")
        ln_var = sem("ln_var")
        ln_root = sem("ln_root")
        ln_scale = sem("ln_scale")
        ln_normed = sem("ln_normed")
        center = sem("center")
        tap_before = sem("tap_before")
        conv_done = sem("conv_done")
        taps_ready = sem("taps_ready")

        block = stack.enter_context(nc.Block())

        def slot_of(s):
            return s % RING

        def shift(s):
            return N_MOD if s >= S_OUT1 else 0

        def mixc(name):
            a, n = C_MIX[name]
            return CM[:, a:a + n]

        def vcol(name, j=0):
            return VEC[:, V[name] + j:V[name] + j + 1]

        def over(ap, n, at=1):
            return ap.unsqueeze(at).broadcast_to([P, n, ap.shape[1]] if at == 1 else [P, ap.shape[1], n])

        def unit_heads(g):
            return [4 * g + h for h in (0, 2, 1, 3)]

        @block.sync
        def _(sp):
            for t in range(TB):
                sp.dma_start(X[:, t, :], x[t, :, :]).then_inc(x_loaded[t], 16)
            sp.dma_start(VEC[:, :], vecs).then_inc(vec_loaded, 16)
            sp.dma_start(CA[:, :], c_all).then_inc(vec_loaded, 16)
            for i in range(RING):
                sp.dma_start(stage[:, i, :], slabs[i, :, :]).then_inc(stage_ready[i], 16)
            sp.dma_start(CM[:, :], c_mix).then_inc(mix_loaded, 16)
            sp.dma_start(LORA[:, :, :], lora).then_inc(mix_loaded, 16)
            full = N_SLABS // RING
            with sp.Fori(1, full) as i:
                for j in range(RING):
                    sp.wait_ge(stage_free[j], i)
                    sp.dma_start(stage[:, j, :], slabs[ds(i * RING + j, 1), :, :].rearrange("a p n -> (a p) n"))\
                      .then_inc(stage_ready[j], 16)
            for s in range(full * RING, N_SLABS):
                sp.wait_ge(stage_free[s % RING], full)
                sp.dma_start(stage[:, s % RING, :], slabs[s, :, :]).then_inc(stage_ready[s % RING], 16)
            sp.wait_ge(x_new, 20)
            sp.dma_start(out.rearrange("t p n -> p t n"), X[:, :, :]).then_inc(out_done, 16)
            sp.wait_ge(out_done, 16)

        @block.gpsimd
        def _(pool):
            pool.memset(ZERO[:, :], 0.0).then_inc(zero_ready, 1)
            def load(slot, n):
                pool.dma_start(MST[:, slot, :], mods[ds(n, 1), :, :].rearrange("a p n -> (a p) n"))\
                    .then_inc(side_loaded[slot], 16)

            def side(slot, i, acc):
                done = i * (RING * POOL_STEPS) + slot * POOL_STEPS
                pool.wait_ge(side_loaded[slot], i * 16 + 16)
                by = SC[:, :, 0:1].broadcast_to([P, KT, 256])
                w = MST[:, slot, :].rearrange("p (k n) -> p k n", k=KT)
                pool.tensor_tensor(w, w, by, ALU.mult).then_inc(side_step, 1)
                for n in range(1, POOL_STEPS - 1):
                    half = SLAB >> n
                    pool.wait_ge(side_step, done + n)
                    pool.tensor_tensor(MST[:, slot, 0:half], MST[:, slot, 0:half], MST[:, slot, half:2 * half], ALU.add)\
                        .then_inc(side_step, 1)
                pool.wait_ge(side_step, done + (POOL_STEPS - 1))
                pool.tensor_copy(acc, MST[:, slot, 0:256]).then_inc(side_step, 1)
                pool.wait_ge(side_step, done + POOL_STEPS)

            pool.wait_ge(hi_ready, 1)
            for slot in range(RING):
                load(slot, slot)
            pool.wait_ge(hid_hi, LEAD)
            with pool.Fori(0, N_SIDE // RING - 1) as i:
                for slot in range(RING):
                    side(slot, i, ACC[:, ds(i * (RING * 256) + slot * 256, 256)])
                    load(slot, i * RING + (slot + RING))
            for slot in range(RING):
                n = N_SIDE - RING + slot
                side(slot, N_SIDE // RING - 1, ACC[:, n * 256:n * 256 + 256])
            pool.wait_ge(slabs_used, S_WIN + N_WIN)
            product = AU[:, :, :, :].rearrange("p t h n -> p (t h n)")
            steps = 0
            for i in range(N_RING_POOL):
                slot = (B_MOD + i) % RING
                pool.wait_ge(stage_ready[slot], 16 * ((B_MOD + i) // RING + 1))
                if i >= 2:
                    pool.wait_ge(sums_read, i - 1)
                for kind in (1, 0):
                    w = stage[:, slot, :]
                    to = product if kind else w
                    if steps:
                        pool.wait_ge(sum_step, steps)
                    pool.tensor_tensor(to.rearrange("p (k n) -> p k n", k=KT), w.rearrange("p (k n) -> p k n", k=KT),
                                       SC[:, :, kind:kind + 1].broadcast_to([P, KT, 256]), ALU.mult).then_inc(sum_step, 1)
                    for n in range(1, SUM_STEPS):
                        half = SLAB >> n
                        on = MOD_SUM[kind][:, i % 2, :] if n == SUM_STEPS - 1 else to[:, 0:half]
                        pool.wait_ge(sum_step, steps + n)
                        pool.tensor_tensor(on, to[:, 0:half], to[:, half:2 * half], ALU.add).then_inc(sum_step, 1)
                    steps += SUM_STEPS
                pool.wait_ge(sum_step, steps)
                pool.sem_inc(stage_free[slot], 1)
            pool.wait_ge(x_new, 16)
            with pool.Fori(0, 6) as i:
                for par in range(2):
                    if par:
                        pool.wait_ge(hidden_done, LEAD + i * 2 + 2 * PAIRS)
                    else:
                        pool.wait_ge(hidden_done, LEAD + i * 2 + (2 * PAIRS - 1))
                    pool.tensor_copy(CW[:, par, :], VEC[:, ds(i * 32 + (V["conv"] + 16 * par), 16)]).then_inc(taps_ready, 1)

        @block.tensor
        def _(pe):
            def mm(out_ap, lhs, rhs, start):
                return pe.matmul(out_ap, lhs, rhs, start=start, stop=True, skip_group_check=True)

            def three(out_ap, w_hi, w_lo, h_high, h_low, first, swap=False):
                ins = None
                for n, (w, h) in enumerate(((w_hi, h_high), (w_hi, h_low), (w_lo, h_high))):
                    lhs, rhs = (h, w) if swap else (w, h)
                    ins = mm(out_ap, lhs, rhs, first and n == 0)
                return ins

            def columns(slot, c, out_ap, hi, lo):
                for k in range(KT):
                    a = k * 256 + c * P
                    ins = three(out_ap, WHI[:, slot, a:a + P], WLO[:, slot, a:a + P],
                                hi[:, k, :], lo[:, k, :], k == 0)
                return ins

            def turn_x(src):
                for k in range(KT):
                    for t in range(TB):
                        o = (k % 2) * 256 + t * P
                        ins = pe.transpose(PS[:, 4 + k // 2, o:o + P], src[:, t, k * P:(k + 1) * P], ident)
                    if k % 2:
                        ins.then_inc(x_turned, 1)

            def down(slot, buf, last=False):
                for t in range(TB):
                    for f in range(2):
                        hi = DHI[:, buf, f, t * P:(t + 1) * P]
                        lo = DLO[:, buf, f, t * P:(t + 1) * P]
                        for n in range(2):
                            a = f * D + n * HALF
                            ins = three(PS[:, 2 * t + n, :], WHI[:, slot, a:a + HALF], WLO[:, slot, a:a + HALF],
                                        hi, lo, False, swap=True)
                    if last and t == 0:
                        ins.then_inc(block_done, 1)
                ins.then_inc(slabs_used, 1)

            def gate_up(base, p, par):
                for m in range(2):
                    pe.wait_ge(lo_ready, base + 3 * p + m + 1)
                    for f in range(2):
                        ins = columns(slot_of(base + m), f, PS[:, 4 + 2 * par + f, m * 256:m * 256 + 256], HHI, HLO)
                    ins.then_inc(slabs_used, 1)

            def ffn_products(q, turn, b):
                for n in range(4):
                    mm(PS[:, n, :], ZERO[:, 0:P], ZERO[:, :], True)
                pe.wait_ge(h_lo, 2 * turn + 2)
                gate_up(b, 0, 0)
                with pe.Fori(0, PAIRS // 2) as i:
                    for par in range(1, 3):
                        p = i * 2 + par
                        pe.wait_ge(hidden_done, LEAD + i * 2 + (PAIRS * q + par - 1))
                        gate_up(b - 1, p, par % 2)
                        pe.wait_ge(hid_lo, i * 2 + (PAIRS * q + par))
                        pe.wait_ge(lo_ready, i * 6 + (b + 3 * par + 2))
                        down(slot_of(b + 1), 1 - par % 2)
                pe.wait_ge(hid_lo, PAIRS * q + PAIRS)
                pe.wait_ge(lo_ready, b + N_FFN)
                down(slot_of(b + N_FFN - 1), 0, last=True)

            pe.wait_ge(zero_ready, 1)
            pe.wait_ge(vec_loaded, 32)
            pe.wait_ge(xs_ready, 2)
            turn_x(XS)
            ffn_products(0, 0, S_FFN1)

            pe.wait_ge(side_step, N_SIDE * POOL_STEPS)
            pe.wait_ge(hidden_done, LEAD + PAIRS)
            for n in range(2 * N_SIDE):
                ins = mm(PS[:, 7, n:n + 1], ACC[:, n * P:(n + 1) * P], ones[:, 0:1], True)
            ins.then_inc(mod_done, 1)

            pe.wait_ge(xs_ready, 4)
            pe.wait_ge(mod_copied, 1)
            turn_x(XS)
            pe.wait_ge(h_lo, 4)

            def win_slab(s):
                pe.wait_ge(lo_ready, S_WIN + s + 1)
                if s >= 2:
                    pe.wait_ge(u_copied, s - 1)
                for c in range(2):
                    ins = columns(slot_of(S_WIN + s), c, PS[:, s % 2, c * 256:c * 256 + 256], HHI, HLO)
                ins.then_inc(slabs_used, 1)

            def sum_heads(j, src, out_ap):
                return mm(out_ap, heads(j), src, j == 0)

            for s in range(3):
                win_slab(s)
            pe.wait_ge(mix_loaded, 32)
            pe.wait_ge(lora_in, 1)
            pe.wait_ge(shifted, 1)
            for j in range(4):
                o = (j % 2) * 256
                mm(PS[:, 4 + j // 2, o:o + 256], LORA[0:64, 0, j * P:(j + 1) * P], LW[0:64, :], True)
            for j in range(4):
                o = (j % 2) * 256
                ins = mm(PS[:, 6 + j // 2, o:o + 256], LORA[64:128, 0, j * P:(j + 1) * P], U[64:128, 0, :], True)
            ins.then_inc(lora_done, 1)
            for s in range(3, 6):
                win_slab(s)
            pe.wait_ge(sigma_ready, 4)
            for j in range(4):
                ins = sum_heads(j, SQ[:, j, :], PS[0:16, 2, 0:256])
            ins.then_inc(head_sum, 1)
            win_slab(6)
            win_slab(7)
            pe.wait_ge(head_rn, 1)
            for j in range(4):
                o = (j % 2) * 256
                ins = mm(PS[:, 4 + j // 2, o:o + 256], spread(j), RN[:, 0, :], True)
            ins.then_inc(head_spread, 1)
            pe.wait_ge(lora_in, 2)
            for j in range(4):
                o = (j % 2) * 256
                ins = mm(PS[:, 6 + j // 2, o:o + 256], LORA[:, 1, j * P:(j + 1) * P], LG[:, :], True)
            ins.then_inc(lora_done, 1)
            win_slab(8)
            pe.wait_ge(feature, 2)
            for j in range(4):
                o = (j % 2) * 256
                ins = mm(PS[:, 4 + j // 2, o:o + 256], mixc("block"), RKR[:, j, :], True)
            ins.then_inc(head_spread, 1)
            win_slab(9)
            win_slab(10)
            for s in (11, 12):
                pe.wait_ge(lo_ready, S_WIN + s + 1)
                slot = slot_of(S_WIN + s)
                for k in range(4):
                    for t in range(TB):
                        a = 4 * (s - 11) + k
                        ins = three(PS[:, 2 + t, :], WHI[:, slot, k * 512:k * 512 + 512],
                                    WLO[:, slot, k * 512:k * 512 + 512], HHI[:, a, t * P:(t + 1) * P],
                                    HLO[:, a, t * P:(t + 1) * P], a == 0, swap=True)
                ins.then_inc(slabs_used, 1)

            def mod_sums(i):
                pe.wait_ge(sum_step, 2 * SUM_STEPS * (i + 1))
                for kind in range(2):
                    for c in range(2):
                        to = (2 * i + c) * 2 + kind
                        ins = mm(PS[:, 7, to:to + 1], MOD_SUM[kind][:, i % 2, c * P:(c + 1) * P], ones[:, 0:1], True)
                ins.then_inc(sums_read, 1)

            def mod_slabs(first, n):
                for i in range(first, first + n):
                    slot = (B_MOD + i) % RING
                    pe.wait_ge(stage_ready[slot], 16 * ((B_MOD + i) // RING + 1))
                    for c in range(2):
                        for k in range(KT):
                            a = k * 256 + c * P
                            ins = mm(PS[:, 7, (2 * i + c) * 2:(2 * i + c) * 2 + 2], stage[:, slot, a:a + P],
                                     SC[:, k, :], k == 0)
                    ins.then_inc(stage_free[slot], 1)

            pe.wait_ge(feature, 4)
            pe.wait_ge(u_copied, 11)

            def turn_feature(src, blk, bank):
                for j in range(4):
                    f = {"a": AR[:, 2 * j + blk, 0, :], "b": BH[:, j, blk * P:(blk + 1) * P],
                         "k": KH[:, j, blk * P:(blk + 1) * P], "v": U[:, 10 + j, blk * P:(blk + 1) * P]}[src]
                    ins = pe.transpose(PS[:, bank, j * P:(j + 1) * P], f, ident)
                ins.then_inc(tok_turned, 1)

            turn_feature("a", 0, 0)
            turn_feature("a", 1, 1)
            pe.wait_ge(sbv_ready, 1)
            for m in range(2):
                pe.wait_ge(qk_square, m + 1)
                for j in range(4):
                    ins = sum_heads(j, (SQ2 if m == 0 else OS)[:, j, :], PS[0:16, 2, m * 256:m * 256 + 256])
            ins.then_inc(head_sum, 1)
            for blk in range(TB):
                pe.wait_ge(tok_copied, blk + 1)
                turn_feature("b", blk, blk)

            pe.wait_ge(gate_copied, 1)
            for m in range(2):
                pe.wait_ge(head_rn, 2 + m)
                for j in range(4):
                    o = (j % 2) * 256
                    ins = mm(PS[:, 3 + 2 * m + j // 2, o:o + 256], spread(j), RN[:, m, :], True)
                ins.then_inc(head_spread, 1)
            pe.wait_ge(qk_ready, 2)
            pe.wait_ge(tok_copied, 4)

            def sb_scores(g):
                if g >= 2:
                    pe.wait_ge(e_masked, g - 1)
                for hh in range(2):
                    pb, bank = 64 * hh, 2 * (g % 2) + hh
                    q, k = U[pb:pb + 64, 14 + g, :], U[pb:pb + 64, 18 + g, :]
                    mm(PS[:, bank, 0:256], k[:, 0:128], q, True)
                    ins = mm(PS[:, bank, 256:384], k[:, 128:256], q[:, 128:256], False)
                ins.then_inc(z_ready, 1)

            def sb_sums(g):
                pe.wait_ge(l_ready, g + 1)
                for hh in range(2):
                    bank, at = 2 * (g % 2) + hh, 2 * (g % 2) + hh
                    mm(PS[:, bank, 0:256], mixc("suffix"), LT[:, at, 0:256], False)
                    mm(PS[:, bank, 128:256], mixc("minus"), LT[:, at, 256:384], False)
                    ins = mm(PS[:, bank, 256:384], mixc("suffix"), LT[:, at, 256:384], False)
                ins.then_inc(e_ready, 1)

            def sb_values(g):
                pe.wait_ge(att_ready, g + 1)
                for hh in range(2):
                    h, pb, at, o = 2 * g + hh, 64 * hh, 2 * (g % 2) + hh, (g % 2) * 256
                    mm(PS[pb:pb + 64, 4 + g // 2, o:o + 256], SBV[:, 0, h * 64:h * 64 + 64], LT[:, at, 0:256], True)
                    ins = mm(PS[pb:pb + 64, 4 + g // 2, o + 128:o + 256], SBV[:, 1, h * 64:h * 64 + 64],
                             LT[:, at, 256:384], False)
                ins.then_inc(o_ready, 1)

            sb_scores(0)
            sb_scores(1)
            for n in range(4):
                if n >= 2:
                    pe.wait_ge(tok_moved, n - 1)
                turn_feature("kkvv"[n], n % 2, 5 + n % 2)
            sb_sums(0)
            sb_sums(1)
            mod_sums(0)
            sb_values(0)
            sb_scores(2)
            sb_values(1)
            pe.wait_ge(tok_moved, 4)
            sb_scores(3)
            mod_sums(1)
            sb_sums(2)
            sb_sums(3)
            sb_values(2)
            sb_values(3)
            mod_sums(2)
            pe.wait_ge(o_copied, 2)
            for j in range(4):
                ins = sum_heads(j, SQ2[:, j, :], PS[0:16, 6, 0:256])
            ins.then_inc(head_sum, 1)
            pe.wait_ge(head_rn, 4)
            for j in range(4):
                o = (j % 2) * 256
                ins = mm(PS[:, 2 + j // 2, o:o + 256], spread(j), RN[:, 0, :], True)
            ins.then_inc(head_spread, 1)
            pe.wait_ge(cat_ready, 1)

            def unit_stage(n, lane, half):
                blk, g = half, lane
                b0, b1, b2 = 3 * lane, 3 * lane + 1, 3 * lane + 2
                t = T[lane]
                hs = unit_heads(g)
                first = 12 * half

                def four(bank, lhs, rhs, width=128):
                    for i in range(4):
                        ins = mm(PS[:, bank, i * width:(i + 1) * width], lhs(i), rhs(i), True)
                    return ins

                def wait(act=0, vec=0, part=0):
                    if act or half:
                        pe.wait_ge(u_act[lane], act + ACTS * half)
                    if vec or half:
                        pe.wait_ge(u_vec[lane], vec + VECS * half)
                    if part:
                        pe.wait_ge(u_part[lane], part + PARTS * half)

                def feat(ap, h):
                    pb = 64 * (h % 2)
                    return ap[pb:pb + 64, h // 2, blk * P:(blk + 1) * P]

                def a_r(h):
                    pb = 64 * (h % 2)
                    return AR[pb:pb + 64, 2 * (h // 2) + blk, :, :].rearrange("p c n -> p (c n)")

                if n == 1:
                    wait(0, 0)
                    for i in range(4):
                        o = (i % 2) * 256
                        mm(PS[:, b0 + i // 2, o:o + 256], feat(KH, hs[i]), a_r(hs[i]), True)
                    for i in range(4):
                        if i == 2 and lane:
                            pe.wait_ge(u_vec[0], VECS * half + 1)
                        o = (i % 2) * 128
                        to = PS[:, b2, o:o + 128] if i < 2 else PS[:, 6, 256 * lane + o:256 * lane + o + 128]
                        ins = mm(to, a_r(hs[i])[:, 0:128], feat(BH, hs[i]), True)
                elif n == 2:
                    wait(vec=2)
                    for i in range(4):
                        o = (i % 2) * 256
                        ins = mm(PS[:, b0 + i // 2, o:o + 256], feat(BH, hs[i]), a_r(hs[i]), True)
                elif n == 3:
                    wait(vec=3, part=2)
                    four(b0, lambda i: t[2][:, i, :], lambda i: t[1][:, i, :])
                    four(b1, lambda i: t[1][:, i, :], lambda i: t[2][:, i, :])
                    ins = four(b2, lambda i: NR[:, 8 * half + 4 * lane + i, 0:128],
                               lambda i: VTOK[:, blk, hs[i] * 64:hs[i] * 64 + 64], 64)
                elif n == 4:
                    wait(act=2, vec=4, part=3)
                    four(b0, lambda i: t[4][:, i, :], lambda i: t[5][:, i, :])
                    four(b1, lambda i: t[4][:, i, :], lambda i: t[3][:, i, :])
                    ins = four(b2, lambda i: t[3][:, i, :], lambda i: t[4][:, i, :])
                elif n == 5:
                    wait(act=4, vec=5)
                    four(b0, lambda i: t[2][:, i, :], lambda i: t[6][:, i, :])
                    ins = four(b1, lambda i: t[1][:, i, :], lambda i: t[2][:, i, :])
                elif n == 6:
                    wait(act=5, vec=6)
                    ins = four(b2, lambda i: t[3][:, i, :], lambda i: t[5][:, i, :])
                elif n in (7, 9):
                    src, low = (t[6], t[4]) if n == 7 else (t[5], t[0])
                    wait(vec=7 if n == 7 else 9, part=5)
                    for i in range(4):
                        pe.transpose(PS[:, b0, i * P:(i + 1) * P], src[:, i, :], ident)
                    ins = four(b1, lambda i: low[:, i, :], lambda i: src[:, i, :])
                elif n in (8, 10):
                    wait(act=6 if n == 8 else 7, vec=8 if n == 8 else 10)
                    ins = four(b2, lambda i: t[1][:, i, :], lambda i: t[2][:, i, :])
                elif n == 11:
                    wait(vec=11)
                    ins = four(b0, lambda i: t[6][:, i, :], lambda i: ANV[:, blk, hs[i], :])
                else:
                    wait(act=8)
                    for i in range(4):
                        h = hs[i]
                        pb, o = 64 * (h % 2), (h // 2 - 2 * g) * 128
                        mm(PS[pb:pb + 64, b1, o:o + 128], AU[:, blk, h, 0:64],
                           MB[:, 8 * half + 4 * lane + i, 128:256], True)
                    c = 1 if blk == 0 else 2
                    rs = 64 * (c % 2)
                    for i in range(4):
                        h = hs[i]
                        pb, o = 64 * (h % 2), (h // 2 - 2 * g) * 64
                        ins = mm(PS[pb:pb + 64, b2, o:o + 64], AU[rs:rs + 64, blk, h, 0:64],
                                 BTOK[rs:rs + 64, blk, h * 64:h * 64 + 64], True)
                ins.then_inc(u_pe[lane], 1)

            for half in range(2):
                for n in range(1, 13):
                    for lane in range(2):
                        unit_stage(n, lane, half)
                    if half == 0 and n in MOD_STAGES:
                        mod_sums(MOD_STAGES[n])

            for lane in range(2):
                pe.wait_ge(u_act[lane], 2 * ACTS)
                pe.wait_ge(u_vec[lane], 2 * VECS)
            for c in range(3):
                blk, rs = c // 2, 64 * (c % 2)
                if c:
                    mod_slabs(5 + c, 1)
                    pe.wait_ge(s_ready, c)
                for h in range(8):
                    pb, j = 64 * (h % 2), h // 2
                    o = PS[pb:pb + 64, 3, j * 64:j * 64 + 64]
                    ch = slice(h * 64, h * 64 + 64)
                    mm(o, BTOK[rs:rs + 64, blk, ch], AU[rs:rs + 64, blk, h, 64:128], True)
                    ins = mm(o, KTOK[rs:rs + 64, blk, ch], VTOK[rs:rs + 64, blk, ch], False)
                    if c:
                        ins = mm(PS[pb:pb + 64, 0, j * 64:j * 64 + 64], ET[pb:pb + 64, c - 1, j, :],
                                 ST[pb:pb + 64, c - 1, j, :], True)
                ins.then_inc(s_products, 1)
            mod_slabs(8, 1)
            mm(PS[0:16, 7, 64:66], heads(0), SC[:, 0, :], True).then_inc(mod_done, 1)
            pe.wait_ge(s_ready, 3)
            for h in range(8):
                pb, j = 64 * (h % 2), h // 2
                g, i = h // 4, unit_heads(h // 4).index(h)
                for blk in range(TB):
                    o = (j % 2) * 256 + blk * P
                    at = 8 * blk + 4 * g + i
                    mm(PS[pb:pb + 64, 4 + j // 2, o:o + P], VTOK[:, blk, h * 64:h * 64 + 64], NR[:, at, 128:256], True)
                    ins = mm(PS[pb:pb + 64, 4 + j // 2, o:o + P], AU[:, blk, h, 64:128], MB[:, at, 128:256], False)
                    for c in (1,) if blk == 0 else (2, 3):
                        q = (c % 2) * 64
                        ins = mm(PS[pb:pb + 64, 4 + j // 2, o + q:o + q + 64], ST[pb:pb + 64, c - 1, j, :],
                                 RT[pb:pb + 64, j, blk * P + q:blk * P + q + 64], False)
            ins.then_inc(y_products, 1)
            pe.wait_ge(y_step, 1)
            for j in range(4):
                ins = mm(PS[:, j // 2, (j % 2) * 256:(j % 2) * 256 + 256], mixc("mean"), YS[:, j, :], True)
            ins.then_inc(y_products, 1)
            pe.wait_ge(y_step, 3)
            for j in range(4):
                ins = sum_heads(j, YQ[:, j, :], PS[0:16, 2, 0:256])
            ins.then_inc(head_sum, 1)
            pe.wait_ge(head_rn, 5)
            for j in range(4):
                ins = mm(PS[:, 4 + j // 2, (j % 2) * 256:(j % 2) * 256 + 256], spread(j), RN[:, 0, :], True)
            ins.then_inc(head_spread, 1)

            def out_products(s0, hi, lo, parts):
                for i in range(4):
                    if i % 2 == 0:
                        pe.wait_ge(parts, i // 2 + 1)
                    pe.wait_ge(lo_ready, s0 + i + 1)
                    slot = slot_of(s0 + i)
                    for t in range(TB):
                        for kk in range(2):
                            k = 2 * i + kk
                            for n in range(2):
                                a = kk * D + n * HALF
                                ins = three(PS[:, 2 * t + n, :], WHI[:, slot, a:a + HALF], WLO[:, slot, a:a + HALF],
                                            hi[:, k, t * P:(t + 1) * P], lo[:, k, t * P:(t + 1) * P], k == 0, swap=True)
                        if i == 3 and t == 0:
                            ins.then_inc(block_done, 1)
                    ins.then_inc(slabs_used, 1)

            out_products(S_OUT1, HHI, HLO, cat_lo)

            for r in range(4):
                pe.wait_ge(gate_diag, r + 1)
                if r >= 2:
                    pe.wait_ge(gate_row_copied, r - 1)
                mm(PS[:, 6 + r % 2, :], ones, DG[:, r % 2, :, :].rearrange("p a n -> p (a n)"), True)\
                    .then_inc(gate_rows, 1)
            pe.wait_ge(ctx_lo, 1)
            pe.wait_ge(lo_ready, S_CTX + 1)
            for c in range(2):
                ins = columns(slot_of(S_CTX), c, PS[:, 4, c * 256:c * 256 + 256], CHI, CLO)
            ins.then_inc(slabs_used, 1)

            def values(s, bank, hi, lo):
                pe.wait_ge(lo_ready, s + 1)
                slot = slot_of(s)
                for t in range(TB):
                    for k in range(KT):
                        ins = three(PS[:, bank, t * 256:t * 256 + 256], WHI[:, slot, k * 256:k * 256 + 256],
                                    WLO[:, slot, k * 256:k * 256 + 256], hi[:, k, t * P:(t + 1) * P],
                                    lo[:, k, t * P:(t + 1) * P], k == 0, swap=True)
                ins.then_inc(slabs_used, 1)

            values(S_CTX + 1, 5, CHI, CLO)

            pe.wait_ge(xs_ready, 6)
            pe.wait_ge(ctx_copied, 3)
            pe.wait_ge(gate_row_copied, 4)
            turn_x(XS)
            ffn_products(1, 2, S_FFN2)

            pe.wait_ge(x_new, 12)
            turn_x(X)
            pe.wait_ge(h_lo, 8)
            pe.wait_ge(att_loaded, 48)

            def win2_slab(s, turn, bank=None):
                pe.wait_ge(lo_ready, S_WIN2 + s + 1)
                if turn >= 2:
                    pe.wait_ge(p_copied, turn - 1)
                bank = turn % 2 if bank is None else bank
                for c in range(2):
                    ins = columns(slot_of(S_WIN2 + s), c, PS[:, bank, c * 256:c * 256 + 256], HHI, HLO)
                ins.then_inc(slabs_used, 1)

            def rotate(bank, tiles):
                for n, tile in enumerate(tiles):
                    o = (n % 2) * 256
                    ins = mm(PS[:, bank + n // 2, o:o + 256], CT[:, 512:640], tile, True)
                ins.then_inc(rotated, 1)

            win2_slab(0, 0)
            values(S_WIN2 + 1, 2, HHI, HLO)
            win2_slab(2, 1)
            pe.wait_ge(k_square, 1)
            mm(PS[0:16, 3, :], heads(0), TR[:, 0:2, :].rearrange("p a n -> p (a n)"), True).then_inc(head_sum, 1)
            win2_slab(3, 2)
            win2_slab(4, 3)
            pe.wait_ge(head_rn, 6)
            mm(PS[:, 4, :], spread(0), RA[:, 0:512], True).then_inc(head_spread, 1)
            pe.wait_ge(p_copied, 3)
            rotate(5, [QR[:, 2 + j, :] for j in range(4)])
            win2_slab(5, 4)
            pe.wait_ge(rope_in, 1)
            rotate(3, [QR[:, 0, :], KALL[:, 1, 0:256]])
            win2_slab(6, 5)
            pe.wait_ge(k_square, 2)
            pe.wait_ge(roped, 3)
            for j in range(4):
                ins = mm(PS[0:16, 3, 0:256], heads(j), TR[:, j, :], j == 0)
            ins.then_inc(head_sum, 1)
            win2_slab(7, 6)
            win2_slab(8, 7)
            pe.wait_ge(head_rn, 7)
            pe.wait_ge(roped, 1)
            for j in range(4):
                o = (j % 2) * 256
                ins = mm(PS[:, 5 + j // 2, o:o + 256], spread(j), RA[:, 0:256], True)
            ins.then_inc(head_spread, 1)
            win2_slab(9, 8)
            pe.wait_ge(rope_in, 2)
            rotate(3, [QR[:, 6 + j, :] for j in range(4)])
            for s in range(10, 13):
                win2_slab(s, s - 1)

            pe.wait_ge(roped, 4)
            pe.wait_ge(v_copied, 1)
            pe.wait_ge(p_copied, 12)

            def score(i):
                br, t, j = i // 8, (i // 4) % 2, i % 4
                if i >= 2:
                    pe.wait_ge(p_ready, 2 * (i - 1))
                for par in range(2):
                    pb = 64 * par
                    ins = mm(PS[:, 2 * (i % 2) + par, :], QN[pb:pb + 64, 4 * br + j, t * P:(t + 1) * P],
                             KALL[pb:pb + 64, br, :], True)
                ins.then_inc(scored, 1)

            def turn_p(i):
                for par, copied in enumerate((pt_act, pt_vec)):
                    pe.wait_ge(p_ready, 2 * i + par + 1)
                    if i:
                        pe.wait_ge(copied, i)
                    for k in range(4):
                        ins = pe.transpose(PS[:, 4 + par, k * P:(k + 1) * P], PM[:, i % 2, par, k * P:(k + 1) * P], ident)
                    ins.then_inc(p_turned, 1)

            def weigh(i):
                br, t, j = i // 8, (i // 4) % 2, i % 4
                if j == 0 and i >= 8:
                    pe.wait_ge(o_scaled, i // 4 - 1)
                for par, copied in enumerate((pt_act, pt_vec)):
                    pe.wait_ge(copied, i + 1)
                    o = j * 128 + par * 64
                    for k in range(4):
                        ins = mm(PS[:, 6 + t, o:o + 64], PT[:, i % 2, par, k * P:(k + 1) * P],
                                 VALL[:, k, br * 128 + par * 64:br * 128 + par * 64 + 64], k == 0)
                ins.then_inc(pv_done, 1)

            for i in range(18):
                if i < 16:
                    score(i)
                if i == 1:
                    win2_slab(13, 12, bank=6)
                if 1 <= i < 17:
                    turn_p(i - 1)
                if i == 2:
                    pe.wait_ge(p_copied, 13)
                if i >= 2:
                    weigh(i - 2)
            pe.wait_ge(o_scaled, 4)
            turn_x(OT)
            for half in range(2):
                for br in range(2):
                    s = S_BRANCH + 2 * half + br
                    pe.wait_ge(h_lo, 10)
                    pe.wait_ge(lo_ready, s + 1)
                    slot = slot_of(s)
                    for c in range(4):
                        o = (c % 2) * 256
                        for k in range(4):
                            a = k * 512 + c * P
                            ins = three(PS[:, 4 * half + 2 * br + c // 2, o:o + 256], WHI[:, slot, a:a + P],
                                        WLO[:, slot, a:a + P], HHI[:, 4 * br + k, :], HLO[:, 4 * br + k, :], k == 0)
                    ins.then_inc(slabs_used, 1)
            out_products(S_OUT2, MHI, MLO, m_lo)

            pe.wait_ge(ln_normed, 4)
            turn_x(X)
            ffn_products(2, 5, S_FFN3)

        @block.scalar
        def _(act):
            n_step = [0]

            def step(ins):
                n_step[0] += 1
                ins.then_inc(act_step, 1)

            def own():
                act.wait_ge(act_step, n_step[0])

            def high(base, p=0):
                slot = slot_of(base)
                act.wait_ge(stage_ready[slot], p * 16 + 16 * ((base + shift(base)) // RING + 1))
                if not (isinstance(p, int) and base + 3 * p < RING):
                    act.wait_ge(slabs_used, p * 3 + (base - RING + 1))
                act.activation(WHI[:, slot, :], stage[:, slot, :], ACT.Copy).then_inc(hi_ready, 1)

            def norm_sums(n, ready):
                for t in range(TB):
                    ready(t)
                    step(act.activation(XS[:, t, :], X[:, t, :], ACT.Square, accum_out=SM[:, t:t + 1]))
                own()
                act.activation(SM[:, 2:4], SM[:, 0:2], ACT.Sqrt, scale=1.0 / D, bias=EPS[:, 0:1]).then_inc(root, 1)

            def h_high(turn):
                for half in range(2):
                    act.wait_ge(h_full, 4 * turn + 2 * half + 2)
                    act.activation(HHI[:, 4 * half:4 * half + 4, :], HF[:, 4 * half:4 * half + 4, :], ACT.Copy)\
                       .then_inc(h_hi, 1)

            def ffn_act(q, b, tail):
                def pair(p, par, i, first=False, ahead=2):
                    k = i * 2 if i is not None else 0
                    six = 2 * i if i is not None else 0
                    if not first:
                        high(b + 3 * par + 2, six)
                    act.wait_ge(slabs_used, six * 3 + (b + 3 * par + (2 if first else 1)))
                    act.wait_ge(hidden_done, LEAD + k + max(PAIRS * q + par - 1, 0))
                    bank = 4 + 2 * (par % 2)
                    if q < 2:
                        act.activation(SG[:, par % 2, :, :], PS[:, bank:bank + 2, 0:256], ACT.Silu)\
                           .then_inc(silu_done, 1)
                    else:
                        act.wait_ge(taps_ready, k + (par + 1))
                        for a in range(4):
                            src = PS[:, bank + a % 2, (a // 2) * 256:(a // 2) * 256 + 256]
                            ins = act.activation(CG[:, par % 2, a, :], src, ACT.Identity,
                                                 scale=CW[:, par % 2, 4 * a + 1:4 * a + 2],
                                                 bias=CW[:, par % 2, 4 * a + 3:4 * a + 4])
                        ins.then_inc(center, 1)
                    if ahead:
                        high(b + 3 * par + 3, six)
                    if q == 2:
                        act.wait_ge(conv_done, k + (par + 1))
                        act.activation(SG[:, par % 2, :, :], CG[:, par % 2, 0:2, :], ACT.Silu).then_inc(silu_done, 1)
                    act.wait_ge(hidden_done, LEAD + k + (PAIRS * q + par + 1))
                    if not first:
                        act.wait_ge(slabs_used, six * 3 + (b + 3 * par - 1))
                    act.activation(DHI[:, par % 2, :, :], HID[:, par % 2, :, :], ACT.Copy).then_inc(hid_hi, 1)
                    if ahead:
                        high(b + 3 * par + 4, six)

                pair(0, 0, None, first=True)
                loops = PAIRS // 2 - (0 if tail else 1)
                with act.Fori(0, loops) as i:
                    for par in range(1, 3):
                        pair(None, par, i)
                if not tail:
                    pair(None, PAIRS - 2, None)
                    pair(None, PAIRS - 1, None, ahead=0)

            act.wait_ge(eps_ready, 1)
            norm_sums(0, lambda t: act.wait_ge(x_loaded[t], 16))
            high(0)
            act.wait_ge(vec_loaded, 32)
            act.activation(SC[:, :, :].rearrange("p k n -> p (k n)"), VEC[:, V["c"]:V["c"] + 16], ACT.Silu)\
               .then_inc(hid_hi, LEAD)
            h_high(0)
            high(1)
            high(2)
            ffn_act(0, S_FFN1, True)

            norm_sums(1, lambda t: act.wait_ge(x_new, 2 * t + 2))
            act.wait_ge(mod_done, 1)
            act.activation(MODV[:, MOD_TILES:48, 0], PS[:, 7, 0:2 * N_SIDE], ACT.Copy).then_inc(mod_copied, 1)
            h_high(1)
            high(S_WIN + 2)

            def copy_u(s):
                act.wait_ge(slabs_used, S_WIN + s + 1)
                act.activation(U[:, 2 * s:2 * s + 2, :].rearrange("p a n -> p (a n)"), PS[:, s % 2, :], ACT.Copy)\
                   .then_inc(u_copied, 1)

            for s in range(11):
                copy_u(s)
                if s + 3 < 13:
                    high(S_WIN + s + 3)
                if s == 1:
                    act.wait_ge(shifted, 1)
                    act.activation(LW[0:64, :], U[0:64, 0, :], ACT.Tanh).then_inc(lora_in, 1)
                    act.activation(LG[:, :], U[:, 1, :], ACT.Sigmoid).then_inc(lora_in, 1)
                if s == 3:
                    act.wait_ge(lora_done, 1)
                    for n, (to, name) in enumerate(((EA, "w0"), (AA, "a0"))):
                        for j in range(4):
                            o = (j % 2) * 256
                            ins = act.activation(to[:, j, :], PS[:, 4 + 2 * n + j // 2, o:o + 256], ACT.Sigmoid,
                                                 bias=vcol(name, j))
                        ins.then_inc(sigma_ready, 1)
                    act.wait_ge(shifted, 3)
                    for j in range(4):
                        ins = act.activation(KK[:, j, :], U[:, 2 + j, :], ACT.Copy, scale=vcol("kk", j))
                    ins.then_inc(sigma_ready, 1)
                    act.wait_ge(sigma_ready, 3)
                    act.activation(SQ[:, :, :], KK[:, :, :], ACT.Square).then_inc(sigma_ready, 1)
                if s == 6:
                    act.wait_ge(head_sum, 1)
                    act.activation(RN[:, 0, :], PS[0:16, 2, 0:256], ACT.Sqrt).then_inc(head_root, 1)
                    act.wait_ge(decay_ready, 1)
                    act.activation(EI[:, :, :], ER[:, :, :], ACT.Exp, scale=DECAY_SCALE).then_inc(exp_ready, 1)
                    act.activation(EA[:, :, :], EA[:, :, :], ACT.Exp, scale=-DECAY_SCALE).then_inc(exp_ready, 1)
                    act.activation(ER[:, :, :], ER[:, :, :], ACT.Exp, scale=-DECAY_SCALE).then_inc(exp_ready, 1)
                if s == 9:
                    act.wait_ge(feature, 2)
                    act.wait_ge(lora_done, 2)
                    act.activation(U[:, 6:10, :].rearrange("p a n -> p (a n)"),
                                   PS[:, 6:8, :].rearrange("p a n -> p (a n)"), ACT.Copy).then_inc(gate_copied, 1)
            act.wait_ge(feature, 4)
            act.wait_ge(u_copied, 11)
            act.activation(SQ2[:, :, :], U[:, 14:18, :], ACT.Square).then_inc(qk_square, 1)
            act.activation(OS[:, :, :], U[:, 18:22, :], ACT.Square).then_inc(qk_square, 1)
            act.wait_ge(slabs_used, S_WIN + N_WIN)
            act.activation(SBV[:, :, :], PS[:, 2:4, :], ACT.Copy).then_inc(sbv_ready, 1)
            for n in range(4):
                blk = n % 2
                act.wait_ge(tok_turned, n + 1)
                to = [ANV[:, blk, :, 0:64], BTOK[:, blk, :]][n // 2]
                src = PS[:, n % 2, :]
                if n < 2:
                    src = src.rearrange("p (h c) -> p h c", h=8)
                act.activation(to, src, ACT.Copy).then_inc(tok_copied, 1)
                if n == 1:
                    act.wait_ge(head_sum, 2)
                    step(act.activation(RN[:, 0, :], PS[0:16, 2, 0:256], ACT.Sqrt, bias=EPS[0:16, 3:4]))
                    act.activation(RN[:, 1, :], PS[0:16, 2, 256:512], ACT.Sqrt, scale=1.0 / HEAD, bias=EPS[0:16, 0:1])\
                       .then_inc(head_root, 1)

            def softplus_tail(g):
                z = ZT[:, 2 * (g % 2):2 * (g % 2) + 2, :]
                act.wait_ge(z_ready, g + 1)
                if g >= 2:
                    act.wait_ge(att_ready, g - 1)
                step(act.activation(z, PS[:, 2 * (g % 2):2 * (g % 2) + 2, 0:384], ACT.Abs))
                own()
                step(act.activation(z, z, ACT.Exp, scale=-1.0))
                own()
                act.activation(z, z, ACT.Ln, bias=ones[:, 0:1]).then_inc(ln_ready, 1)

            def weights(g):
                act.wait_ge(e_masked, g + 1)
                part = slice(2 * (g % 2), 2 * (g % 2) + 2)
                act.activation(LT[:, part, :], ZT[:, part, :], ACT.Exp).then_inc(att_ready, 1)

            def outputs(n):
                act.wait_ge(o_ready, 2 * n + 2)
                if n == 0:
                    act.wait_ge(head_rn, 2)
                step(act.activation(OS[:, 2 * n:2 * n + 2, :].rearrange("p a n -> p (a n)"), PS[:, 4 + n, :], ACT.Copy))
                own()
                act.activation(SQ2[:, 2 * n:2 * n + 2, :], OS[:, 2 * n:2 * n + 2, :], ACT.Square).then_inc(o_copied, 1)

            softplus_tail(0)
            softplus_tail(1)
            weights(0)
            weights(1)
            softplus_tail(2)
            softplus_tail(3)
            outputs(0)
            weights(2)
            weights(3)
            outputs(1)
            act.wait_ge(head_sum, 3)
            act.activation(RN[:, 0, :], PS[0:16, 6, 0:256], ACT.Sqrt, scale=1.0 / HEAD, bias=EPS[0:16, 0:1])\
               .then_inc(head_root, 1)

            def copies(n, lane, half):
                b0, b1, b2 = 3 * lane, 3 * lane + 1, 3 * lane + 2
                t, blk, g = T[lane], half, lane
                todo = {3: [(t[3], b0), ("nv", b2)], 4: [(t[1], b1), (t[2], b2)], 5: [(t[3], b1)],
                        7: [(t[1], b0)], 9: [(t[1], b0)], 11: [("au", b0)], 12: [("et", b2)]}.get(n, [])
                if todo:
                    act.wait_ge(u_pe[lane], 12 * half + n)
                for to, bank in todo:
                    if to == "nv":
                        for par in range(2):
                            src = PS[:, bank, par * 128:par * 128 + 128].rearrange("p (a n) -> p a n", a=2)
                            ins = act.activation(ANV[:, blk, 4 * g + par:4 * g + par + 3:2, 64:128], src, ACT.Copy)
                        ins.then_inc(u_act[lane], 1)
                    elif to == "au":
                        for par in range(2):
                            src = PS[:, bank, par * 256:par * 256 + 256].rearrange("p (a n) -> p a n", a=2)
                            ins = act.activation(AU[:, blk, 4 * g + par:4 * g + par + 3:2, :], src, ACT.Copy)
                        ins.then_inc(u_act[lane], 1)
                    elif to == "et":
                        act.activation(ET[:, blk, 2 * g:2 * g + 2, :],
                                       PS[:, bank, 0:128].rearrange("p (a n) -> p a n", a=2), ACT.Copy)\
                           .then_inc(u_act[lane], 1)
                    else:
                        act.activation(to[:, :, :], PS[:, bank, :].rearrange("p (a n) -> p a n", a=4), ACT.Copy)\
                           .then_inc(u_act[lane], 1)

            for half in range(2):
                for n in range(1, 13):
                    if half == 0 and n == 11:
                        act.wait_ge(sum_step, 2 * SUM_STEPS * N_RING_POOL)
                    for lane in range(2):
                        copies(n, lane, half)

            act.wait_ge(y_products, 1)
            act.activation(YS[:, :, :].rearrange("p a n -> p (a n)"), PS[:, 4:6, :].rearrange("p a n -> p (a n)"),
                           ACT.Copy).then_inc(y_step, 1)
            act.wait_ge(y_step, 2)
            act.activation(YQ[:, :, :], YC[:, :, :], ACT.Square).then_inc(y_step, 1)
            act.activation(HHI[:, 0:4, :], HF[:, 0:4, :], ACT.Copy).then_inc(cat_hi, 1)
            act.wait_ge(head_sum, 4)
            act.activation(RN[:, 0, :], PS[0:16, 2, 0:256], ACT.Sqrt, scale=1.0 / HEAD, bias=EPS[0:16, 2:3])\
               .then_inc(head_root, 1)
            for s in range(3):
                high(S_OUT1 + s)
            act.wait_ge(cat_ready, 2)
            act.activation(HHI[:, 4:8, :], HF[:, 4:8, :], ACT.Copy).then_inc(cat_hi, 1)
            high(S_OUT1 + 3)

            act.dma_start(CX[:, :, :], ctx_t).then_inc(att_loaded, 16)
            act.dma_start(CT[:, :], c_att).then_inc(att_loaded, 16)
            act.dma_start(ROWS[:, :], rows[0:1, 4 * D:N_ROW].broadcast_to([P, 264])).then_inc(att_loaded, 16)
            act.dma_start(ROW[:, :], rows[0:1, 0:2 * D].broadcast_to([P, 2 * D])).then_inc(row_loaded, 16)
            for half in range(2):
                part = slice(4 * half, 4 * half + 4)
                act.wait_ge(ctx_full, half + 1)
                act.activation(CHI[:, part, :], CX[:, part, :], ACT.Copy).then_inc(ctx_hi, 1)
            high(S_CTX)
            for r in range(4):
                act.wait_ge(gate_rows, r + 1)
                act.activation(GB[:, r // 2, (r % 2) * HALF:(r % 2) * HALF + HALF], PS[:, 6 + r % 2, :], ACT.Copy)\
                   .then_inc(gate_row_copied, 1)
            high(S_CTX + 1)
            norm_sums(2, lambda t: act.wait_ge(x_new, 4 + 2 * t + 2))
            high(S_FFN2)
            high(S_FFN2 + 1)
            h_high(2)
            high(S_FFN2 + 2)
            ffn_act(1, S_FFN2, True)

            high(S_WIN2 + 2)
            h_high(3)

            def out_of(turn, s, to, tile, func=ACT.Identity):
                act.wait_ge(slabs_used, S_WIN2 + s + 1)
                bank = 6 if s == 13 else turn % 2
                for a in range(2):
                    ins = act.activation(to[a], PS[:, bank, a * 256:a * 256 + 256], func, bias=vcol("b2", tile + a))
                ins.then_inc(p_copied, 1)

            def win2_out(s):
                turn = s if s == 0 else s - 1
                if s == 0:
                    out_of(0, 0, (QR[:, 0, :], KALL[:, 1, 0:256]), 0)
                elif s < 6:
                    out_of(turn, s, (QR[:, 2 * s - 2, :], QR[:, 2 * s - 1, :]), 2 * s - 2)
                elif s < 14:
                    out_of(turn, s, (GT[:, 2 * s - 12, :], GT[:, 2 * s - 11, :]), 2 * s - 2, ACT.Sigmoid)

            win2_out(0)
            high(S_WIN2 + 3)
            act.wait_ge(p_copied, 1)
            act.activation(TR[:, 0:2, :].rearrange("p a n -> p (a n)"), KALL[:, 1, :], ACT.Square).then_inc(k_square, 1)
            high(S_WIN2 + 4)
            win2_out(2)
            high(S_WIN2 + 5)
            act.wait_ge(head_sum, 5)
            act.activation(RA[:, 0:512], PS[0:16, 3, :], ACT.Sqrt, scale=1.0 / HEAD, bias=EPS[0:16, 0:1])\
               .then_inc(head_root, 1)
            win2_out(3)
            high(S_WIN2 + 6)
            win2_out(4)
            high(S_WIN2 + 7)
            win2_out(5)
            high(S_WIN2 + 8)
            act.wait_ge(roped, 1)
            act.wait_ge(p_copied, 5)
            act.activation(TR[:, :, :], QR[:, 6:10, :], ACT.Square).then_inc(k_square, 1)
            act.wait_ge(head_sum, 6)
            act.activation(RA[:, 0:256], PS[0:16, 3, 0:256], ACT.Sqrt, scale=1.0 / HEAD, bias=EPS[0:16, 0:1])\
               .then_inc(head_root, 1)
            for s in range(6, 13):
                win2_out(s)
                high(S_WIN2 + s + 3)

            def exps(i):
                act.wait_ge(max_done, i + 1)
                if i >= 2:
                    act.wait_ge(p_turned, 2 * i - 2)
                for par in range(2):
                    at = 2 * i + par
                    act.activation(PM[:, i % 2, par, :], PS[:, 2 * (i % 2) + par, :], ACT.Exp, scale=SCALE,
                                   bias=SM[:, 32 + at:33 + at], accum_out=SM[:, 64 + at:65 + at]).then_inc(p_ready, 1)

            def copy_pt(i):
                act.wait_ge(p_turned, 2 * i + 1)
                if i >= 2:
                    act.wait_ge(pv_done, i - 1)
                act.activation(PT[:, i % 2, 0, :], PS[:, 4, :], ACT.Copy).then_inc(pt_act, 1)

            for i in range(17):
                if i >= 1:
                    copy_pt(i - 1)
                if i < 16:
                    exps(i)
                if i == 1:
                    win2_out(13)
                    high(S_BRANCH + 2)
                if i == 8:
                    act.wait_ge(sink_in, 1)
                    act.activation(SM[:, 96:112], SM[:, 96:112], ACT.Exp).then_inc(sink_exp, 1)
            h_high(4)
            for half in range(2):
                act.wait_ge(merged, half + 1)
                part = slice(4 * half, 4 * half + 4)
                act.activation(MHI[:, part, :], MF[:, part, :], ACT.Copy).then_inc(m_hi, 1)
                high(S_BRANCH + 3 + 2 * half)
                high(S_BRANCH + 4 + 2 * half)
            high(S_OUT2 + 3)
            high(S_FFN3)

            def ln_act(n):
                for t in range(TB):
                    act.wait_ge(ln_var, 2 * n + t + 1)
                    act.activation(SM[:, 16 + 4 * t + 2:16 + 4 * t + 3], SM[:, 16 + 4 * t + 1:16 + 4 * t + 2], ACT.Sqrt,
                                   bias=EPS[:, 1:2]).then_inc(ln_root, 1)
                for t in range(TB):
                    act.wait_ge(ln_scale, 2 * n + t + 1)
                    for h in range(2):
                        part = X[:, t, h * HALF:(h + 1) * HALF]
                        act.activation(part, part, ACT.Identity, scale=SM[:, 19 + 4 * t:20 + 4 * t],
                                       bias=SM[:, 24 + t:25 + t]).then_inc(ln_normed, 1)

            high(S_FFN3 + 1)
            ln_act(0)
            h_high(5)
            high(S_FFN3 + 2)
            act.wait_ge(x_new, 16)
            act.dma_start(ROW[:, :], rows[0:1, 2 * D:4 * D].broadcast_to([P, 2 * D])).then_inc(row_loaded, 16)
            ffn_act(2, S_FFN3, False)
            ln_act(1)

        @block.vector
        def _(vec):
            n_step = [0]

            def step(ins):
                n_step[0] += 1
                ins.then_inc(vec_step, 1)

            def own():
                vec.wait_ge(vec_step, n_step[0])

            def low(base, p=0):
                slot = slot_of(base)
                vec.wait_ge(hi_ready, p * 3 + (base + 1))
                vec.tensor_tensor(WLO[:, slot, :], stage[:, slot, :], WHI[:, slot, :].bitcast(F32), ALU.subtract)\
                   .then_inc(lo_ready, 1)
                vec.wait_ge(lo_ready, p * 3 + (base + 1))
                vec.sem_inc(stage_free[slot], 1)

            def norm_scale(n):
                vec.wait_ge(root, n + 1)
                step(vec.reciprocal(SM[:, 4:6], SM[:, 2:4]))
                own()
                for t in range(TB):
                    vec.tensor_scalar(XS[:, t, :], X[:, t, :], SM[:, 4 + t:5 + t], None, ALU.mult)\
                       .then_inc(xs_ready, 1)

            def h_scale(turn, mul, add=None):
                for n in range(4):
                    vec.wait_ge(x_turned, 4 * turn + n + 1)
                    for k in (2 * n, 2 * n + 1):
                        ins = vec.tensor_scalar(HF[:, k, :], PS[:, 4 + n, (k % 2) * 256:(k % 2) * 256 + 256], mul(k),
                                                add(k) if add else None, ALU.mult, ALU.add if add else ALU.bypass)
                    ins.then_inc(h_full, 1)
                for half in range(2):
                    vec.wait_ge(h_hi, 2 * turn + half + 1)
                    part = slice(4 * half, 4 * half + 4)
                    vec.tensor_tensor(HLO[:, part, :], HF[:, part, :], HHI[:, part, :].bitcast(F32), ALU.subtract)\
                       .then_inc(h_lo, 1)

            def add_half(n, s, half=0.5):
                for t in range(TB):
                    if t == 0:
                        vec.wait_ge(block_done, n)
                    else:
                        vec.wait_ge(slabs_used, s)
                    for n in range(2):
                        part = X[:, t, n * HALF:(n + 1) * HALF]
                        vec.scalar_tensor_tensor(part, PS[:, 2 * t + n, :], half, part, ALU.mult, ALU.add)\
                           .then_inc(x_new, 1)

            def ffn_vec(q, b, tail):
                def pair(par, i, first=False, ahead=2):
                    k = i * 2 if i is not None else 0
                    if not first:
                        low(b + 3 * par + 2, k)
                    if q == 2:
                        vec.wait_ge(center, k + (par + 1))
                        bank = 4 + 2 * (par % 2)
                        for m in range(2):
                            if m:
                                vec.wait_ge(tap_before, k + (par + 1))
                            for a in range(4):
                                src = PS[:, bank + a % 2, (a // 2) * 256:(a // 2) * 256 + 256]
                                c = CG[:, par % 2, a, :]
                                src, c = (src[:, 1:256], c[:, 0:255]) if m else (src[:, 0:255], c[:, 1:256])
                                ins = vec.scalar_tensor_tensor(c, src, CW[:, par % 2, 4 * a + 2 * m:4 * a + 2 * m + 1],
                                                               c, ALU.mult, ALU.add)
                            ins.then_inc(conv_done if m else tap_before, 1)
                        if ahead:
                            low(b + 3 * par + 3, k)
                    vec.wait_ge(silu_done, k + (PAIRS * q + par + 1))
                    vec.wait_ge(hid_hi, LEAD + k + max(PAIRS * q + par - 1, 0))
                    bank = 4 + 2 * (par % 2)
                    up = PS[:, bank:bank + 2, 256:512] if q < 2 else CG[:, par % 2, 2:4, :]
                    vec.tensor_tensor(HID[:, par % 2, :, :], SG[:, par % 2, :, :], up, ALU.mult).then_inc(hidden_done, 1)
                    if ahead and q < 2:
                        low(b + 3 * par + 3, k)
                    vec.wait_ge(hid_hi, LEAD + k + (PAIRS * q + par + 1))
                    vec.tensor_tensor(DLO[:, par % 2, :, :], HID[:, par % 2, :, :],
                                      DHI[:, par % 2, :, :].bitcast(F32), ALU.subtract).then_inc(hid_lo, 1)
                    if ahead:
                        low(b + 3 * par + 4, k)

                pair(0, None, first=True)
                with vec.Fori(0, PAIRS // 2 - (0 if tail else 1)) as i:
                    for par in range(1, 3):
                        pair(par, i)
                if not tail:
                    pair(PAIRS - 2, None)
                    pair(PAIRS - 1, None, ahead=0)

            vec.memset(EPS[:, 0:1], RMS_EPS).then_inc(hidden_done, LEAD)
            step(vec.memset(EPS[:, 1:2], LN_EPS))
            step(vec.memset(EPS[:, 2:3], LNX_EPS))
            vec.memset(EPS[:, 3:4], HEAD * RMS_EPS).then_inc(eps_ready, 1)
            for t in range(TB):
                vec.wait_ge(x_loaded[t], 16)
            vec.wait_ge(vec_loaded, 32)
            norm_scale(0)
            low(0)
            h_scale(0, lambda k: VEC[:, V["g1"] + k:V["g1"] + k + 1])
            low(1)
            low(2)
            ffn_vec(0, S_FFN1, True)
            add_half(1, S_FFN1 + N_FFN)

            norm_scale(1)
            h_scale(1, lambda k: vcol("g2", k))
            low(S_WIN + 2)
            step(vec.tensor_scalar(KA1[:, :], VEC[:, V["ka"]:V["ka"] + 4], -1.0, 1.0, ALU.mult, ALU.add))

            def shift_tokens(s):
                vec.wait_ge(u_copied, s + 1)
                own()
                u = U[:, 2 * s:2 * s + 2, :]
                step(vec.tensor_tensor(DT[:, :, 1:256], u[:, :, 0:255], u[:, :, 1:256], ALU.subtract))
                step(vec.tensor_scalar(DT[:, :, 0:1], u[:, :, 0:1], -1.0, None, ALU.mult))
                own()
                for a in range(2):
                    ins = vec.scalar_tensor_tensor(U[:, 2 * s + a, :], DT[:, a, :], vcol("mu", 2 * s + a),
                                                   U[:, 2 * s + a, :], ALU.mult, ALU.add)
                ins.then_inc(shifted, 1)

            def flat(ap):
                return ap.rearrange("p a n -> p (a n)")

            for s in range(7):
                shift_tokens(s)
                low(S_WIN + s + 3)
                if s == 3:
                    vec.wait_ge(sigma_ready, 2)
                    for j in range(4):
                        step(vec.tensor_tensor_scan(ER[:, j, :], mixc("chunk"), EA[:, j, :], 0.0, ALU.mult, ALU.add))
                    own()
                    vec.tensor_tensor(flat(EA), flat(ER), flat(EA), ALU.subtract).then_inc(decay_ready, 1)
                if s == 4:
                    vec.wait_ge(sigma_ready, 3)
                    vec.wait_ge(shifted, 5)
                    for m in range(2):
                        for a in range(2):
                            j = 2 * m + a
                            step(vec.tensor_scalar(DT[:, a, :], AA[:, j, :], vcol("ka", j), KA1[:, j:j + 1],
                                                   ALU.mult, ALU.add))
                        own()
                        step(vec.tensor_tensor(U[:, 2 + 2 * m:4 + 2 * m, :], U[:, 2 + 2 * m:4 + 2 * m, :], DT[:, :, :],
                                               ALU.mult))
                        own()
            vec.wait_ge(head_root, 1)
            step(vec.tensor_scalar(RN[:, 0, :], RN[:, 0, :], 1e-12, None, ALU.max))
            own()
            vec.reciprocal(RN[:, 0, :], RN[:, 0, :]).then_inc(head_rn, 1)
            low(S_WIN + 10)
            vec.wait_ge(shifted, 7)
            for j in range(4):
                step(vec.scalar_tensor_tensor(RKR[:, j, :], U[:, 6 + j, :], vcol("rk", j), U[:, 2 + j, :],
                                              ALU.mult, ALU.mult))
            vec.wait_ge(exp_ready, 3)
            step(vec.tensor_copy(DL[:, :, :], ER[:, :, 63:256:64]))

            def by_block(ap):
                return ap.rearrange("p a (b n) -> p (a b) n", b=2)

            vec.tensor_tensor(AR[:, :, 1, :], by_block(U[:, 6:10, :]), by_block(ER), ALU.mult).then_inc(feature, 1)
            vec.wait_ge(head_spread, 1)
            vec.tensor_tensor(flat(KK), flat(KK), PS[:, 4:6, :].rearrange("p a n -> p (a n)"), ALU.mult)\
               .then_inc(feature, 1)
            low(S_WIN + 11)
            vec.wait_ge(feature, 2)
            step(vec.scalar_tensor_tensor(AR[:, :, 0, :], by_block(KK), -1.0, by_block(EA), ALU.mult, ALU.mult))
            step(vec.tensor_tensor(flat(AA), flat(KK), flat(AA), ALU.mult))
            vec.tensor_tensor(flat(KH), flat(U[:, 2:6, :]), flat(EI), ALU.mult).then_inc(feature, 1)
            own()
            vec.tensor_tensor(flat(BH), flat(AA), flat(EI), ALU.mult).then_inc(feature, 1)
            low(S_WIN + 12)
            vec.wait_ge(head_spread, 2)
            step(vec.tensor_tensor(flat(RKR), PS[:, 4:6, :].rearrange("p a n -> p (a n)"), flat(U[:, 10:14, :]), ALU.mult))

            vec.wait_ge(head_root, 2)
            for m in range(2):
                vec.reciprocal(RN[:, m, :], RN[:, m, :]).then_inc(head_rn, 1)
            for m, name in enumerate(("sbq", "sbk")):
                vec.wait_ge(head_spread, 3 + m)
                u = flat(U[:, 14 + 4 * m:18 + 4 * m, :])
                vec.scalar_tensor_tensor(u, u, vcol(name), PS[:, 3 + 2 * m:5 + 2 * m, :].rearrange("p a n -> p (a n)"),
                                         ALU.mult, ALU.mult).then_inc(qk_ready, 1)

            def softplus(g):
                part = slice(2 * (g % 2), 2 * (g % 2) + 2)
                vec.wait_ge(ln_ready, g + 1)
                step(vec.scalar_tensor_tensor(LT[:, part, :], PS[:, part, 0:384], 0.0, ZT[:, part, :], ALU.max, ALU.add))
                own()
                vec.tensor_tensor(LT[:, part, :], LT[:, part, :], over(mixc("sbmask"), 2), ALU.mult).then_inc(l_ready, 1)

            def exponents(g):
                part = slice(2 * (g % 2), 2 * (g % 2) + 2)
                vec.wait_ge(e_ready, g + 1)
                vec.tensor_tensor(ZT[:, part, :], PS[:, part, 0:384], over(mixc("sbneg"), 2), ALU.min)\
                   .then_inc(e_masked, 1)

            for n in range(4):
                vec.wait_ge(tok_turned, 4 + n + 1)
                vec.tensor_copy((KTOK, VTOK)[n // 2][:, n % 2, :], PS[:, 5 + n % 2, :]).then_inc(tok_moved, 1)
            for first in (0, 2):
                for g in (first, first + 1):
                    softplus(g)
                for g in (first, first + 1):
                    exponents(g)
            vec.wait_ge(head_root, 3)
            vec.reciprocal(RN[:, 0, :], RN[:, 0, :]).then_inc(head_rn, 1)
            vec.wait_ge(head_spread, 5)
            for j in range(4):
                o = (j % 2) * 256
                ins = vec.scalar_tensor_tensor(HF[:, j, :], OS[:, j, :], vcol("sbo", j), PS[:, 2 + j // 2, o:o + 256],
                                               ALU.mult, ALU.mult)
            ins.then_inc(cat_ready, 1)

            def shares(n, lane, half):
                b0, b1, b2 = 3 * lane, 3 * lane + 1, 3 * lane + 2
                t, blk, g = T[lane], half, lane
                at = 8 * half + 4 * lane

                def tiles(bank):
                    return PS[:, bank, :].rearrange("p (a n) -> p a n", a=4)

                def double(bank):
                    return PS[:, bank:bank + 2, :].rearrange("p b (a n) -> p (b a) n", a=2)

                if n in (1, 2, 3, 4, 5, 6, 7, 8, 9, 10, 12):
                    vec.wait_ge(u_pe[lane], 12 * half + n)
                done = lambda ins: ins.then_inc(u_vec[lane], 1)

                def part(to, src, mask, op=ALU.mult):
                    vec.tensor_tensor(to[:, :, :], src, over(mask, 4), op).then_inc(u_part[lane], 1)

                if n == 1:
                    if half:
                        vec.wait_ge(u_pe[lane], 12)
                    two = over(mixc("lower"), 2)
                    vec.tensor_tensor(t[0][:, 0:2, :], tiles(b2)[:, 0:2, :], two, ALU.mult)
                    done(vec.tensor_tensor(t[0][:, 2:4, :], tiles(6)[:, 2 * lane:2 * lane + 2, :], two, ALU.mult))
                    done(vec.tensor_tensor(NR[:, at:at + 4, :], double(b0), over(mixc("mask2"), 4), ALU.mult))
                elif n == 2:
                    done(vec.tensor_tensor(MB[:, at:at + 4, :], double(b0), over(mixc("mask2"), 4), ALU.mult))
                    vec.wait_ge(u_vec[lane], VECS * half + 3)
                    part(t[2], t[0][:, :, :], mixc("same16"))
                    part(t[1], MB[:, at:at + 4, 0:128], mixc("same16"))
                    vec.wait_ge(u_part[lane], PARTS * half + 2)
                    part(t[5], t[1][:, :, :], ident, ALU.add)
                elif n == 3:
                    done(vec.tensor_copy(t[4][:, :, :], tiles(b1)))
                elif n in (4, 5, 6, 8, 10):
                    to, old, bank = {4: (6, 5, b0), 5: (5, 6, b0), 6: (6, 5, b2), 8: (5, 6, b2), 10: (6, 5, b2)}[n]
                    done(vec.tensor_tensor(t[to][:, :, :], t[old][:, :, :], tiles(bank), ALU.add))
                    if n == 5:
                        part(t[4], t[0][:, :, :], mixc("only32"))
                        vec.wait_ge(u_part[lane], PARTS * half + 4)
                        part(t[0], t[0][:, :, :], mixc("only64"))
                elif n in (7, 9):
                    done(vec.tensor_copy(t[2][:, :, :], tiles(b1)))
                elif n == 12:
                    r = AR[:, 4 * g + blk:4 * g + blk + 3:2, 1, :]
                    done(vec.tensor_tensor(RT[:, 2 * g:2 * g + 2, blk * P:(blk + 1) * P],
                                           PS[:, b1, 0:256].rearrange("p (a n) -> p a n", a=2), r, ALU.add))

            for half in range(2):
                for n in range(1, 13):
                    for lane in range(2):
                        shares(n, lane, half)
            for c in range(3):
                vec.wait_ge(s_products, c + 1)
                src = PS[:, 3, 0:256].rearrange("p (a n) -> p a n", a=4)
                decay = DL[:, :, c:c + 1].broadcast_to([P, 4, HEAD])
                if c:
                    through = PS[:, 0, 0:256].rearrange("p (a n) -> p a n", a=4)
                    step(vec.tensor_tensor(ST[:, c, :, :], through, ST[:, c - 1, :, :], ALU.add))
                    own()
                    step(vec.tensor_tensor(ST[:, c, :, :], src, ST[:, c, :, :], ALU.add))
                    own()
                    src = ST[:, c, :, :]
                vec.tensor_tensor(ST[:, c, :, :], src, decay, ALU.mult).then_inc(s_ready, 1)
            vec.wait_ge(y_products, 2)
            vec.tensor_tensor(flat(YC), flat(YS), PS[:, 0:2, :].rearrange("p a n -> p (a n)"), ALU.subtract)\
               .then_inc(y_step, 1)
            vec.wait_ge(head_root, 4)
            vec.reciprocal(RN[:, 0, :], RN[:, 0, :]).then_inc(head_rn, 1)
            vec.wait_ge(cat_hi, 1)
            vec.tensor_tensor(HLO[:, 0:4, :], HF[:, 0:4, :], HHI[:, 0:4, :].bitcast(F32), ALU.subtract).then_inc(cat_lo, 1)
            low(S_OUT1)
            vec.wait_ge(head_spread, 6)
            step(vec.tensor_tensor(flat(YS), flat(YC), PS[:, 4:6, :].rearrange("p a n -> p (a n)"), ALU.mult))
            own()
            for j in range(4):
                step(vec.scalar_tensor_tensor(YC[:, j, :], YS[:, j, :], vcol("lnw", j), RKR[:, j, :], ALU.mult, ALU.add))
            own()
            for j in range(4):
                ins = vec.scalar_tensor_tensor(HF[:, 4 + j, :], YC[:, j, :], vcol("lnb", j), U[:, 6 + j, :],
                                               ALU.add, ALU.mult)
            ins.then_inc(cat_ready, 1)
            low(S_OUT1 + 1)
            vec.wait_ge(cat_hi, 2)
            vec.tensor_tensor(HLO[:, 4:8, :], HF[:, 4:8, :], HHI[:, 4:8, :].bitcast(F32), ALU.subtract).then_inc(cat_lo, 1)
            low(S_OUT1 + 2)
            low(S_OUT1 + 3)

            vec.wait_ge(mod_done, 2)
            vec.wait_ge(mod_copied, 1)
            step(vec.tensor_tensor(MODV[:, 0:MOD_TILES, :], PS[:, 7, 0:2 * MOD_TILES].rearrange("p (a n) -> p a n", n=2),
                                   over(VEC[:, V["bmod"]:V["bmod"] + MOD_TILES], 2, 2), ALU.add))
            step(vec.tensor_tensor(MODV[:, MOD_TILES:48, 0], MODV[:, MOD_TILES:48, 0],
                                   VEC[:, V["bmod"] + MOD_TILES:V["bmod"] + 48], ALU.add))
            own()
            vec.tensor_scalar(MODP[:, 0:MOD_TILES, :], MODV[:, 0:MOD_TILES, :], 1.0, None, ALU.add).then_inc(mod_ready, 1)
            vec.tensor_scalar(MODP[:, MOD_TILES:48, 0], MODV[:, MOD_TILES:48, 0], 1.0, None, ALU.add)\
               .then_inc(mod_ready, 1)
            vec.wait_ge(att_loaded, 48)
            vec.wait_ge(mod_ready, 2)
            for half in range(2):
                for k in range(4 * half, 4 * half + 4):
                    ins = vec.tensor_scalar(CX[:, k, :], CX[:, k, :], MODP[:, 8 + k, 1:2], MODV[:, k, 1:2],
                                            ALU.mult, ALU.add)
                ins.then_inc(ctx_full, 1)
            for r in range(4):
                if r >= 2:
                    vec.wait_ge(gate_rows, r - 1)
                for a in range(4):
                    col = (16 if r < 2 else 40) + 4 * (r % 2) + a
                    ins = vec.tensor_scalar(DG[:, r % 2, a, :], ident, MODV[:, col, 0:1], None, ALU.mult)
                ins.then_inc(gate_diag, 1)
                if r == 1:
                    for half in range(2):
                        part = slice(4 * half, 4 * half + 4)
                        vec.wait_ge(ctx_hi, half + 1)
                        ins = vec.tensor_tensor(CLO[:, part, :], CX[:, part, :], CHI[:, part, :].bitcast(F32), ALU.subtract)
                    ins.then_inc(ctx_lo, 1)
                    low(S_CTX)
            add_half(2, S_OUT1 + N_OUT, 1.0)
            norm_scale(2)
            low(S_CTX + 1)
            low(S_FFN2)
            vec.wait_ge(slabs_used, S_CTX + 1)
            for n in range(2):
                vec.tensor_scalar(KALL[:, n, 256:512], PS[:, 4, n * 256:n * 256 + 256], vcol("b2", n), None, ALU.add)\
                   .then_inc(ctx_copied, 1)

            def add_value_bias(to, bank):
                return vec.tensor_tensor(to, PS[:, bank, :].rearrange("p (a n) -> p a n", a=2),
                                         over(ROWS[:, 0:256], 2), ALU.add)

            low(S_FFN2 + 1)
            vec.wait_ge(slabs_used, S_CTX + 2)
            add_value_bias(VALL[:, 2:4, :], 5).then_inc(ctx_copied, 1)
            h_scale(2, lambda k: vcol("g3", k))
            low(S_FFN2 + 2)
            ffn_vec(1, S_FFN2, True)
            add_half(3, S_FFN2 + N_FFN)

            low(S_WIN2 + 2)
            h_scale(3, lambda k: MODP[:, 8 + k, 0:1], lambda k: MODV[:, k, 0:1])
            low(S_WIN2 + 3)
            vec.wait_ge(slabs_used, S_WIN2 + 2)
            add_value_bias(VALL[:, 0:2, :], 2).then_inc(v_copied, 1)
            low(S_WIN2 + 4)
            low(S_WIN2 + 5)
            vec.wait_ge(head_root, 5)
            vec.reciprocal(RA[:, 0:512], RA[:, 0:512]).then_inc(head_rn, 1)
            vec.wait_ge(head_spread, 7)
            vec.scalar_tensor_tensor(KALL[:, 1, :], KALL[:, 1, :], vcol("kg"), PS[:, 4, :], ALU.mult, ALU.mult)\
               .then_inc(rope_in, 1)
            low(S_WIN2 + 6)

            def rope(n, to, src, bank, tiles):
                cos, sin = over(CT[:, 0:256], tiles), over(CT[:, 256:512], tiles)
                ps = PS[:, bank:bank + (tiles + 1) // 2, :].rearrange("p b (a n) -> p (b a) n", a=2)[:, 0:tiles, :]
                vec.wait_ge(rotated, n)
                step(vec.tensor_tensor(TR[:, 0:tiles, :], ps, sin, ALU.mult))
                step(vec.tensor_tensor(to, src, cos, ALU.mult))
                own()
                return vec.tensor_tensor(to, to, TR[:, 0:tiles, :], ALU.add)

            rope(1, QN[:, 0:4, :], QR[:, 2:6, :], 5, 4).then_inc(roped, 1)
            low(S_WIN2 + 7)
            vec.wait_ge(rotated, 2)
            for n in range(2):
                src, to = (QR[:, 0, :], KALL[:, 0, 0:256]) if n == 0 else (KALL[:, 1, 0:256], KALL[:, 1, 0:256])
                step(vec.tensor_tensor(TK[:, n, :], PS[:, 3, n * 256:n * 256 + 256], CT[:, 256:512], ALU.mult))
                step(vec.tensor_tensor(to, src, CT[:, 0:256], ALU.mult))
                own()
                vec.tensor_tensor(to, to, TK[:, n, :], ALU.add).then_inc(roped, 1)
            low(S_WIN2 + 8)
            vec.wait_ge(head_root, 6)
            vec.reciprocal(RA[:, 0:256], RA[:, 0:256]).then_inc(head_rn, 1)
            low(S_WIN2 + 9)
            vec.wait_ge(head_spread, 8)
            q = flat(QR[:, 6:10, :])
            vec.scalar_tensor_tensor(q, q, vcol("qg"), PS[:, 5:7, :].rearrange("p a n -> p (a n)"), ALU.mult, ALU.mult)\
               .then_inc(rope_in, 1)
            low(S_WIN2 + 10)
            vec.wait_ge(rope_in, 2)
            rope(3, QN[:, 4:8, :], QR[:, 6:10, :], 3, 4).then_inc(roped, 1)
            for s in range(11, 16):
                low(S_WIN2 + s)
            step(vec.tensor_scalar(NS[:, :], ROWS[:, 256:264], -1.0, None, ALU.mult))
            own()

            def maxima(i):
                br, t, j = i // 8, (i // 4) % 2, i % 4
                vec.wait_ge(scored, i + 1)
                ps = PS[:, 2 * (i % 2):2 * (i % 2) + 2, :]
                if br == 0:
                    o = 128 * (1 - t)
                    step(vec.tensor_tensor(ps[:, :, o:o + 128], ps[:, :, o:o + 128],
                                           over(CT[:, 640 + 128 * t:768 + 128 * t], 2), ALU.add))
                    own()
                at = 2 * i
                step(vec.tensor_reduce(SM[:, at % 16:at % 16 + 2], ps, mybir.AxisListType.X, ALU.max))
                own()
                to, mx = SM[:, 32 + at:34 + at], SM[:, at % 16:at % 16 + 2]
                if br == 0:
                    vec.scalar_tensor_tensor(to, mx, -SCALE, NS[:, j:j + 5:4], ALU.mult, ALU.min).then_inc(max_done, 1)
                else:
                    vec.tensor_scalar(to, mx, -SCALE, None, ALU.mult).then_inc(max_done, 1)

            def scale_o(n):
                br, t = n // 2, n % 2
                vec.wait_ge(pv_done, 4 * n + 4)
                at = 64 + 8 * n
                if br == 0:
                    step(vec.tensor_tensor(SM[:, at:at + 8], SM[:, at:at + 8], SM[:, 96 + 8 * n:104 + 8 * n], ALU.add))
                    own()
                step(vec.reciprocal(SM[:, at:at + 8], SM[:, at:at + 8]))
                own()
                vec.tensor_tensor(OT[:, t, br * 512:br * 512 + 512].rearrange("p (h c) -> p h c", h=8),
                                  PS[:, 6 + t, :].rearrange("p (h c) -> p h c", h=8),
                                  SM[:, at:at + 8].unsqueeze(2).broadcast_to([P, 8, 64]), ALU.mult).then_inc(o_scaled, 1)

            for i in range(17):
                if i < 16:
                    maxima(i)
                if i >= 1:
                    vec.wait_ge(p_turned, 2 * i)
                    if i >= 3:
                        vec.wait_ge(pv_done, i - 2)
                    vec.tensor_copy(PT[:, (i - 1) % 2, 1, :], PS[:, 5, :]).then_inc(pt_vec, 1)
                if i == 2:
                    low(S_BRANCH + 2)
                if i == 7:
                    vec.wait_ge(max_done, 8)
                    for t in range(TB):
                        for par in range(2):
                            ins = vec.tensor_tensor(SM[:, 96 + 8 * t + par:104 + 8 * t + par:2],
                                                    SM[:, 32 + 8 * t + par:40 + 8 * t + par:2],
                                                    ROWS[:, 256 + 4 * par:260 + 4 * par], ALU.add)
                    ins.then_inc(sink_in, 1)
                if i == 9:
                    vec.wait_ge(sink_exp, 1)
                if i in (9, 13, 15):
                    scale_o((9, 13, 15).index(i))
            scale_o(3)
            h_scale(4, lambda k: 1.0)
            for half in range(2):
                vec.wait_ge(slabs_used, S_BRANCH + 2 * half + 2)
                part = slice(4 * half, 4 * half + 4)
                bank = 4 * half
                step(vec.tensor_tensor(flat(MF[:, part, :]), flat(GT[:, part, :]),
                                       PS[:, bank:bank + 2, :].rearrange("p a n -> p (a n)"), ALU.mult))
                step(vec.tensor_tensor(flat(MT), flat(GT[:, 8 + 4 * half:12 + 4 * half, :]),
                                       PS[:, bank + 2:bank + 4, :].rearrange("p a n -> p (a n)"), ALU.mult))
                own()
                vec.tensor_tensor(flat(MF[:, part, :]), flat(MF[:, part, :]), flat(MT), ALU.add).then_inc(merged, 1)
                vec.wait_ge(m_hi, half + 1)
                vec.tensor_tensor(MLO[:, part, :], MF[:, part, :], MHI[:, part, :].bitcast(F32), ALU.subtract)\
                   .then_inc(m_lo, 1)
                low(S_BRANCH + 3 + 2 * half)
                low(S_BRANCH + 4 + 2 * half)
            low(S_OUT2 + 3)
            low(S_FFN3)

            def layer_norm(n, used):
                vec.wait_ge(block_done, 4 + n)
                vec.wait_ge(gate_row_copied, 4)

                def residual(t):
                    y = PS[:, 2 * t:2 * t + 2, :].rearrange("p a n -> p (a n)")
                    step(vec.tensor_tensor(YT[:, t, :], GB[:, n, :], y, ALU.mult))
                    own()
                    step(vec.scalar_tensor_tensor(X[:, t, :], X[:, t, :], DEEPNORM_ALPHA, YT[:, t, :], ALU.mult, ALU.add))
                    own()
                    for h in range(2):
                        step(vec.bn_stats(BN[:, t, h, :], X[:, t, h * HALF:(h + 1) * HALF]))
                    own()
                    vec.bn_aggr(SM[:, 16 + 4 * t:18 + 4 * t], BN[:, t, :, :].rearrange("p a n -> p (a n)"))\
                       .then_inc(ln_var, 1)

                def factors(t):
                    vec.wait_ge(ln_root, 2 * n + t + 1)
                    step(vec.reciprocal(SM[:, 19 + 4 * t:20 + 4 * t], SM[:, 18 + 4 * t:19 + 4 * t]))
                    own()
                    vec.scalar_tensor_tensor(SM[:, 24 + t:25 + t], SM[:, 16 + 4 * t:17 + 4 * t], -1.0,
                                             SM[:, 19 + 4 * t:20 + 4 * t], ALU.mult, ALU.mult).then_inc(ln_scale, 1)

                residual(0)
                vec.wait_ge(slabs_used, used)
                residual(1)
                factors(0)
                factors(1)

            def layer_gain(n):
                vec.wait_ge(row_loaded, 16 * n + 16)
                for t in range(TB):
                    for h in range(2):
                        part = slice(h * HALF, (h + 1) * HALF)
                        vec.wait_ge(ln_normed, 4 * n + 2 * t + h + 1)
                        step(vec.tensor_tensor(X[:, t, part], X[:, t, part], ROW[:, h * HALF:(h + 1) * HALF], ALU.mult))
                        own()
                        vec.tensor_tensor(X[:, t, part], X[:, t, part], ROW[:, D + h * HALF:D + (h + 1) * HALF], ALU.add)\
                           .then_inc(x_new, 1)

            step(vec.tensor_tensor(GAIN[:, 0, :], VEC[:, V["ln1g"]:V["ln1g"] + KT], MODP[:, 32:40, 0], ALU.mult))
            step(vec.tensor_tensor(GAIN[:, 1, :], VEC[:, V["ln1b"]:V["ln1b"] + KT], MODP[:, 32:40, 0], ALU.mult))
            own()
            step(vec.tensor_tensor(GAIN[:, 1, :], GAIN[:, 1, :], MODV[:, 24:32, 0], ALU.add))
            own()
            low(S_FFN3 + 1)
            layer_norm(0, S_OUT2 + N_OUT)
            h_scale(5, lambda k: GAIN[:, 0, k:k + 1], lambda k: GAIN[:, 1, k:k + 1])
            layer_gain(0)
            low(S_FFN3 + 2)
            ffn_vec(2, S_FFN3, False)
            layer_norm(1, S_FFN3 + N_FFN)
            layer_gain(1)
    return nc


def place(pieces, width):
    import numpy as np
    return np.ascontiguousarray(np.concatenate([np.asarray(p, np.float32).reshape(P, -1) for p in pieces], axis=1))


def constants():
    import numpy as np
    i, j = np.arange(P)[:, None], np.arange(P)[None, :]
    heads = np.zeros((P, 4, 16))
    spread = np.zeros((P, 4, P))
    for t in range(4):
        for h in range(2):
            heads[64 * h:64 * h + 64, t, 2 * t + h] = 1
            spread[2 * t + h, t, 64 * h:64 * h + 64] = 1
    c_all = place([np.eye(P), np.ones((P, P)), heads, spread], N_ALL)

    same = lambda n: i // n == j // n
    on = np.ones((P, P))
    strict = i < j
    c_mix = place([
        strict & same(64), (i <= j) & same(64),
        (j < i) & same(64),
        same(16), same(32) & ~same(16), same(64) & ~same(32),
        -1.0 * (i >= j), -on,
        strict, on, strict,
        np.where(strict, 0, NEG), 0 * on, np.where(strict, 0, NEG),
        same(64), same(64) / 64.0,
        np.where(np.arange(SEQ)[None, :] % 64 == 0, 0.0, 1.0) * np.ones((P, 1)),
    ], N_MIX)

    grid, theta, n_freq = 64, np.float32(10000.0), HEAD // 4
    freq = theta ** (-np.arange(n_freq, dtype=np.float32) / np.float32(n_freq))
    pos = np.arange(SEQ)
    where = np.arange(P) % HEAD
    axis = np.where((where < 32)[:, None], (pos // grid)[None, :], (pos % grid)[None, :]).astype(np.float32)
    angle = axis * freq[where % 16][:, None].astype(np.float32)
    rot = np.zeros((P, P))
    for c in range(P):
        if c % 32 < 16:
            rot[c + 16, c] = -1
        else:
            rot[c - 16, c] = 1
    c_att = place([np.cos(angle), np.sin(angle), rot,
                   np.where(j <= i, 0, NEG), np.where(j >= i, 0, NEG)], N_ATT)
    return c_all, c_mix, c_att


HEAD_ORDER = [0, 4, 1, 5, 2, 6, 3, 7]


def layout(i):
    import numpy as np
    f = {k: np.asarray(v, np.float32) for k, v in i.items()}

    def by_columns(w, width=256):
        kt, n = w.shape[0] // P, w.shape[1] // width
        return w.reshape(kt, P, n, width).transpose(2, 1, 0, 3).reshape(n, P, kt * width)

    def by_rows(w):
        per = SLAB // w.shape[1]
        return w.reshape(-1, per, P, w.shape[1]).transpose(0, 2, 1, 3).reshape(-1, P, SLAB)

    def ffn(gate, up, down):
        g, u, d = by_columns(gate), by_columns(up), by_rows(down)
        order = [g[0], u[0]]
        for p in range(1, PAIRS):
            order += [g[p], u[p], d[p - 1]]
        return order + [d[PAIRS - 1]]

    w = f["w_in"][0]
    sb, rw = w[:, :1536], w[:, 1536:]
    win = np.concatenate([rw[:, 1536:1664], rw[:, 1664:1792], rw[:, 512:1024], rw[:, 0:512], rw[:, 1024:1536],
                          sb[:, 0:1024]], axis=1)
    w2 = f["w_in_2"][0]
    by_head = np.concatenate([np.arange(h * HEAD, (h + 1) * HEAD) for h in HEAD_ORDER])
    qa, ka, va = w2[:, 0:512][:, by_head], w2[:, 512:640], w2[:, 640:768]
    qb, kb, vb = w2[:, 768:1280][:, by_head], w2[:, 1280:1408], w2[:, 1408:1536]
    keys, values = np.concatenate([ka, kb], axis=1), np.concatenate([va, vb], axis=1)
    ba, bb = by_columns(f["w_branch_a_2"][0][by_head], 512), by_columns(f["w_branch_b_2"][0][by_head], 512)
    mod = by_columns(f["w_mod_2"][0])
    slabs = (ffn(f["ffn1_gate"][0], f["ffn1_up"][0], f["ffn1_down"][0])
             + list(by_columns(win)) + list(by_rows(sb[:, 1024:1536]))
             + list(mod[:N_MOD]) + list(by_rows(f["w_out"][0]))
             + list(by_columns(keys)) + list(by_columns(values))
             + ffn(f["ffn2_gate"][0], f["ffn2_up"][0], f["ffn2_down"][0])
             + list(by_columns(keys)) + list(by_columns(values))
             + list(by_columns(np.concatenate([qa, qb, w2[:, 1536:]], axis=1)))
             + [ba[0], bb[0], ba[1], bb[1]] + list(by_rows(f["w_out_2"][0]))
             + ffn(f["w_up_2"][0][:, :D_FF], f["w_up_2"][0][:, D_FF:], f["w_down_2"][0]))
    slabs = np.stack(slabs)

    def cols(v):
        return v.reshape(-1, P).T

    mu = f["rw_mu"][0]
    mu = np.concatenate([mu[1536:1664], mu[1664:1792], mu[512:1024], mu[0:512], mu[1024:1536]])
    b2 = f["b_in_2"][0]
    b2 = np.concatenate([b2[512:640], b2[1280:1408], b2[0:512][by_head], b2[768:1280][by_head], b2[1536:]])
    twice = lambda v: np.concatenate([v, v]).reshape(P, 1)
    cw, cb = f["conv_w_2"][0], f["conv_b_2"][0]
    taps = np.concatenate([cw, cb[None]], axis=0).reshape(4, 2, PAIRS, 2, P)
    taps = taps.transpose(4, 2, 1, 3, 0).reshape(P, PAIRS * 16)
    taps = np.concatenate([taps, np.zeros((P, 16), np.float32)], axis=1)
    c2 = np.stack([cols(f["c_2"][0]), cols(f["c_ctx_2"])], axis=2).reshape(P, 16)
    vecs = np.concatenate([
        cols(f["norm_ffn1"][0]), cols(f["norm_mix"][0]), cols(f["norm_ffn2"][0]), twice(f["sb_q_norm"][0]),
        twice(f["sb_k_norm"][0]), cols(f["sb_out_norm"][0]), cols(mu), cols(f["rw_w0"][0]), cols(f["rw_a0"][0]),
        cols(f["rw_k_k"][0]), cols(f["rw_k_a"][0]), cols(f["rw_r_k"][0].reshape(-1)), cols(f["rw_ln_w"][0]),
        cols(f["rw_ln_b"][0]), c2, cols(f["b_mod_2"][0]), cols(b2), twice(f["q_norm_g_2"][0]),
        twice(f["k_norm_g_2"][0]), cols(f["ln1_g_2"][0]), cols(f["ln1_b_2"][0]), taps], axis=1)
    c_all, c_mix, c_att = constants()
    lora = np.stack([np.concatenate([f["rw_w2"][0], f["rw_a2"][0]]), f["rw_g2"][0]], axis=1)
    b_in = f["b_in_2"][0]
    rows = np.concatenate([f["ln1_g_2"][0], f["ln1_b_2"][0], f["ln2_g_2"][0], f["ln2_b_2"][0],
                           b_in[640:768], b_in[1408:1536], f["attn_sink_2"][0]]).reshape(1, N_ROW)
    return {
        "slabs": slabs, "mods": np.ascontiguousarray(mod[N_MOD:]), "x": f["x"][0].reshape(TB, P, D),
        "ctx_t": f["ctx_2"][0].T.reshape(KT, P, SEQ).transpose(1, 0, 2),
        "vecs": vecs, "c_all": c_all, "c_mix": c_mix, "c_att": c_att, "lora": lora, "rows": rows,
    }


def kernel(**inputs):
    import numpy as np
    import concourse.bacc as bacc
    from concourse.bass_utils import run_bass_kernel_spmd

    nc = bacc.Bacc("TRN2", target_bir_lowering=False, num_devices=1)
    arrays = {f"in_{k}": np.ascontiguousarray(v) for k, v in layout(inputs).items()}
    args = [nc.dram_tensor(k, a.shape, mybir.dt.from_np(a.dtype), kind="ExternalInput").ap()
            for k, a in arrays.items()]
    out = nc.dram_tensor("out", (TB, P, D), F32, kind="ExternalOutput").ap()
    build_block(nc, *args, out)
    r = run_bass_kernel_spmd(nc, [arrays], core_ids=[0])
    return r.results[0]["out"].reshape(1, SEQ, D)
```
